# Optimizing a Trainium2 kernel written in Bass

```python
import jax, jax.numpy as jnp
from jax import lax
import numpy as np

D_MODEL = 1024
BATCH = 1
SEQ = 128
DEPTH = 2
DEC_BATCH = 1
DEC_SEQ = 512
PAST_LEN = 128

GRID_W = 64
CHUNK = 128
D_MIX = D_MODEL
D_GMLP = D_MIX // 2
D_MLSTM = D_MIX - D_GMLP
H_GMLP = 4
H_MLSTM = 4
DH = D_MLSTM // H_MLSTM
CONV_K = 3
N_KEYS = 128
N_EXPERTS = N_KEYS * N_KEYS
PEER_HEADS = 8
PEER_TOPK = 16
D_KEY = 256
D_HALF = D_KEY // 2
N_GATES = 4 * H_MLSTM
D_IN = 2 * D_GMLP + 4 * D_MLSTM + N_GATES
SPLITS = [D_GMLP, 2 * D_GMLP, 2 * D_GMLP + 2 * D_MLSTM, 2 * D_GMLP + 3 * D_MLSTM, 2 * D_GMLP + 4 * D_MLSTM]
EPS = 1e-6

kernel_name = 'hybrid_gmlp_mlstm_peer_diffusion_step'

def rmsnorm(x, w=None):
    xf = x.astype(jnp.float32)
    y = xf * lax.rsqrt(jnp.mean(xf * xf, axis=-1, keepdims=True) + EPS)
    if w is not None:
        y = y * w.astype(jnp.float32)
    return y.astype(x.dtype)

def modulation(cond, w_mod, b_mod):
    m = jax.nn.silu(cond) @ w_mod + b_mod
    return jnp.split(m[:, None, :], 6, axis=-1)

def conv_ctx(x, w):
    S = x.shape[1]
    xp = jnp.pad(x, ((0, 0), (1, 1), (0, 0)))
    return sum(xp[:, j:j + S] * w[1, j] for j in range(CONV_K))

def conv_grid(x, w):
    B, S, C = x.shape
    rows = S // GRID_W
    xp = jnp.pad(x.reshape(B, rows, GRID_W, C), ((0, 0), (1, 1), (1, 1), (0, 0)))
    y = sum(xp[:, i:i + rows, j:j + GRID_W] * w[i, j] for i in range(CONV_K) for j in range(CONV_K))
    return y.reshape(B, S, C)

def chunk_gmlp(u, v, w_s, b_s):
    B, S, _ = u.shape
    nc = S // CHUNK
    vh = rmsnorm(v.reshape(B, S, H_GMLP, D_GMLP // H_GMLP)).reshape(B, nc, CHUNK, H_GMLP, D_GMLP // H_GMLP)
    mixed = jnp.einsum('hts,bcshd->bcthd', w_s, vh) + b_s.T[:, :, None]
    return u * mixed.reshape(B, S, D_GMLP)

def mlstm_scan(q, k, v, ig, lf, C0, n0, m0):
    B, H, S, _ = q.shape
    nc = S // CHUNK

    def to_chunks(a):
        return jnp.moveaxis(a.reshape(B, H, nc, CHUNK, *a.shape[3:]), 2, 0)

    xs = (to_chunks(q), to_chunks(k), to_chunks(v), to_chunks(ig), to_chunks(lf))
    causal = jnp.tril(jnp.ones((CHUNK, CHUNK), dtype=bool))

    def step(carry, inp):
        C, n, m = carry
        qc, kc, vc, ic, fc = inp
        b = jnp.cumsum(fc, axis=-1)
        dmat = jnp.where(causal, b[..., :, None] - b[..., None, :] + ic[..., None, :], -jnp.inf)
        prior = b + m[..., None]
        m_t = jnp.maximum(prior, jnp.max(dmat, axis=-1))
        w_intra = jnp.exp(dmat - m_t[..., None])
        w_prior = jnp.exp(prior - m_t)
        s = jnp.einsum('bhtd,bhsd->bhts', qc, kc) * w_intra
        num = w_prior[..., None] * jnp.einsum('bhtd,bhde->bhte', qc, C) + jnp.einsum('bhts,bhse->bhte', s, vc)
        den = w_prior * jnp.einsum('bhtd,bhd->bht', qc, n) + jnp.sum(s, axis=-1)
        h = num / jnp.maximum(jnp.abs(den), jnp.exp(-m_t))[..., None]
        bL = b[..., -1]
        log_end = bL[..., None] - b + ic
        m_new = jnp.maximum(bL + m, jnp.max(log_end, axis=-1))
        w_end = jnp.exp(log_end - m_new[..., None])
        decay = jnp.exp(bL + m - m_new)
        C_new = decay[..., None, None] * C + jnp.einsum('bhs,bhsd,bhse->bhde', w_end, kc, vc)
        n_new = decay[..., None] * n + jnp.einsum('bhs,bhsd->bhd', w_end, kc)
        return (C_new, n_new, m_new), h

    init = (C0.astype(jnp.float32), n0.astype(jnp.float32), m0.astype(jnp.float32))
    (C, n, m), hs = lax.scan(step, init, xs)
    return jnp.moveaxis(hs, 0, 2).reshape(B, H, S, DH), C, n, m

def token_mixers(h, conv_fn, C0, n0, m0, w_in, b_gate, conv_w, w_s, b_s, norm_w, w_out):
    B, S, _ = h.shape
    u, vs, qk, v, o, g = jnp.split(h @ w_in, SPLITS, axis=-1)
    y_a = chunk_gmlp(u, vs, w_s, b_s)
    q, k = jnp.split(jax.nn.silu(conv_fn(qk, conv_w)), 2, axis=-1)

    def heads(a):
        return a.reshape(B, S, H_MLSTM, DH).transpose(0, 2, 1, 3).astype(jnp.float32)

    q, k, v = heads(q), heads(k) * (DH ** -0.5), heads(v)
    gates = (g.reshape(B, S, 4, H_MLSTM).astype(jnp.float32) + b_gate.astype(jnp.float32)).transpose(2, 0, 3, 1)
    ig_f, lf_f = gates[0], jax.nn.log_sigmoid(gates[1])
    ig_b, lf_b = gates[2], jax.nn.log_sigmoid(gates[3])
    h_f, Cf, nf, mf = mlstm_scan(q, k, v, ig_f, lf_f, C0[:, 0], n0[:, 0], m0[:, 0])
    rev = lambda a: jnp.flip(a, axis=2)
    h_b, Cb, nb, mb = mlstm_scan(rev(q), rev(k), rev(v), rev(ig_b), rev(lf_b), C0[:, 1], n0[:, 1], m0[:, 1])
    hm = (h_f + rev(h_b)).transpose(0, 2, 1, 3)
    hm = rmsnorm(hm).reshape(B, S, D_MLSTM) * norm_w.astype(jnp.float32)
    y_b = hm.astype(h.dtype) * jax.nn.sigmoid(o)
    out = jnp.concatenate([y_a, y_b], axis=-1) @ w_out
    return out, (jnp.stack([Cf, Cb], axis=1), jnp.stack([nf, nb], axis=1), jnp.stack([mf, mb], axis=1))

def peer(h, w_pq, sub_keys, expert_u, expert_v):
    B, S, D = h.shape
    t = h.reshape(-1, D)
    T = t.shape[0]
    qh = (t @ w_pq).reshape(T, PEER_HEADS, 2, D_HALF).astype(jnp.float32)
    scores = jnp.einsum('thpd,hpkd->thpk', qh, sub_keys.astype(jnp.float32))
    s_top, i_top = lax.top_k(scores, PEER_TOPK)
    cand = s_top[:, :, 0, :, None] + s_top[:, :, 1, None, :]
    cand_idx = i_top[:, :, 0, :, None] * N_KEYS + i_top[:, :, 1, None, :]
    best, pos = lax.top_k(cand.reshape(T, PEER_HEADS, -1), PEER_TOPK)
    idx = jnp.take_along_axis(cand_idx.reshape(T, PEER_HEADS, -1), pos, axis=-1)
    gate = jax.nn.softmax(best, axis=-1).astype(h.dtype)

    def block(args):
        tb, ib, gb = args
        act = jax.nn.gelu(jnp.einsum('td,thkd->thk', tb, expert_u[ib]))
        return jnp.einsum('thk,thkd->td', gb * act, expert_v[ib])

    nb = T // CHUNK
    out = lax.map(block, (t.reshape(nb, CHUNK, D), idx.reshape(nb, CHUNK, PEER_HEADS, PEER_TOPK),
                          gate.reshape(nb, CHUNK, PEER_HEADS, PEER_TOPK)))
    return out.reshape(B, S, D)

def layer(x, mod, conv_fn, C0, n0, m0, w_in, b_gate, conv_w, w_s, b_s, norm_w, w_out,
          peer_wq, peer_keys, peer_u, peer_v):
    sh1, sc1, g1, sh2, sc2, g2 = mod
    hin = rmsnorm(x) * (1 + sc1) + sh1
    mix, state = token_mixers(hin, conv_fn, C0, n0, m0, w_in, b_gate, conv_w, w_s, b_s, norm_w, w_out)
    x = x + g1 * mix
    hin = rmsnorm(x) * (1 + sc2) + sh2
    x = x + g2 * peer(hin, peer_wq, peer_keys, peer_u, peer_v)
    return x, state

def setup_inputs(seed: int = 0) -> dict:
    key = jax.random.key(seed)
    ks = jax.random.split(key, 24)
    nrm = lambda k, shape, s: s * jax.random.normal(k, shape, jnp.float32)
    f_off = jnp.linspace(3.0, 6.0, H_MLSTM)
    z_off = jnp.zeros((H_MLSTM,), jnp.float32)
    gate_off = jnp.stack([z_off, f_off, z_off, f_off])
    return {
        'x_prompt': nrm(ks[0], (BATCH, SEQ, D_MODEL), 1.0),
        'x_sample': nrm(ks[1], (DEC_BATCH, DEC_SEQ, D_MODEL), 1.0),
        'state_C': nrm(ks[2], (DEC_BATCH, DEPTH, 2, H_MLSTM, DH, DH), DH ** -0.5),
        'state_n': nrm(ks[3], (DEC_BATCH, DEPTH, 2, H_MLSTM, DH), 1.0),
        'state_m': nrm(ks[4], (DEC_BATCH, DEPTH, 2, H_MLSTM), 0.5),
        'c': nrm(ks[5], (DEC_BATCH, D_MODEL), 1.0),
        'c_ctx': nrm(ks[6], (D_MODEL,), 1.0),
        'w_mod': nrm(ks[7], (DEPTH, D_MODEL, 6 * D_MODEL), 0.5 * D_MODEL ** -0.5),
        'b_mod': nrm(ks[8], (DEPTH, 6 * D_MODEL), 0.02),
        'w_in': nrm(ks[9], (DEPTH, D_MODEL, D_IN), D_MODEL ** -0.5),
        'b_gate': gate_off[None] + nrm(ks[10], (DEPTH, 4, H_MLSTM), 0.1),
        'conv_w': nrm(ks[11], (DEPTH, CONV_K, CONV_K, 2 * D_MLSTM), 0.3),
        'w_s': nrm(ks[12], (DEPTH, H_GMLP, CHUNK, CHUNK), CHUNK ** -0.5),
        'b_s': 1.0 + nrm(ks[13], (DEPTH, H_GMLP, CHUNK), 0.1),
        'mlstm_norm_w': 1.0 + nrm(ks[14], (DEPTH, D_MLSTM), 0.05),
        'w_out': nrm(ks[15], (DEPTH, D_MIX, D_MODEL), D_MIX ** -0.5),
        'peer_wq': nrm(ks[16], (DEPTH, D_MODEL, PEER_HEADS * D_KEY), D_MODEL ** -0.5),
        'peer_keys': nrm(ks[17], (DEPTH, PEER_HEADS, 2, N_KEYS, D_HALF), D_HALF ** -0.5),
        'peer_u': nrm(ks[18], (DEPTH, N_EXPERTS, D_MODEL), D_MODEL ** -0.5),
        'peer_v': nrm(ks[19], (DEPTH, N_EXPERTS, D_MODEL), 0.5),
        'final_norm_w': 1.0 + nrm(ks[20], (D_MODEL,), 0.05),
    }

def reference(x_prompt, x_sample, state_C, state_n, state_m, c, c_ctx, w_mod, b_mod, w_in, b_gate,
              conv_w, w_s, b_s, mlstm_norm_w, w_out, peer_wq, peer_keys, peer_u, peer_v, final_norm_w):
    B = x_prompt.shape[0]
    zC = jnp.zeros((B, 2, H_MLSTM, DH, DH), jnp.float32)
    zn = jnp.zeros((B, 2, H_MLSTM, DH), jnp.float32)
    zm = jnp.zeros((B, 2, H_MLSTM), jnp.float32)
    xp, xs = x_prompt, x_sample
    new_C, new_n, new_m = [], [], []
    for l in range(DEPTH):
        params = (w_in[l], b_gate[l], conv_w[l], w_s[l], b_s[l], mlstm_norm_w[l], w_out[l],
                  peer_wq[l], peer_keys[l], peer_u[l], peer_v[l])
        mod_ctx = modulation(c_ctx[None], w_mod[l], b_mod[l])
        mod_lat = modulation(c, w_mod[l], b_mod[l])
        xp, (Cl, nl, ml) = layer(xp, mod_ctx, conv_ctx, zC, zn, zm, *params)
        xs, _ = layer(xs, mod_lat, conv_grid, state_C[:, l], state_n[:, l], state_m[:, l], *params)
        new_C.append(Cl)
        new_n.append(nl)
        new_m.append(ml)
    y_prompt = rmsnorm(xp, final_norm_w)
    y_sample = rmsnorm(xs, final_norm_w)
    new_state_C = jnp.stack(new_C, axis=1).astype(x_prompt.dtype)
    new_state_n = jnp.stack(new_n, axis=1).astype(x_prompt.dtype)
    new_state_m = jnp.stack(new_m, axis=1).astype(x_prompt.dtype)
    return (y_prompt, y_sample, new_state_C, new_state_n, new_state_m)


_drawn_inputs = setup_inputs


def setup_inputs(seed=0):
    import zlib

    import numpy as np

    out = dict(_drawn_inputs(seed))
    spreads = {}
    factors = {'state_C': 4.438, 'state_n': 4.2, 'state_m': 6.365, 'mlstm_norm_w': 4.339}
    for name, (base, spread) in spreads.items():
        noise = np.random.default_rng([zlib.crc32(name.encode()), seed]).standard_normal(out[name].shape)
        drawn = base * np.exp(spread * noise) if base else spread * noise
        out[name] = __import__('jax').numpy.asarray(drawn.astype(out[name].dtype))
    for name, factor in factors.items():
        out[name] = (out[name] * factor).astype(out[name].dtype)
    return out
```

```python
from contextlib import ExitStack

import concourse.bass as bass
from concourse import mybir

F32 = mybir.dt.float32
U32 = mybir.dt.uint32
I32 = mybir.dt.int32
ALU = mybir.AluOpType
ACT = mybir.ActivationFunctionType
AX = mybir.AxisListType

P = 128
D = 1024
KD = D // P
SAMPLE_TILES = 4
TILES = SAMPLE_TILES + 1
CTX = TILES - 1
T = TILES * P
NS = SAMPLE_TILES * P
DEPTH = 2
GRID_W = 64
HEADS = 4
DH = 128
R = 2 * HEADS
ROWS = 64
D_G = 512
D_IN = 2 * D_G + 4 * D_G + 4 * HEADS
N_KEYS = 128
N_EXPERTS = N_KEYS * N_KEYS
PH = 8
TOPK = 16
EPS = 1e-6
LOWEST = -3.0e38
VA = DH + 1


class Lane:

    def __init__(self, eng, own):
        self.eng, self.own, self.sent, self.settled = eng, own, {}, {}

    def do(self, ins, sem=None):
        sem = self.own if sem is None else sem
        ins.then_inc(sem, 1)
        self.sent[sem.name] = (sem, self.sent.get(sem.name, (sem, 0))[1] + 1)
        return ins

    def settle(self):
        for name, (sem, n) in self.sent.items():
            if self.settled.get(name) != n:
                self.eng.wait_ge(sem, n)
                self.settled[name] = n


def build(nc, io):
    ctx = ExitStack()
    cleared = []

    def sb(name, shape, dt=F32):
        return ctx.enter_context(nc.sbuf_tensor(name, shape, dt))

    def sem(name):
        s = ctx.enter_context(nc.semaphore(name))
        cleared.append(s)
        return s

    with ctx:
        x_res = sb("x_res", [P, TILES, D])
        y_nat = sb("y_nat", [P, TILES, D])
        big = sb("big", [P, 32000])
        gates_area = sb("gates_area", [P, 4480])
        kn_area = sb("kn_area", [P, 2560])
        ident = sb("ident", [P, P])
        ones_row = sb("ones_row", [ROWS, P])
        cap = sb("cap", [P, 2, P])
        iota16 = sb("iota16", [P, TOPK])
        cond_t = sb("cond_t", [P, KD, 2])
        mod_t = sb("mod_t", [P, DEPTH, 48, 2])
        bmod_t = sb("bmod_t", [P, DEPTH, 48])
        mod_l = sb("mod_l", [P, 48, 2])
        wgate = sb("wgate", [P, KD, 2, ROWS])
        bgate = sb("bgate", [ROWS, 2])
        convw = sb("convw", [P, KD, 9])
        wst = sb("wst", [P, HEADS, P])
        bst = sb("bst", [P, HEADS])
        normw = sb("normw", [P, D_G])
        m0 = sb("m0", [ROWS, 1])
        stat = sb("stat", [P, 4, 24])
        cols = sb("cols", [P, 4, TILES, R])
        decb = sb("decb", [P, R, TILES])
        small = sb("small", [ROWS, 4, TILES])
        m_out = sb("m_out", [ROWS, 1])
        n_io = sb("n_io", [P, R])
        exp_base = sb("exp_base", [P, 1])
        den = sb("den", [P, 2, HEADS])
        ps = ctx.enter_context(nc.psum_tensor("ps", [P, 8, 512], F32))

        def carve(area, at, *shape, dt=None):
            n = 1
            for s in shape:
                n *= s
            v = area[:, at:at + n]
            if dt is not None:
                v = v.bitcast(dt)
            if len(shape) == 2:
                return v.rearrange("p (a b) -> p a b", a=shape[0])
            if len(shape) == 3:
                return v.rearrange("p (a b c) -> p a b c", a=shape[0], b=shape[1])
            return v

        h_t = carve(big, 0, KD, T)
        w0 = carve(big, 5120, KD, D)
        w1 = carve(big, 5120 + 8192, KD, D)
        wq = [w0, w1]
        qk_t = carve(big, 21504, KD, T)
        v_a = carve(big, 26624, TILES, HEADS, VA)
        vs = carve(big, 29204, TILES, D_G)
        hm = vs
        p_w = carve(big, 5120 + 8192, R, T)
        kw = carve(big, 5120 + 8192 + R * T, 2, D_G)
        cn = carve(big, 5120, R, VA)
        hn = carve(big, 5120 + R * VA, HEADS, VA)
        k_n = carve(kn_area, 0, TILES, D_G)
        gate_b = carve(kn_area, 0, 2, D)
        keys_t = carve(kn_area, 0, 2 * PH, N_KEYS)

        def rows(i):
            return gates_area[0:ROWS, i * T:(i + 1) * T]

        g_a, g_lf, g_b, g_m, g_wp, g_em, g_nm = [rows(i) for i in range(7)]
        g_we = g_lf
        exp_idx = carve(gates_area, 0, TILES, P, dt=U32)
        exp_gate = carve(gates_area, 640, TILES, P)
        diag = carve(gates_area, 1280, TOPK, P)
        h_cur = gates_area[:, 3328:4352]
        q_ts = carve(big, 21504, 2, T)
        sc2 = carve(big, 21504 + 1280, 2, T)
        top_v = carve(big, 21504 + 2560, TILES, 2 * PH, TOPK)
        top_i = carve(big, 21504 + 3840, TILES, 2 * PH, TOPK, dt=U32)
        cand = carve(big, 26624, PH, 256)
        cand2 = carve(big, 26624 + 2048, PH, 256)
        best = carve(big, 30720, PH, TOPK)
        pos = carve(big, 30848, PH, TOPK, dt=U32)
        pa = carve(big, 30976, PH, TOPK, dt=U32)
        pb = carve(big, 31104, PH, TOPK, dt=U32)
        paf = carve(big, 31232, PH, TOPK)
        pbf = carve(big, 31360, PH, TOPK)
        i1f = carve(big, 31488, PH, TOPK)
        i2f = carve(big, 31616, PH, TOPK)
        top_if = carve(big, 31744, 2 * PH, TOPK)
        USLOTS, VSLOTS = TOPK, 8
        u_ring = carve(big, 0, USLOTS, D)
        v_ring = carve(big, USLOTS * D, VSLOTS, D)
        act_c = carve(big, 24576, 2, TOPK)
        wact = carve(big, 24576 + 32, 2, TOPK)
        idx_cur = carve(big, 24576 + 64, PH * TOPK, dt=U32)

        def pair(q):
            return ps[:, 2 * q:2 * q + 2, :].rearrange("p a b -> p (a b)")

        s_in = sem("inputs_loaded")
        s_const = sem("constants_made")
        s_load = sem("layer_loaded")
        s_cond = sem("condition_activated")
        s_ml = sem("layer_modulation_copied")
        with nc.Block() as block:
            @block.sync
            def _(sp):
                sp.dma_start(x_res[:, 0:SAMPLE_TILES, :], io["x_sample"].rearrange("a (t p) d -> p (a t) d", p=P)).then_inc(s_in, 16)
                sp.dma_start(x_res[:, CTX, :], io["x_prompt"].rearrange("a p d -> (a p) d")).then_inc(s_in, 16)
                sp.dma_start(cond_t[:, :, :], io["cond_t"]).then_inc(s_in, 16)
                sp.dma_start(bmod_t[:, :, :], io["bmod_t"]).then_inc(s_in, 16)
                sp.wait_ge(s_in, 64)

            @block.gpsimd
            def _(pool):
                lane = Lane(pool, s_const)
                lane.do(pool.memset(ident[:, :], 0.0))
                lane.do(pool.memset(cap[:, :, :], 0.0))
                lane.do(pool.memset(ones_row[:, :], 1.0))
                lane.do(pool.memset(exp_base[:, :], 0.0))
                lane.do(pool.memset(m_out[:, :], 0.0))
                lane.do(pool.iota(iota16[:, :], pattern=[[1, TOPK]], base=0, channel_multiplier=0,
                                  allow_small_or_imprecise_dtypes=True))
                lane.settle()
                lane.do(pool.affine_select(out=ident[:, :], in_=ident[:, :], compare_op=ALU.not_equal, fill=1.0,
                                           base=0, pattern=[[-1, P]], channel_multiplier=1))
                lane.do(pool.affine_select(out=cap[:, 0, :], in_=cap[:, 0, :], compare_op=ALU.is_ge, fill=LOWEST,
                                           base=0, pattern=[[1, P]], channel_multiplier=-1))
                lane.do(pool.affine_select(out=cap[:, 1, :], in_=cap[:, 1, :], compare_op=ALU.is_ge, fill=LOWEST,
                                           base=0, pattern=[[-1, P]], channel_multiplier=1))
                lane.settle()

            @block.scalar
            def _(act):
                act.wait_ge(s_in, 64)
                nc.scalar.activation(cond_t[:, :, :], cond_t[:, :, :], ACT.Silu).then_inc(s_cond, 1)

        s_wm = [sem("mod_weights_0"), sem("mod_weights_1")]
        s_wm_used = sem("mod_weights_used")
        s_mod = sem("mod_ready")
        NB = DEPTH * 6
        wmod = io["w_mod"].rearrange("l (k p) (j n) -> l j p k n", p=P, n=D)
        with nc.Block() as block:
            @block.sync
            def _(sp):
                for j in range(NB):
                    if j >= 2:
                        sp.wait_ge(s_wm_used, j - 1)
                    sp.dma_start(wq[j % 2], wmod[j // 6, j % 6]).then_inc(s_wm[j % 2], 16)

            @block.tensor
            def _(pe):
                for j in range(NB):
                    pe.wait_ge(s_wm[j % 2], 16 * (j // 2 + 1))
                    if j >= 2:
                        pe.wait_ge(s_mod, j - 1)
                    for n in range(8):
                        for k in range(KD):
                            last = pe.matmul(ps[:, j % 2, 2 * n:2 * n + 2], wq[j % 2][:, k, n * P:(n + 1) * P],
                                             cond_t[:, k, :], start=(k == 0), stop=(k == KD - 1))
                    last.then_inc(s_wm_used, 1)

            @block.vector
            def _(dve):
                for j in range(NB):
                    l, m = j // 6, j % 6
                    dve.wait_ge(s_wm_used, j + 1)
                    dve.scalar_tensor_tensor(
                        out=mod_t[:, l, 8 * m:8 * m + 8, :],
                        in0=ps[:, j % 2, 0:16].rearrange("p (a b) -> p a b", b=2),
                        scalar=1.0 if m in (1, 4) else 0.0,
                        in1=bmod_t[:, l, 8 * m:8 * m + 8].unsqueeze(2).broadcast_to([P, 8, 2]),
                        op0=ALU.add, op1=ALU.add).then_inc(s_mod, 1)

        s_gu = [ctx.enter_context(nc.semaphore(f"u_row_{k}")) for k in range(USLOTS)]
        s_gv = [ctx.enter_context(nc.semaphore(f"v_row_{k}")) for k in range(VSLOTS)]

        with nc.Fori(0, DEPTH) as l:
            L = bass.ds(l, 1)

            def of(name, pattern):
                return io[name][L].rearrange(pattern)

            win = io["w_in"][L].rearrange("a (k p) n -> p (a k) n", p=P)
            s_w = [sem(f"w_{n}") for n in ("uv", "qk", "vo", "out", "q0", "q1")]
            with nc.Block() as block:
                @block.sync
                def _(sp):
                    sp.dma_start(wgate[:, :, :, :], of("w_gate", "a p k g r -> p (a k) g r")).then_inc(s_load, 16)
                    sp.dma_start(bgate[:, :], of("b_gate", "a p g -> p (a g)")).then_inc(s_load, 16)
                    sp.dma_start(convw[:, :, :], of("conv_w", "a p k n -> p (a k) n")).then_inc(s_load, 16)
                    sp.dma_start(wst[:, :, :], of("w_st", "a p h t -> p (a h) t")).then_inc(s_load, 16)
                    sp.dma_start(bst[:, :], of("b_st", "a p h -> p (a h)")).then_inc(s_load, 16)
                    sp.dma_start(normw[:, :], of("mlstm_norm_w", "a n -> a n").broadcast_to([P, D_G])).then_inc(s_load, 16)
                    sp.dma_start(m0[:, :], of("state_m", "a p o -> (a p) o")).then_inc(s_load, 16)
                    sp.dma_start(w1, win[:, :, 2 * D_G:4 * D_G]).then_inc(s_w[1], 16)
                    sp.dma_start(w0, win[:, :, 0:2 * D_G]).then_inc(s_w[0], 16)
                    sp.wait_ge(s_load, 7 * 16)

                @block.vector
                def _(dve):
                    dve.tensor_copy(mod_l[:, :, :], mod_t[:, L, :, :].rearrange("p a b c -> p (a b) c")).then_inc(s_ml, 1)

            def norm_block(tag, sh, sc, natural):
                own = sem(f"{tag}_vector_steps")
                s_ms = sem(f"{tag}_mean_squares")
                s_sq = sem(f"{tag}_roots")
                s_xn = sem(f"{tag}_normalised")
                s_tr = sem(f"{tag}_transposed")
                s_ht = sem(f"{tag}_ht_latent")
                s_hc = sem(f"{tag}_ht_context")
                s_back = sem(f"{tag}_back")
                s_nat = sem(f"{tag}_natural")
                ss, rs = stat[:, 0, 0:TILES], stat[:, 1, 0:TILES]
                with nc.Block() as block:
                    @block.vector
                    def _(dve):
                        lane = Lane(dve, own)
                        for t in range(TILES):
                            lane.do(dve.tensor_tensor_reduce(out=y_nat[:, t, :], in0=x_res[:, t, :], in1=x_res[:, t, :],
                                                             scale=1.0, scalar=0.0, op0=ALU.mult, op1=ALU.add,
                                                             accum_out=stat[:, 0, t:t + 1]))
                        lane.settle()
                        lane.do(dve.tensor_scalar(ss, ss, 1.0 / D, EPS, ALU.mult, ALU.add), s_ms)
                        dve.wait_ge(s_sq, 1)
                        lane.do(dve.reciprocal(rs, ss))
                        lane.settle()
                        for t in range(TILES):
                            lane.do(dve.tensor_scalar(y_nat[:, t, :], x_res[:, t, :], stat[:, 1, t:t + 1], None, ALU.mult), s_xn)
                        for k in range(KD):
                            dve.wait_ge(s_tr, k + 1)
                            lane.do(dve.tensor_scalar(h_t[:, k, NS:T], pair(k % 4)[:, NS:T], mod_l[:, 8 * sc + k, 1:2],
                                                      mod_l[:, 8 * sh + k, 1:2], ALU.mult, ALU.add), s_hc)

                    @block.scalar
                    def _(act):
                        act.wait_ge(s_ms, 1)
                        act.activation(ss, ss, ACT.Sqrt).then_inc(s_sq, 1)
                        for k in range(KD):
                            act.wait_ge(s_tr, k + 1)
                            act.activation(h_t[:, k, 0:NS], pair(k % 4)[:, 0:NS], ACT.Identity,
                                           bias=mod_l[:, 8 * sh + k, 0:1], scale=mod_l[:, 8 * sc + k, 0:1]).then_inc(s_ht, 1)
                        for t in range(TILES if natural else 0):
                            act.wait_ge(s_back, t + 1)
                            act.activation(y_nat[:, t, :], pair(t % 4), ACT.Copy).then_inc(s_nat, 1)

                    @block.tensor
                    def _(pe):
                        for k in range(KD):
                            if k == 0:
                                pe.wait_ge(s_xn, TILES)
                            if k >= 4:
                                pe.wait_ge(s_ht, k - 3)
                                pe.wait_ge(s_hc, k - 3)
                            for t in range(TILES):
                                last = pe.transpose(pair(k % 4)[:, t * P:(t + 1) * P], y_nat[:, t, k * P:(k + 1) * P], ident[:, :])
                            last.then_inc(s_tr, 1)
                        for t in range(TILES if natural else 0):
                            if t == 0:
                                pe.wait_ge(s_ht, KD)
                                pe.wait_ge(s_hc, KD)
                            if t >= 4:
                                pe.wait_ge(s_nat, t - 3)
                            for k in range(KD):
                                last = pe.transpose(pair(t % 4)[:, k * P:(k + 1) * P], h_t[:, k, t * P:(t + 1) * P], ident[:, :])
                            last.then_inc(s_back, 1)

            norm_block("norm1", 0, 1, False)

            own = sem("proj_vector_steps")
            s_gmm = sem("gate_products")
            s_ones = sem("v_ones_made")
            s_qk = sem("qk_products")
            s_conv = sem("qk_convolved")
            s_convfree = sem("qk_banks_free")
            s_silu = sem("qk_silu")
            s_kn = sem("k_scaled")
            s_uv = sem("uv_products")
            s_uve = sem("uv_evacuated")
            s_neg = sem("gate_minus_abs")
            s_sp = sem("gate_softplus")
            s_aown = sem("proj_scalar_steps")
            s_rowx = sem("gate_rows_ready")
            s_rowe = sem("gate_rows_exponentials")
            s_w0free = sem("uv_weights_used")
            ig_ps, fg_ps = pair(2)[0:ROWS, 0:T], pair(3)[0:ROWS, 0:T]
            with nc.Block() as block:
                @block.sync
                def _(sp):
                    sp.wait_ge(s_w0free, 1)
                    sp.dma_start(w0, win[:, :, 4 * D_G:6 * D_G]).then_inc(s_w[2], 16)

                @block.tensor
                def _(pe):
                    for g in range(2):
                        for a, b in ((0, NS), (NS, T)):
                            for k in range(KD):
                                last = pe.matmul(pair(2 + g)[0:ROWS, a:b], wgate[:, k, g, :], h_t[:, k, a:b],
                                                 start=(k == 0), stop=(k == KD - 1))
                        last.then_inc(s_gmm, 1)
                    pe.wait_ge(s_w[1], 16)
                    for j in range(KD):
                        if j >= 2:
                            pe.wait_ge(s_convfree, j - 1)
                        for a, b in ((0, NS), (NS, T)):
                            for k in range(KD):
                                last = pe.matmul(pair(j % 2)[:, a:b], w1[:, k, j * P:(j + 1) * P], h_t[:, k, a:b],
                                                 start=(k == 0), stop=(k == KD - 1))
                        last.then_inc(s_qk, 1)
                    n = 0
                    for phase in range(2):
                        pe.wait_ge(s_w[0] if phase == 0 else s_w[2], 16)
                        for half in range(2):
                            for t in range(TILES):
                                if n < 4:
                                    pe.wait_ge(s_neg, 1)
                                else:
                                    pe.wait_ge(s_uve, n - 3)
                                for k in range(KD):
                                    last = pe.matmul(ps[:, 4 + n % 4, :], h_t[:, k, t * P:(t + 1) * P],
                                                     w0[:, k, half * D_G:(half + 1) * D_G],
                                                     start=(k == 0), stop=(k == KD - 1))
                                last.then_inc(s_uv, 1)
                                n += 1
                        if phase == 0:
                            pe.wait_ge(s_uv, n)
                            pe.sem_inc(s_w0free, 1)

                @block.scalar
                def _(act):
                    act.wait_ge(s_neg, 1)
                    act.activation(g_wp, g_wp, ACT.Exp).then_inc(s_aown, 1)
                    act.wait_ge(s_aown, 1)
                    act.activation(g_wp, g_wp, ACT.Ln, bias=1.0).then_inc(s_sp, 1)
                    for j in range(KD):
                        act.wait_ge(s_conv, j + 1)
                        act.activation(qk_t[:, j, :], qk_t[:, j, :], ACT.Silu).then_inc(s_silu, 1)
                    n = 0
                    for phase in range(2):
                        for half in range(2):
                            for t in range(TILES):
                                act.wait_ge(s_uv, n + 1)
                                src = ps[:, 4 + n % 4, :]
                                if phase == 0 and half == 0:
                                    act.activation(y_nat[:, t, 0:D_G], src, ACT.Copy).then_inc(s_uve, 1)
                                elif phase == 0:
                                    act.activation(vs[:, t, :], src, ACT.Copy).then_inc(s_uve, 1)
                                elif half == 0:
                                    act.activation(v_a[:, t, :, 0:DH], src.rearrange("p (h d) -> p h d", d=DH),
                                                   ACT.Copy).then_inc(s_uve, 1)
                                else:
                                    act.activation(y_nat[:, t, D_G:D], src, ACT.Sigmoid).then_inc(s_uve, 1)
                                n += 1
                    act.wait_ge(s_rowx, 1)
                    act.activation(g_wp, g_wp, ACT.Exp, scale=-1.0).then_inc(s_rowe, 1)
                    act.activation(g_em, g_em, ACT.Exp, scale=-1.0).then_inc(s_rowe, 1)
                    act.activation(g_we, g_we, ACT.Exp).then_inc(s_rowe, 1)
                    act.activation(small[:, 2, :], small[:, 2, :], ACT.Exp).then_inc(s_rowe, 1)

                @block.gpsimd
                def _(pool):
                    pool.memset(v_a[:, :, :, DH:VA], 1.0).then_inc(s_ones, 1)
                    for j in range(HEADS, KD):
                        pool.wait_ge(s_silu, j + 1)
                        pool.tensor_scalar(qk_t[:, j, :], qk_t[:, j, :], float(DH) ** -0.5, None, ALU.mult).then_inc(s_kn, 1)

                @block.vector
                def _(dve):
                    lane = Lane(dve, own)
                    dve.wait_ge(s_gmm, 2)
                    lane.do(dve.tensor_scalar(g_a, ig_ps, bgate[:, 0:1], None, ALU.add))
                    lane.do(dve.tensor_scalar(g_lf, fg_ps, bgate[:, 1:2], None, ALU.add))
                    lane.settle()
                    lane.do(dve.tensor_scalar(g_nm, g_lf, -1.0, None, ALU.mult))
                    lane.settle()
                    lane.do(dve.tensor_tensor(g_wp, g_lf, g_nm, ALU.min), s_neg)
                    lane.settle()
                    for j in range(KD):
                        src, dst = pair(j % 2), qk_t[:, j, :]
                        dve.wait_ge(s_qk, j + 1)
                        lane.do(dve.tensor_scalar(dst, src[:, 0:T], convw[:, j, 4:5], None, ALU.mult))
                        g_src = src[:, 0:NS].rearrange("p (r c) -> p r c", c=GRID_W)
                        g_dst = dst[:, 0:NS].rearrange("p (r c) -> p r c", c=GRID_W)
                        rr = NS // GRID_W
                        for tap in range(9):
                            di, dj = tap // 3 - 1, tap % 3 - 1
                            if tap == 4:
                                continue
                            r0, r1 = max(0, -di), rr - max(0, di)
                            c0, c1 = max(0, -dj), GRID_W - max(0, dj)
                            lane.settle()
                            out = g_dst[:, r0:r1, c0:c1]
                            if di == 0:
                                o2 = dst[:, NS + c0:T - max(0, dj)]
                                lane.do(dve.scalar_tensor_tensor(out=o2, in0=src[:, NS + c0 + dj:T - max(0, dj) + dj],
                                                                 scalar=convw[:, j, tap:tap + 1], in1=o2,
                                                                 op0=ALU.mult, op1=ALU.add))
                            lane.do(dve.scalar_tensor_tensor(out=out, in0=g_src[:, r0 + di:r1 + di, c0 + dj:c1 + dj],
                                                             scalar=convw[:, j, tap:tap + 1], in1=out,
                                                             op0=ALU.mult, op1=ALU.add))
                        lane.settle()
                        dve.engine_nop().then_inc(s_convfree, 1)
                        dve.engine_nop().then_inc(s_conv, 1)
                    dve.wait_ge(s_sp, 1)
                    lane.do(dve.scalar_tensor_tensor(out=g_lf, in0=g_lf, scalar=0.0, in1=g_wp, op0=ALU.min, op1=ALU.subtract))
                    lane.settle()

                    def span(row, c, back, dir_):
                        lo, hi = 32 * dir_, 32 * dir_ + HEADS
                        if not back:
                            return row[lo:hi, c * P:(c + 1) * P]
                        first, last = (c + 1) * P - 1, c * P - 1
                        return row[lo:hi, first:(last if last >= 0 else None):-1]

                    lane.do(dve.memset(g_b, 0.0))
                    lane.do(dve.memset(g_m, 0.0))
                    lane.do(dve.memset(small[:, :, :], 0.0))
                    lane.settle()
                    for c in range(TILES):
                        for d in range(2):
                            lane.do(dve.tensor_tensor_scan(span(g_b, c, d == 1, d), ones_row[32 * d:32 * d + HEADS, :],
                                                           span(g_lf, c, d == 1, d), 0.0, ALU.mult, ALU.add))
                    lane.settle()
                    lane.do(dve.tensor_tensor(g_a, g_a, g_b, ALU.subtract))
                    lane.do(dve.tensor_copy(small[0:HEADS, 0, 0:1], m0[0:HEADS, :]))
                    lane.do(dve.tensor_copy(small[32:32 + HEADS, 0, SAMPLE_TILES - 1:SAMPLE_TILES], m0[32:32 + HEADS, :]))
                    lane.settle()
                    for i in range(TILES):
                        for d in range(2):
                            c = i if d == 0 or i == CTX else SAMPLE_TILES - 1 - i
                            lo, hi = 32 * d, 32 * d + HEADS
                            sa = span(g_a, c, d == 1, d)
                            lane.do(dve.tensor_tensor_scan(span(g_m, c, d == 1, d), sa, sa, small[lo:hi, 0, c:c + 1],
                                                           ALU.max, ALU.max))
                        lane.settle()
                        for d in range(2):
                            c = i if d == 0 or i == CTX else SAMPLE_TILES - 1 - i
                            lo, hi = 32 * d, 32 * d + HEADS
                            end = c * P + (P - 1 if d == 0 else 0)
                            lane.do(dve.tensor_copy(small[lo:hi, 1, c:c + 1], g_m[lo:hi, end:end + 1]))
                            nxt = m_out[lo:hi, :] if i == CTX else None
                            if i < SAMPLE_TILES - 1:
                                cc = i + 1 if d == 0 else SAMPLE_TILES - 2 - i
                                nxt = small[lo:hi, 0, cc:cc + 1]
                            if nxt is not None:
                                lane.do(dve.tensor_tensor(nxt, g_b[lo:hi, end:end + 1], g_m[lo:hi, end:end + 1], ALU.add))
                        lane.settle()
                    by_c = lambda row: row.rearrange("p (c t) -> p c t", t=P)
                    spread = lambda q: small[:, q, :].unsqueeze(2).broadcast_to([ROWS, TILES, P])
                    lane.do(dve.tensor_scalar(g_nm, g_m, -1.0, None, ALU.mult))
                    lane.do(dve.tensor_tensor(by_c(g_wp), by_c(g_m), spread(0), ALU.subtract))
                    lane.do(dve.tensor_tensor(g_em, g_b, g_m, ALU.add))
                    lane.do(dve.tensor_tensor(by_c(g_we), by_c(g_a), spread(1), ALU.subtract))
                    lane.do(dve.tensor_tensor(small[:, 2, :], small[:, 0, :], small[:, 1, :], ALU.subtract))
                    lane.settle()
                    dve.engine_nop().then_inc(s_rowx, 1)

            own2 = sem("gmlp_vector_steps")
            s_v2 = sem("gmlp_mean_squares")
            s_r2 = sem("gmlp_roots")
            s_vh = sem("gmlp_normalised")
            s_mix = sem("gmlp_products")
            s_ya = sem("gmlp_done")
            s_ct = sem("gate_columns_transposed")
            s_kt = sem("k_transposed")
            s_ke = sem("k_natural")
            s_colr = sem("gate_columns_read")
            s_scr = sem("gmlp_squares")
            ms2, rs2 = stat[:, 2, 0:20], stat[:, 3, 0:20]
            with nc.Block() as block:
                @block.vector
                def _(dve):
                    lane = Lane(dve, own2)
                    v20 = vs.rearrange("p t (h d) -> p (t h) d", d=DH)
                    k20 = k_n.rearrange("p t (h d) -> p (t h) d", d=DH)
                    lane.do(dve.tensor_tensor(k20, v20, v20, ALU.mult))
                    lane.settle()
                    lane.do(dve.tensor_reduce(ms2, k20, AX.X, ALU.add))
                    lane.settle()
                    lane.do(dve.tensor_scalar(ms2, ms2, 1.0 / DH, EPS, ALU.mult, ALU.add), s_v2)
                    dve.wait_ge(s_ct, 1)
                    c20 = cols.rearrange("p q c r -> p (q c) r")
                    t20 = ps[:, 4:7, :].rearrange("p a b -> p (a b)")[:, 0:20 * ROWS].rearrange("p (n r) -> p n r", r=ROWS)
                    lane.do(dve.tensor_copy(c20[:, :, 0:HEADS], t20[:, :, 0:HEADS]))
                    lane.do(dve.tensor_copy(c20[:, :, HEADS:R], t20[:, :, 32:32 + HEADS]))
                    lane.do(dve.tensor_copy(decb.rearrange("p r c -> p (r c)"), ps[:, 7, 0:R * TILES]))
                    dve.wait_ge(s_r2, 1)
                    lane.do(dve.reciprocal(rs2, ms2))
                    lane.settle()
                    lane.do(dve.tensor_tensor(v20, v20, rs2.unsqueeze(2).broadcast_to([P, 20, DH]), ALU.mult), s_vh)
                    for h in range(HEADS):
                        dve.wait_ge(s_mix, h + 1)
                        for a, b in ((0, SAMPLE_TILES), (SAMPLE_TILES, TILES)):
                            yv = y_nat[:, a:b, h * DH:(h + 1) * DH]
                            lane.do(dve.scalar_tensor_tensor(
                                out=yv, in0=pair(h % 2)[:, a * P:b * P].rearrange("p (t d) -> p t d", d=DH),
                                scalar=bst[:, h:h + 1], in1=yv, op0=ALU.add, op1=ALU.mult), s_ya)

                @block.scalar
                def _(act):
                    act.wait_ge(s_v2, 1)
                    act.activation(ms2, ms2, ACT.Sqrt).then_inc(s_r2, 1)
                    for c in range(TILES):
                        act.wait_ge(s_kt, c + 1)
                        act.activation(k_n[:, c, :], ps[:, c % 4 if c < 4 else 0, :], ACT.Copy).then_inc(s_ke, 1)

                @block.tensor
                def _(pe):
                    for q, row in enumerate((g_a, g_wp, g_em, g_we)):
                        for c in range(TILES):
                            n = (q * TILES + c) * ROWS
                            pe.transpose(ps[:, 4 + n // 512, n % 512:n % 512 + ROWS], row[:, c * P:(c + 1) * P],
                                         ident[0:ROWS, 0:ROWS])
                    for r in range(R):
                        row = 32 * (r // HEADS) + r % HEADS
                        last = pe.matmul(ps[:, 7, r * TILES:(r + 1) * TILES],
                                         ident[0:ROWS, row:row + 1].broadcast_to([ROWS, P]), small[:, 2, :],
                                         start=True, stop=True)
                    last.then_inc(s_ct, 1)
                    pe.wait_ge(s_v2, 1)
                    for c in range(TILES):
                        if c == 4:
                            pe.wait_ge(s_ke, 1)
                        for h in range(HEADS):
                            last = pe.transpose(ps[:, c % 4, h * DH:(h + 1) * DH], qk_t[:, HEADS + h, c * P:(c + 1) * P], ident[:, :])
                        last.then_inc(s_kt, 1)
                    pe.wait_ge(s_vh, 1)
                    pe.wait_ge(s_ke, TILES)
                    for h in range(HEADS):
                        if h >= 2:
                            pe.wait_ge(s_ya, 2 * (h - 1))
                        for a, b in ((0, SAMPLE_TILES), (SAMPLE_TILES, TILES)):
                            last = pe.matmul(pair(h % 2)[:, a * P:b * P], wst[:, h, :],
                                             vs[:, a:b, h * DH:(h + 1) * DH], start=True, stop=True)
                        last.then_inc(s_mix, 1)

            own3 = sem("intra_vector_steps")
            s_sc = sem("scores")
            s_nm = sem("minus_m_spread")
            s_e1 = sem("exponents")
            s_e2 = sem("exponents_capped")
            s_e3 = sem("exponentials")
            s_p = sem("intra_weights")
            s_cl = sem("states_loaded")
            with nc.Block() as block:
                @block.sync
                def _(sp):
                    sp.dma_start(cn[:, :, 0:DH], of("state_C", "a r d e -> d (a r) e")).then_inc(s_cl, 16)
                    sp.dma_start(n_io[:, :], of("state_n", "a d r -> d (a r)")).then_inc(s_cl, 16)
                    sp.wait_ge(s_cl, 32)

                @block.tensor
                def _(pe):
                    for h in range(HEADS):
                        if h:
                            pe.wait_ge(s_p, 2 * h)
                        for c in range(TILES):
                            last = pe.matmul(pair(0)[:, c * P:(c + 1) * P], qk_t[:, HEADS + h, c * P:(c + 1) * P],
                                             qk_t[:, h, c * P:(c + 1) * P], start=True, stop=True)
                        last.then_inc(s_sc, 1)
                        for d in range(2):
                            row = 32 * d + h
                            for a, b in ((0, NS), (NS, T)):
                                last = pe.matmul(pair(1 + d)[:, a:b], ident[0:ROWS, row:row + 1].broadcast_to([ROWS, P]),
                                                 g_nm[:, a:b], start=True, stop=True)
                            last.then_inc(s_nm, 1)

                @block.vector
                def _(dve):
                    n = 0
                    for h in range(HEADS):
                        for d in range(2):
                            r = d * HEADS + h
                            dve.wait_ge(s_nm, n + d + 1)
                            dve.tensor_tensor(p_w[:, r, :].rearrange("p (c t) -> p c t", t=P),
                                              pair(1 + d)[:, 0:T].rearrange("p (c t) -> p c t", t=P),
                                              cols[:, 0, :, r:r + 1].broadcast_to([P, TILES, P]), ALU.add).then_inc(s_e1, 1)
                        dve.wait_ge(s_sc, h + 1)
                        for d in range(2):
                            r = d * HEADS + h
                            dve.wait_ge(s_e3, n + d + 1)
                            dve.tensor_tensor(p_w[:, r, :], pair(0)[:, 0:T], p_w[:, r, :], ALU.mult).then_inc(s_p, 1)
                        n += 2

                @block.gpsimd
                def _(pool):
                    for n in range(R):
                        h, d = n // 2, n % 2
                        pool.wait_ge(s_e1, n + 1)
                        v = p_w[:, d * HEADS + h, :].rearrange("p (c t) -> p c t", t=P)
                        pool.tensor_tensor(v, v, cap[:, d:d + 1, :].broadcast_to([P, TILES, P]), ALU.add).then_inc(s_e2, 1)

                @block.scalar
                def _(act):
                    for n in range(R):
                        h, d = n // 2, n % 2
                        act.wait_ge(s_e2, n + 1)
                        v = p_w[:, d * HEADS + h, :]
                        act.activation(v, v, ACT.Exp).then_inc(s_e3, 1)

            own4 = sem("chain_vector_steps")
            s_kw = sem("k_weighted")
            s_mm = sem("chain_products")
            s_hn = sem("chain_outputs_read")
            s_cn = sem("chain_state")
            s_n0 = sem("normaliser_placed")
            s_nf = sem("normaliser_taken")
            s_st = sem("states_stored")
            steps = []
            for i in range(TILES):
                for d in range(2):
                    steps.append((d, i if d == 0 or i == CTX else SAMPLE_TILES - 1 - i))
            heads_of = lambda b: ps[:, b:b + 2, 0:2 * VA].rearrange("p a (h e) -> p a h e", e=VA)
            four = lambda ap: ap.rearrange("p (a h) e -> p a h e", a=2)
            with nc.Block() as block:
                @block.gpsimd
                def _(pool):
                    for n, (d, c) in enumerate(steps):
                        if n >= 2:
                            pool.wait_ge(s_mm, n - 1)
                        pool.tensor_tensor(kw[:, n % 2, :].rearrange("p (h e) -> p h e", e=DH),
                                           k_n[:, c, :].rearrange("p (h e) -> p h e", e=DH),
                                           cols[:, 3, c, d * HEADS:(d + 1) * HEADS].unsqueeze(2).broadcast_to([P, HEADS, DH]),
                                           ALU.mult).then_inc(s_kw, 1)

                @block.tensor
                def _(pe):
                    for n, (d, c) in enumerate(steps):
                        pe.wait_ge(s_kw, n + 1)
                        if n == 0:
                            pe.wait_ge(s_n0, 1)
                        if n >= 1:
                            pe.wait_ge(s_cn, n)
                        for h in range(HEADS):
                            r = d * HEADS + h
                            b, e = h // 2, (h % 2) * VA
                            if c != CTX:
                                pe.matmul(ps[:, b, e:e + VA], qk_t[:, h, c * P:(c + 1) * P], cn[:, r, :], start=True, stop=True)
                            pe.matmul(ps[:, 2 + b, e:e + VA], p_w[:, r, c * P:(c + 1) * P], v_a[:, c, h, :], start=True, stop=True)
                            last = pe.matmul(ps[:, 4 + b, e:e + VA], kw[:, n % 2, h * DH:(h + 1) * DH], v_a[:, c, h, :],
                                             start=True, stop=True)
                        last.then_inc(s_mm, 1)

                @block.vector
                def _(dve):
                    lane = Lane(dve, own4)
                    lane.do(dve.memset(hm[:, :, :], 0.0))
                    lane.do(dve.tensor_copy(cn[:, :, DH], n_io[:, :]), s_n0)
                    hn4 = four(hn)
                    for n, (d, c) in enumerate(steps):
                        rr = slice(d * HEADS, (d + 1) * HEADS)
                        dve.wait_ge(s_mm, n + 1)
                        lane.settle()
                        if c != CTX:
                            wp = cols[:, 1, c, rr].unsqueeze(2).broadcast_to([P, HEADS, VA])
                            lane.do(dve.tensor_tensor(hn4, heads_of(0), four(wp), ALU.mult))
                            dec = decb[:, rr, c:c + 1].broadcast_to([P, HEADS, VA])
                            lane.do(dve.tensor_tensor(cn[:, rr, :], cn[:, rr, :], dec, ALU.mult))
                            lane.settle()
                            lane.do(dve.tensor_tensor(hn4, hn4, heads_of(2), ALU.add))
                            lane.do(dve.tensor_tensor(four(cn[:, rr, :]), four(cn[:, rr, :]), heads_of(4), ALU.add), s_cn)
                        else:
                            lane.do(dve.tensor_copy(hn4, heads_of(2)))
                            lane.do(dve.tensor_copy(four(cn[:, rr, :]), heads_of(4)), s_cn)
                        lane.settle()
                        dd = hn[:, :, DH:VA].rearrange("p h o -> p (h o)")
                        lane.do(dve.tensor_scalar(den[:, 0, :], dd, -1.0, None, ALU.mult))
                        lane.settle()
                        lane.do(dve.tensor_tensor(den[:, 0, :], den[:, 0, :], dd, ALU.max))
                        lane.settle()
                        lane.do(dve.tensor_tensor(den[:, 0, :], den[:, 0, :], cols[:, 2, c, rr], ALU.max))
                        lane.settle()
                        lane.do(dve.reciprocal(den[:, 1, :], den[:, 0, :]))
                        lane.settle()
                        lane.do(dve.tensor_tensor(hn[:, :, 0:DH], hn[:, :, 0:DH],
                                                  den[:, 1, :].unsqueeze(2).broadcast_to([P, HEADS, DH]), ALU.mult))
                        lane.settle()
                        hmc = hm[:, c, :].rearrange("p (h e) -> p h e", e=DH)
                        lane.do(dve.tensor_tensor(hmc, hmc, hn[:, :, 0:DH], ALU.add))
                    lane.do(dve.tensor_copy(n_io[:, :], cn[:, :, DH]), s_nf)
                    lane.settle()

                @block.sync
                def _(sp):
                    sp.wait_ge(s_cn, len(steps))
                    for r in range(R):
                        sp.dma_start(io["new_C"][L].rearrange("a r d e -> (a r) d e")[r], cn[:, r, 0:DH]).then_inc(s_st, 16)
                    sp.dma_start(io["new_m"][L].rearrange("a r o -> (a r) o"), m_out[:, :]).then_inc(s_st, 16)
                    sp.wait_ge(s_nf, 1)
                    sp.dma_start(io["new_n"][L].rearrange("a d r -> (a d) r"), n_io[:, :]).then_inc(s_st, 16)
                    sp.wait_ge(s_st, 16 * (R + 2))

            own5 = sem("out_vector_steps")
            s_m5 = sem("head_mean_squares")
            s_r5 = sem("head_roots")
            s_yb = sem("mixed_ready")
            s_tr5 = sem("mixed_transposed")
            s_te5 = sem("mixed_t_ready")
            s_gb = sem("gate1_spread")
            s_gbe = sem("gate1_ready")
            s_o5 = sem("out_products")
            s_x5 = sem("residual_added")
            s_t5 = sem("out_banks_read")
            tmp5 = carve(big, 21504, 2, 512)

            def spread_gate(pe, m, done):
                for cnd in range(2):
                    for k in range(KD):
                        last = pe.matmul(ps[:, 4 + 2 * cnd + k // 4, (k % 4) * P:(k % 4 + 1) * P],
                                         mod_l[:, 8 * m + k, cnd:cnd + 1].broadcast_to([P, P]), ident[:, :], start=True, stop=True)
                last.then_inc(done, 1)

            with nc.Block() as block:
                @block.sync
                def _(sp):
                    sp.dma_start(w0, io["w_out"][L].rearrange("a (k p) n -> p (a k) n", p=P)).then_inc(s_w[3], 16)
                    sp.dma_start(w1, io["peer_wq"][L].rearrange("a (k p) n -> p (a k) n", p=P)[:, :, D:2 * D]).then_inc(s_w[5], 16)

                @block.vector
                def _(dve):
                    lane = Lane(dve, own5)
                    h20 = hm.rearrange("p t (h d) -> p (t h) d", d=DH)
                    j20 = k_n.rearrange("p t (h d) -> p (t h) d", d=DH)
                    lane.do(dve.tensor_tensor(j20, h20, h20, ALU.mult))
                    lane.settle()
                    lane.do(dve.tensor_reduce(ms2, j20, AX.X, ALU.add))
                    lane.settle()
                    lane.do(dve.tensor_scalar(ms2, ms2, 1.0 / DH, EPS, ALU.mult, ALU.add), s_m5)
                    for t in range(TILES):
                        lane.do(dve.tensor_tensor(y_nat[:, t, D_G:D], y_nat[:, t, D_G:D], normw[:, :], ALU.mult))
                    dve.wait_ge(s_r5, 1)
                    lane.do(dve.reciprocal(rs2, ms2))
                    lane.settle()
                    lane.do(dve.tensor_tensor(h20, h20, rs2.unsqueeze(2).broadcast_to([P, 20, DH]), ALU.mult))
                    lane.settle()
                    lane.do(dve.tensor_tensor(y_nat[:, :, D_G:D], y_nat[:, :, D_G:D], hm[:, :, :], ALU.mult), s_yb)
                    n = 0
                    dve.wait_ge(s_gbe, 1)
                    for t in range(TILES):
                        for half in range(2):
                            dve.wait_ge(s_o5, n + 1)
                            cnd = 1 if t == CTX else 0
                            sl = slice(half * 512, (half + 1) * 512)
                            if n >= 2:
                                lane.settle()
                            lane.do(dve.tensor_tensor(tmp5[:, n % 2, :], ps[:, n % 4, :], gate_b[:, cnd, sl], ALU.mult), s_t5)
                            lane.settle()
                            lane.do(dve.tensor_tensor(x_res[:, t, sl], x_res[:, t, sl], tmp5[:, n % 2, :], ALU.add))
                            n += 1

                @block.scalar
                def _(act):
                    act.wait_ge(s_m5, 1)
                    act.activation(ms2, ms2, ACT.Sqrt).then_inc(s_r5, 1)
                    act.wait_ge(s_gb, 1)
                    act.activation(gate_b.rearrange("p a b -> p (a b)"), ps[:, 4:8, :].rearrange("p a b -> p (a b)"), ACT.Copy).then_inc(s_gbe, 1)
                    for k in range(KD):
                        act.wait_ge(s_tr5, k + 1)
                        act.activation(h_t[:, k, :], pair(k % 4)[:, 0:T], ACT.Copy).then_inc(s_te5, 1)

                @block.tensor
                def _(pe):
                    pe.wait_ge(s_m5, 1)
                    spread_gate(pe, 2, s_gb)
                    pe.wait_ge(s_yb, 1)
                    for k in range(KD):
                        if k == 2:
                            pe.wait_ge(s_gbe, 1)
                        if k >= 4:
                            pe.wait_ge(s_te5, k - 3)
                        for t in range(TILES):
                            last = pe.transpose(pair(k % 4)[:, t * P:(t + 1) * P], y_nat[:, t, k * P:(k + 1) * P], ident[:, :])
                        last.then_inc(s_tr5, 1)
                    pe.wait_ge(s_te5, KD)
                    pe.wait_ge(s_w[3], 16)
                    n = 0
                    for t in range(TILES):
                        for half in range(2):
                            if n >= 4:
                                pe.wait_ge(s_t5, n - 3)
                            for k in range(KD):
                                last = pe.matmul(ps[:, n % 4, :], h_t[:, k, t * P:(t + 1) * P],
                                                 w0[:, k, half * 512:(half + 1) * 512], start=(k == 0), stop=(k == KD - 1))
                            last.then_inc(s_o5, 1)
                            n += 1

            s_key = sem("keys_loaded")
            with nc.Block() as block:
                @block.sync
                def _(sp):
                    sp.dma_start(w0, io["peer_wq"][L].rearrange("a (k p) n -> p (a k) n", p=P)[:, :, 0:D]).then_inc(s_w[4], 16)
                    sp.dma_start(keys_t, of("keys_t", "a p g k -> p (a g) k")).then_inc(s_key, 16)

            norm_block("norm2", 3, 4, True)

            own6 = sem("topk_vector_steps")
            s_q = sem("queries")
            s_qe = sem("queries_copied")
            s_s = sem("key_scores")
            s_top = sem("keys_chosen")
            with nc.Block() as block:
                @block.tensor
                def _(pe):
                    for g in range(2 * PH + 1):
                        if g < 2 * PH:
                            w = wq[g // PH]
                            if g % PH == 0:
                                pe.wait_ge(s_w[4 + g // PH], 16)
                            if g >= 2:
                                pe.wait_ge(s_qe, g - 1)
                            for a, b in ((0, NS), (NS, T)):
                                for k in range(KD):
                                    last = pe.matmul(pair(g % 2)[:, a:b], w[:, k, (g % PH) * P:(g % PH + 1) * P], h_t[:, k, a:b],
                                                     start=(k == 0), stop=(k == KD - 1))
                            last.then_inc(s_q, 1)
                        if g >= 1:
                            f = g - 1
                            if f == 0:
                                pe.wait_ge(s_key, 16)
                            pe.wait_ge(s_qe, f + 1)
                            if f >= 2:
                                pe.wait_ge(s_top, f - 1)
                            for t in range(TILES):
                                last = pe.matmul(pair(2 + f % 2)[:, t * P:(t + 1) * P], q_ts[:, f % 2, t * P:(t + 1) * P],
                                                 keys_t[:, f, :], start=True, stop=True)
                            last.then_inc(s_s, 1)

                @block.scalar
                def _(act):
                    for g in range(2 * PH):
                        act.wait_ge(s_q, g + 1)
                        if g >= 2:
                            act.wait_ge(s_s, g - 1)
                        act.activation(q_ts[:, g % 2, :], pair(g % 2)[:, 0:T], ACT.Copy).then_inc(s_qe, 1)

                @block.vector
                def _(dve):
                    lane = Lane(dve, own6)
                    for g in range(2 * PH):
                        dve.wait_ge(s_s, g + 1)
                        src = [pair(2 + g % 2)[:, t * P:(t + 1) * P] for t in range(TILES)]
                        cut = [sc2[:, g % 2, t * P:(t + 1) * P] for t in range(TILES)]
                        for t in range(TILES):
                            lane.do(dve.max(top_v[:, t, g, 0:8], src[t]))
                        lane.settle()
                        for t in range(TILES):
                            lane.do(dve.match_replace(cut[t], top_v[:, t, g, 0:8], src[t], LOWEST))
                        for t in range(TILES):
                            lane.do(dve.max_index(top_i[:, t, g, 0:8], top_v[:, t, g, 0:8], src[t]))
                        lane.settle()
                        for t in range(TILES):
                            lane.do(dve.max(top_v[:, t, g, 8:16], cut[t]))
                        lane.settle()
                        for t in range(TILES - 1):
                            lane.do(dve.max_index(top_i[:, t, g, 8:16], top_v[:, t, g, 8:16], cut[t]))
                        lane.do(dve.max_index(top_i[:, CTX, g, 8:16], top_v[:, CTX, g, 8:16], cut[CTX]), s_top)

            own7 = sem("pair_vector_steps")
            s_b7 = sem("pair_best")
            s_e7 = sem("pair_exponentials")
            with nc.Fori(0, TILES) as t:
                Tt = bass.ds(t, 1)
                with nc.Block() as block:
                    @block.vector
                    def _(dve):
                        lane = Lane(dve, own7)
                        tv = top_v[:, Tt, :, :].rearrange("p a (h x) k -> p (a h) x k", x=2)
                        ti = top_i[:, Tt, :, :].rearrange("p a g k -> p (a g) k")
                        c4 = cand.rearrange("p h (a b) -> p h a b", b=TOPK)
                        lane.do(dve.tensor_copy(top_if, ti))
                        lane.do(dve.tensor_copy(c4, tv[:, :, 0, :].unsqueeze(3).broadcast_to([P, PH, TOPK, TOPK])))
                        lane.settle()
                        lane.do(dve.tensor_tensor(c4, c4, tv[:, :, 1, :].unsqueeze(2).broadcast_to([P, PH, TOPK, TOPK]), ALU.add))
                        lane.settle()
                        for h in range(PH):
                            lane.do(dve.max(best[:, h, 0:8], cand[:, h, :]))
                        lane.settle()
                        for h in range(PH):
                            lane.do(dve.match_replace(cand2[:, h, :], best[:, h, 0:8], cand[:, h, :], LOWEST))
                        for h in range(PH):
                            lane.do(dve.max_index(pos[:, h, 0:8], best[:, h, 0:8], cand[:, h, :]))
                        lane.settle()
                        for h in range(PH):
                            lane.do(dve.max(best[:, h, 8:16], cand2[:, h, :]))
                        lane.settle()
                        for h in range(PH):
                            lane.do(dve.max_index(pos[:, h, 8:16], best[:, h, 8:16], cand2[:, h, :]))
                        lane.settle()
                        g_t = exp_gate[:, Tt, :].rearrange("p a (h k) -> p (a h) k", k=TOPK)
                        lane.do(dve.tensor_tensor(g_t, best, best[:, :, 0:1].broadcast_to([P, PH, TOPK]), ALU.subtract))
                        lane.do(dve.tensor_scalar(pa, pos, 4, None, ALU.logical_shift_right))
                        lane.do(dve.tensor_scalar(pb, pos, 15, None, ALU.bitwise_and))
                        lane.settle()
                        dve.engine_nop().then_inc(s_b7, 1)
                        lane.do(dve.tensor_copy(paf, pa))
                        lane.do(dve.tensor_copy(pbf, pb))
                        lane.settle()
                        it = iota16[:, :].unsqueeze(1).unsqueeze(1).broadcast_to([P, PH, TOPK, TOPK])
                        tif = top_if.rearrange("p (h x) k -> p h x k", x=2)
                        c24 = cand2.rearrange("p h (a b) -> p h a b", b=TOPK)
                        for buf, q in ((c4, paf), (c24, pbf)):
                            lane.do(dve.tensor_tensor(buf, q.unsqueeze(3).broadcast_to([P, PH, TOPK, TOPK]), it, ALU.is_equal))
                        lane.settle()
                        for x, buf in enumerate((c4, c24)):
                            lane.do(dve.tensor_tensor(buf, buf, tif[:, :, x, :].unsqueeze(2).broadcast_to([P, PH, TOPK, TOPK]), ALU.mult))
                        lane.settle()
                        lane.do(dve.tensor_reduce(i1f, c4, AX.X, ALU.add))
                        lane.do(dve.tensor_reduce(i2f, c24, AX.X, ALU.add))
                        lane.settle()
                        lane.do(dve.scalar_tensor_tensor(out=i1f, in0=i1f, scalar=float(N_KEYS), in1=i2f, op0=ALU.mult, op1=ALU.add))
                        lane.settle()
                        lane.do(dve.tensor_scalar(exp_idx[:, Tt, :].rearrange("p a (h k) -> p (a h) k", k=TOPK), i1f,
                                                  exp_base[:, 0:1], None, ALU.add))
                        dve.wait_ge(s_e7, 1)
                        sm = den.rearrange("p a h -> p (a h)")
                        lane.do(dve.tensor_reduce(sm, g_t, AX.X, ALU.add))
                        lane.settle()
                        lane.do(dve.reciprocal(sm, sm))
                        lane.settle()
                        lane.do(dve.tensor_tensor(g_t, g_t, sm.unsqueeze(2).broadcast_to([P, PH, TOPK]), ALU.mult))
                        lane.settle()

                    @block.scalar
                    def _(act):
                        act.wait_ge(s_b7, 1)
                        act.activation(exp_gate[:, Tt, :], exp_gate[:, Tt, :], ACT.Exp).then_inc(s_e7, 1)

                with nc.Block() as block:
                    @block.gpsimd
                    def _(pool):
                        for s in (own7, s_b7, s_e7):
                            pool.sem_clear(s)

            s_gb2 = sem("gate2_spread")
            s_gbe2 = sem("gate2_ready")
            with nc.Block() as block:
                @block.vector
                def _(dve):
                    dve.tensor_scalar(exp_base[:, :], exp_base[:, :], float(N_EXPERTS), None, ALU.add).then_inc(s_gbe2, 1)
                    dve.wait_ge(s_gb2, 1)
                    dve.tensor_copy(gate_b.rearrange("p a b -> p (a b)"), ps[:, 4:8, :].rearrange("p a b -> p (a b)")).then_inc(s_gbe2, 1)

                @block.tensor
                def _(pe):
                    spread_gate(pe, 5, s_gb2)

            s_dot = sem("dots_done")
            s_act = sem("gelus_done")
            s_cur = sem("token_rows_copied")
            s_ic = sem("indices_copied")
            s_wa = sem("weights_ready")
            s_dg = sem("diagonals_ready")
            s_pv = sem("v_rows_used")
            own8 = sem("expert_vector_steps")
            per_tile = (s_dot, s_act, s_cur, s_ic, s_wa, s_dg, s_pv, own8)

            def expert_tile(t, cnd):
                Tt = bass.ds(t, 1)
                turn = l * TILES + t
                with nc.Block() as block:
                    @block.gpsimd
                    def _(pool):
                        pool.tensor_copy(idx_cur, exp_idx[:, Tt, :].rearrange("p a k -> p (a k)")).then_inc(s_ic, 1)
                        pool.wait_ge(s_ic, 1)

                        def u_row(h, k):
                            if h >= 1:
                                pool.wait_ge(s_dot, (h - 1) * TOPK + k + 1)
                            pool.indirect_dma_start(
                                out=u_ring[:, k, :], out_offset=None, in_=io["peer_u"][:, :],
                                in_offset=bass.IndirectOffsetOnAxis(ap=idx_cur[:, h * TOPK + k:h * TOPK + k + 1], axis=0),
                            ).then_inc(s_gu[k], 16)

                        def v_row(h, k):
                            n = h * TOPK + k
                            if n >= VSLOTS:
                                pool.wait_ge(s_pv, n - VSLOTS + 1)
                            pool.indirect_dma_start(
                                out=v_ring[:, n % VSLOTS, :], out_offset=None, in_=io["peer_v"][:, :],
                                in_offset=bass.IndirectOffsetOnAxis(ap=idx_cur[:, n:n + 1], axis=0),
                            ).then_inc(s_gv[n % VSLOTS], 16)

                        for k in range(TOPK):
                            u_row(0, k)
                        for h in range(PH):
                            for k in range(TOPK):
                                if h + 1 < PH:
                                    u_row(h + 1, k)
                                v_row(h, k)

                    @block.vector
                    def _(dve):
                        lane = Lane(dve, own8)
                        lane.do(dve.tensor_copy(h_cur, y_nat[:, Tt, :].rearrange("p a d -> p (a d)")))
                        lane.settle()
                        for h in range(PH):
                            for k in range(TOPK):
                                dve.wait_ge(s_gu[k], 16 * (turn * PH + h + 1))
                                lane.do(dve.tensor_tensor_reduce(out=u_ring[:, k, :], in0=u_ring[:, k, :], in1=h_cur,
                                                                 scale=1.0, scalar=0.0, op0=ALU.mult, op1=ALU.add,
                                                                 accum_out=act_c[:, h % 2, k:k + 1]), s_dot)
                            dve.wait_ge(s_act, h + 1)
                            lane.do(dve.tensor_tensor(wact[:, h % 2, :], act_c[:, h % 2, :],
                                                      exp_gate[:, Tt, h * TOPK:(h + 1) * TOPK].rearrange("p a k -> p (a k)"), ALU.mult))
                            lane.settle()
                            if h >= 1:
                                dve.wait_ge(s_pv, h * TOPK)
                            for k in range(TOPK):
                                lane.do(dve.tensor_scalar(diag[:, k, :], ident[:, :], wact[:, h % 2, k:k + 1], None, ALU.mult), s_dg)
                        dve.wait_ge(s_pv, PH * TOPK)
                        lane.do(dve.tensor_tensor(h_cur, ps[:, 0:2, :].rearrange("p a b -> p (a b)"), gate_b[:, cnd, :], ALU.mult))
                        lane.settle()
                        xt = x_res[:, Tt, :].rearrange("p a d -> p (a d)")
                        lane.do(dve.tensor_tensor(xt, xt, h_cur, ALU.add))
                        lane.settle()

                    @block.scalar
                    def _(act):
                        for h in range(PH):
                            act.wait_ge(s_dot, (h + 1) * TOPK)
                            act.activation(act_c[:, h % 2, :], act_c[:, h % 2, :], ACT.Gelu_apprx_tanh).then_inc(s_act, 1)

                    @block.tensor
                    def _(pe):
                        for h in range(PH):
                            for k in range(TOPK):
                                n = h * TOPK + k
                                pe.wait_ge(s_dg, n + 1)
                                pe.wait_ge(s_gv[n % VSLOTS], 16 * (turn * (PH * TOPK // VSLOTS) + n // VSLOTS + 1))
                                for half in range(2):
                                    last = pe.matmul(ps[:, half, :], diag[:, k, :], v_ring[:, n % VSLOTS, half * 512:(half + 1) * 512],
                                                     start=(n == 0), stop=(n == PH * TOPK - 1))
                                last.then_inc(s_pv, 1)

                with nc.Block() as block:
                    @block.gpsimd
                    def _(pool):
                        for s in per_tile:
                            pool.sem_clear(s)

            with nc.Fori(0, SAMPLE_TILES) as t:
                expert_tile(t, 0)
            expert_tile(CTX, 1)

            with nc.Block() as block:
                @block.gpsimd
                def _(pool):
                    for s in cleared:
                        pool.sem_clear(s)

        own9 = sem("final_vector_steps")
        s_fw = sem("final_weight_loaded")
        s_m9 = sem("final_mean_squares")
        s_r9 = sem("final_roots")
        s_y9 = sem("final_rows")
        s_out = sem("outputs_stored")
        fw = gates_area[:, 0:D]
        with nc.Block() as block:
            @block.sync
            def _(sp):
                sp.dma_start(fw, io["final_norm_w"].broadcast_to([P, D])).then_inc(s_fw, 16)
                for t in range(TILES):
                    sp.wait_ge(s_y9, t + 1)
                    dst = io["y_prompt"][0] if t == CTX else io["y_sample"][0, t * P:(t + 1) * P, :]
                    sp.dma_start(dst, y_nat[:, t, :]).then_inc(s_out, 16)
                sp.wait_ge(s_out, 16 * TILES)

            @block.scalar
            def _(act):
                act.wait_ge(s_m9, 1)
                act.activation(stat[:, 0, 0:TILES], stat[:, 0, 0:TILES], ACT.Sqrt).then_inc(s_r9, 1)

            @block.vector
            def _(dve):
                lane = Lane(dve, own9)
                ss = stat[:, 0, 0:TILES]
                for t in range(TILES):
                    lane.do(dve.tensor_tensor_reduce(out=y_nat[:, t, :], in0=x_res[:, t, :], in1=x_res[:, t, :],
                                                     scale=1.0, scalar=0.0, op0=ALU.mult, op1=ALU.add,
                                                     accum_out=stat[:, 0, t:t + 1]))
                lane.settle()
                lane.do(dve.tensor_scalar(ss, ss, 1.0 / D, EPS, ALU.mult, ALU.add), s_m9)
                dve.wait_ge(s_r9, 1)
                dve.wait_ge(s_fw, 16)
                lane.do(dve.reciprocal(stat[:, 1, 0:TILES], ss))
                lane.settle()
                for t in range(TILES):
                    lane.do(dve.scalar_tensor_tensor(out=y_nat[:, t, :], in0=x_res[:, t, :], scalar=stat[:, 1, t:t + 1],
                                                     in1=fw, op0=ALU.mult, op1=ALU.mult), s_y9)


def kernel(**inputs):
    import numpy as np
    import concourse.bacc as bacc
    from concourse.bass_utils import run_bass_kernel_spmd

    a = {k: np.ascontiguousarray(v) for k, v in inputs.items()}
    w_g = a["w_in"][:, :, D_IN - 4 * HEADS:].reshape(DEPTH, KD, P, 2, 2, HEADS)
    w_gate = np.zeros((DEPTH, P, KD, 2, ROWS), np.float32)
    b_gate = np.zeros((DEPTH, ROWS, 2), np.float32)
    state_m = np.zeros((DEPTH, ROWS, 1), np.float32)
    for d in range(2):
        rows = slice(32 * d, 32 * d + HEADS)
        w_gate[..., rows] = w_g[:, :, :, d].transpose(0, 2, 1, 3, 4)
        b_gate[:, rows, :] = a["b_gate"].reshape(DEPTH, 2, 2, HEADS)[:, d].transpose(0, 2, 1)
        state_m[:, rows, 0] = a["state_m"][0, :, d]
    cols = lambda v: v.reshape(KD, P).T
    arrays = {
        "x_sample": a["x_sample"], "x_prompt": a["x_prompt"],
        "cond_t": np.stack([cols(a["c"][0]), cols(a["c_ctx"])], axis=2),
        "w_mod": a["w_mod"], "bmod_t": a["b_mod"].reshape(DEPTH, 48, P).transpose(2, 0, 1),
        "w_in": a["w_in"], "w_gate": w_gate, "b_gate": b_gate, "state_m": state_m,
        "conv_w": a["conv_w"].reshape(DEPTH, 9, KD, P).transpose(0, 3, 2, 1),
        "w_st": a["w_s"].transpose(0, 3, 1, 2), "b_st": a["b_s"].transpose(0, 2, 1),
        "mlstm_norm_w": a["mlstm_norm_w"],
        "state_C": a["state_C"].reshape(DEPTH, R, DH, DH),
        "state_n": a["state_n"].reshape(DEPTH, R, DH).transpose(0, 2, 1),
        "w_out": a["w_out"], "peer_wq": a["peer_wq"],
        "keys_t": a["peer_keys"].reshape(DEPTH, 2 * PH, N_KEYS, DH).transpose(0, 3, 1, 2),
        "peer_u": a["peer_u"].reshape(DEPTH * N_EXPERTS, D), "peer_v": a["peer_v"].reshape(DEPTH * N_EXPERTS, D),
        "final_norm_w": a["final_norm_w"].reshape(1, D),
    }
    arrays = {k: np.ascontiguousarray(v) for k, v in arrays.items()}
    outs = {
        "y_prompt": (1, P, D), "y_sample": (1, NS, D), "new_C": (DEPTH, R, DH, DH),
        "new_n": (DEPTH, DH, R), "new_m": (DEPTH, ROWS, 1),
    }
    nc = bacc.Bacc("TRN2", target_bir_lowering=False, num_devices=1)
    io = {k: nc.dram_tensor(f"in_{k}", v.shape, mybir.dt.from_np(v.dtype), kind="ExternalInput").ap() for k, v in arrays.items()}
    io.update({k: nc.dram_tensor(f"out_{k}", s, F32, kind="ExternalOutput").ap() for k, s in outs.items()})
    build(nc, io)
    r = run_bass_kernel_spmd(nc, [{f"in_{k}": v for k, v in arrays.items()}], core_ids=[0]).results[0]
    return (r["out_y_prompt"], r["out_y_sample"], r["out_new_C"].reshape(1, DEPTH, 2, HEADS, DH, DH),
            r["out_new_n"].transpose(0, 2, 1).reshape(1, DEPTH, 2, HEADS, DH),
            r["out_new_m"].reshape(1, DEPTH, 2, ROWS // 2)[..., 0:HEADS])
```

```python
from contextlib import ExitStack

import concourse.bass as bass
from concourse import mybir

F32 = mybir.dt.float32
U32 = mybir.dt.uint32
I32 = mybir.dt.int32
ALU = mybir.AluOpType
ACT = mybir.ActivationFunctionType
AX = mybir.AxisListType

P = 128
D = 1024
KD = D // P
SAMPLE_TILES = 4
TILES = SAMPLE_TILES + 1
CTX = TILES - 1
T = TILES * P
NS = SAMPLE_TILES * P
DEPTH = 2
GRID_W = 64
HEADS = 4
DH = 128
R = 2 * HEADS
ROWS = 64
D_G = 512
D_IN = 2 * D_G + 4 * D_G + 4 * HEADS
N_KEYS = 128
N_EXPERTS = N_KEYS * N_KEYS
PH = 8
TOPK = 16
EPS = 1e-6
LOWEST = -3.0e38
DENSE = 3
ND = DENSE * P
GATHERED = (3, 4)
USLOTS, VSLOTS = TOPK, 8
OCT = 8
STEPS = N_KEYS // (len(GATHERED) * PH)
VA = DH + 1


class Lane:

    def __init__(self, eng, own):
        self.eng, self.own, self.sent, self.settled = eng, own, {}, {}

    def do(self, ins, sem=None):
        sem = self.own if sem is None else sem
        ins.then_inc(sem, 1)
        self.sent[sem.name] = (sem, self.sent.get(sem.name, (sem, 0))[1] + 1)
        return ins

    def settle(self):
        for name, (sem, n) in self.sent.items():
            if self.settled.get(name) != n:
                self.eng.wait_ge(sem, n)
                self.settled[name] = n


def build(nc, io):
    ctx = ExitStack()
    cleared = []

    def sb(name, shape, dt=F32):
        return ctx.enter_context(nc.sbuf_tensor(name, shape, dt))

    def sem(name):
        s = ctx.enter_context(nc.semaphore(name))
        cleared.append(s)
        return s

    with ctx:
        x_res = sb("x_res", [P, TILES, D])
        y_nat = sb("y_nat", [P, TILES, D])
        big = sb("big", [P, 32000])
        gates_area = sb("gates_area", [P, 4480])
        kn_area = sb("kn_area", [P, 2560])
        ident = sb("ident", [P, P])
        ones_row = sb("ones_row", [ROWS, P])
        cap = sb("cap", [P, 2, P])
        iota16 = sb("iota16", [P, TOPK])
        cond_t = sb("cond_t", [P, KD, 2])
        mod_t = sb("mod_t", [P, DEPTH, 48, 2])
        bmod_t = sb("bmod_t", [P, DEPTH, 48])
        mod_l = sb("mod_l", [P, 48, 2])
        wgate = sb("wgate", [P, KD, 2, ROWS])
        bgate = sb("bgate", [ROWS, 2])
        convw = sb("convw", [P, KD, 9])
        wst = sb("wst", [P, HEADS, P])
        bst = sb("bst", [P, HEADS])
        normw = sb("normw", [P, D_G])
        m0 = sb("m0", [ROWS, 1])
        stat = sb("stat", [P, 4, 24])
        cols = sb("cols", [P, 4, TILES, R])
        decb = sb("decb", [P, R, TILES])
        small = sb("small", [ROWS, 4, TILES])
        m_out = sb("m_out", [ROWS, 1])
        n_io = sb("n_io", [P, R])
        exp_base = sb("exp_base", [P, 1])
        spare = sb("spare", [P, 2])
        gate_dram = nc.dram_tensor("expert_gates", (N_KEYS, P, ND), F32, kind="Internal").ap()
        den = sb("den", [P, 2, HEADS])
        ps = ctx.enter_context(nc.psum_tensor("ps", [P, 8, 512], F32))

        def carve(area, at, *shape, dt=None):
            n = 1
            for s in shape:
                n *= s
            v = area[:, at:at + n]
            if dt is not None:
                v = v.bitcast(dt)
            if len(shape) == 2:
                return v.rearrange("p (a b) -> p a b", a=shape[0])
            if len(shape) == 3:
                return v.rearrange("p (a b c) -> p a b c", a=shape[0], b=shape[1])
            return v

        h_t = carve(big, 0, KD, T)
        w0 = carve(big, 5120, KD, D)
        w1 = carve(big, 5120 + 8192, KD, D)
        wq = [w0, w1]
        qk_t = carve(big, 21504, KD, T)
        v_a = carve(big, 26624, TILES, HEADS, VA)
        vs = carve(big, 29204, TILES, D_G)
        hm = vs
        p_w = carve(big, 5120 + 8192, R, T)
        kw = carve(big, 5120 + 8192 + R * T, 2, D_G)
        cn = carve(big, 5120, R, VA)
        hn = carve(big, 5120 + R * VA, HEADS, VA)
        k_n = carve(kn_area, 0, TILES, D_G)
        gate_b = carve(kn_area, 0, 2, D)
        keys_t = carve(kn_area, 0, 2 * PH, N_KEYS)

        def rows(i):
            return gates_area[0:ROWS, i * T:(i + 1) * T]

        g_a, g_lf, g_b, g_m, g_wp, g_em, g_nm = [rows(i) for i in range(7)]
        g_we = g_lf
        exp_idx = carve(gates_area, 0, TILES, P, dt=U32)
        exp_gate = carve(gates_area, T, TILES, P)
        exp_i1 = carve(gates_area, 2 * T, TILES, P)
        exp_i2 = carve(gates_area, 3 * T, TILES, P)
        q_ts = carve(big, 21504, 2, T)
        sc2 = carve(big, 21504 + 1280, 2, T)
        top_v = carve(big, 21504 + 2560, TILES, 2 * PH, TOPK)
        top_i = carve(big, 21504 + 3840, TILES, 2 * PH, TOPK, dt=U32)
        cand = carve(big, 26624, PH, 256)
        cand2 = carve(big, 26624 + 2048, PH, 256)
        best = carve(big, 30720, PH, TOPK)
        pos = carve(big, 30848, PH, TOPK, dt=U32)
        pa = carve(big, 30976, PH, TOPK, dt=U32)
        pb = carve(big, 31104, PH, TOPK, dt=U32)
        paf = carve(big, 31232, PH, TOPK)
        pbf = carve(big, 31360, PH, TOPK)
        i1f = carve(big, 31488, PH, TOPK)
        i2f = carve(big, 31616, PH, TOPK)
        top_if = carve(big, 31744, 2 * PH, TOPK)
        gate_s = carve(big, 5120, N_KEYS, P)
        hot1 = carve(big, 21504, 2, OCT, P)
        hot2 = carve(big, 21504 + 2 * OCT * P, 2, OCT, P)
        choice_t = carve(big, 25600, 3, P)
        choice_c = carve(big, 25984, 2, 3, OCT)
        iota_k = big[:, 26048:26048 + N_KEYS]
        u_ring = carve(big, 5120, USLOTS, D)
        v_ring = carve(big, 21504, VSLOTS, D)
        acc = big[:, 29696:30720]
        v_s = [big[:, 30720:31744], y_nat[:, 2, :]]
        u_s = [y_nat[:, n, :].rearrange("p (k e) -> p k e", e=P) for n in range(2)]
        g_s = [gates_area[:, 4096:4096 + ND], kn_area[:, 2048:2048 + ND]]
        gelu_s = [gates_area[:, 2560:2560 + ND], gates_area[:, 2944:2944 + ND]]
        h_s = [gates_area[:, 3328:3328 + ND], gates_area[:, 3712:3712 + ND]]
        act_c = kn_area[:, 2432:2432 + TOPK]
        wact = kn_area[:, 2448:2448 + TOPK]

        def pair(q):
            return ps[:, 2 * q:2 * q + 2, :].rearrange("p a b -> p (a b)")

        s_in = sem("inputs_loaded")
        s_const = sem("constants_made")
        s_load = sem("layer_loaded")
        s_cond = sem("condition_activated")
        s_ml = sem("layer_modulation_copied")
        with nc.Block() as block:
            @block.sync
            def _(sp):
                sp.dma_start(x_res[:, 0:SAMPLE_TILES, :], io["x_sample"].rearrange("a (t p) d -> p (a t) d", p=P)).then_inc(s_in, 16)
                sp.dma_start(x_res[:, CTX, :], io["x_prompt"].rearrange("a p d -> (a p) d")).then_inc(s_in, 16)
                sp.dma_start(cond_t[:, :, :], io["cond_t"]).then_inc(s_in, 16)
                sp.dma_start(bmod_t[:, :, :], io["bmod_t"]).then_inc(s_in, 16)
                sp.wait_ge(s_in, 64)

            @block.gpsimd
            def _(pool):
                lane = Lane(pool, s_const)
                lane.do(pool.memset(ident[:, :], 0.0))
                lane.do(pool.memset(cap[:, :, :], 0.0))
                lane.do(pool.memset(ones_row[:, :], 1.0))
                lane.do(pool.memset(exp_base[:, :], 0.0))
                lane.do(pool.memset(m_out[:, :], 0.0))
                lane.do(pool.iota(iota16[:, :], pattern=[[1, TOPK]], base=0, channel_multiplier=0,
                                  allow_small_or_imprecise_dtypes=True))
                lane.settle()
                lane.do(pool.affine_select(out=ident[:, :], in_=ident[:, :], compare_op=ALU.not_equal, fill=1.0,
                                           base=0, pattern=[[-1, P]], channel_multiplier=1))
                lane.do(pool.affine_select(out=cap[:, 0, :], in_=cap[:, 0, :], compare_op=ALU.is_ge, fill=LOWEST,
                                           base=0, pattern=[[1, P]], channel_multiplier=-1))
                lane.do(pool.affine_select(out=cap[:, 1, :], in_=cap[:, 1, :], compare_op=ALU.is_ge, fill=LOWEST,
                                           base=0, pattern=[[-1, P]], channel_multiplier=1))
                lane.settle()

            @block.scalar
            def _(act):
                act.wait_ge(s_in, 64)
                nc.scalar.activation(cond_t[:, :, :], cond_t[:, :, :], ACT.Silu).then_inc(s_cond, 1)

        s_wm = [sem("mod_weights_0"), sem("mod_weights_1")]
        s_wm_used = sem("mod_weights_used")
        s_mod = sem("mod_ready")
        NB = DEPTH * 6
        wmod = io["w_mod"].rearrange("l (k p) (j n) -> l j p k n", p=P, n=D)
        with nc.Block() as block:
            @block.sync
            def _(sp):
                for j in range(NB):
                    if j >= 2:
                        sp.wait_ge(s_wm_used, j - 1)
                    sp.dma_start(wq[j % 2], wmod[j // 6, j % 6]).then_inc(s_wm[j % 2], 16)

            @block.tensor
            def _(pe):
                for j in range(NB):
                    pe.wait_ge(s_wm[j % 2], 16 * (j // 2 + 1))
                    if j >= 2:
                        pe.wait_ge(s_mod, j - 1)
                    for n in range(8):
                        for k in range(KD):
                            last = pe.matmul(ps[:, j % 2, 2 * n:2 * n + 2], wq[j % 2][:, k, n * P:(n + 1) * P],
                                             cond_t[:, k, :], start=(k == 0), stop=(k == KD - 1))
                    last.then_inc(s_wm_used, 1)

            @block.vector
            def _(dve):
                for j in range(NB):
                    l, m = j // 6, j % 6
                    dve.wait_ge(s_wm_used, j + 1)
                    dve.scalar_tensor_tensor(
                        out=mod_t[:, l, 8 * m:8 * m + 8, :],
                        in0=ps[:, j % 2, 0:16].rearrange("p (a b) -> p a b", b=2),
                        scalar=1.0 if m in (1, 4) else 0.0,
                        in1=bmod_t[:, l, 8 * m:8 * m + 8].unsqueeze(2).broadcast_to([P, 8, 2]),
                        op0=ALU.add, op1=ALU.add).then_inc(s_mod, 1)

        s_gu = [ctx.enter_context(nc.semaphore(f"u_row_{k}")) for k in range(USLOTS)]
        s_gv = [ctx.enter_context(nc.semaphore(f"v_row_{k}")) for k in range(VSLOTS)]

        with nc.Fori(0, DEPTH) as l:
            L = bass.ds(l, 1)

            def of(name, pattern):
                return io[name][L].rearrange(pattern)

            win = io["w_in"][L].rearrange("a (k p) n -> p (a k) n", p=P)
            s_w = [sem(f"w_{n}") for n in ("uv", "qk", "vo", "out", "q0", "q1")]
            with nc.Block() as block:
                @block.sync
                def _(sp):
                    sp.dma_start(wgate[:, :, :, :], of("w_gate", "a p k g r -> p (a k) g r")).then_inc(s_load, 16)
                    sp.dma_start(bgate[:, :], of("b_gate", "a p g -> p (a g)")).then_inc(s_load, 16)
                    sp.dma_start(convw[:, :, :], of("conv_w", "a p k n -> p (a k) n")).then_inc(s_load, 16)
                    sp.dma_start(wst[:, :, :], of("w_st", "a p h t -> p (a h) t")).then_inc(s_load, 16)
                    sp.dma_start(bst[:, :], of("b_st", "a p h -> p (a h)")).then_inc(s_load, 16)
                    sp.dma_start(normw[:, :], of("mlstm_norm_w", "a n -> a n").broadcast_to([P, D_G])).then_inc(s_load, 16)
                    sp.dma_start(m0[:, :], of("state_m", "a p o -> (a p) o")).then_inc(s_load, 16)
                    sp.dma_start(w1, win[:, :, 2 * D_G:4 * D_G]).then_inc(s_w[1], 16)
                    sp.dma_start(w0, win[:, :, 0:2 * D_G]).then_inc(s_w[0], 16)
                    sp.wait_ge(s_load, 7 * 16)

                @block.vector
                def _(dve):
                    dve.tensor_copy(mod_l[:, :, :], mod_t[:, L, :, :].rearrange("p a b c -> p (a b) c")).then_inc(s_ml, 1)

            def norm_block(tag, sh, sc, natural):
                own = sem(f"{tag}_vector_steps")
                s_ms = sem(f"{tag}_mean_squares")
                s_sq = sem(f"{tag}_roots")
                s_xn = sem(f"{tag}_normalised")
                s_tr = sem(f"{tag}_transposed")
                s_ht = sem(f"{tag}_ht_latent")
                s_hc = sem(f"{tag}_ht_context")
                s_back = sem(f"{tag}_back")
                s_nat = sem(f"{tag}_natural")
                ss, rs = stat[:, 0, 0:TILES], stat[:, 1, 0:TILES]
                with nc.Block() as block:
                    @block.vector
                    def _(dve):
                        lane = Lane(dve, own)
                        for t in range(TILES):
                            lane.do(dve.tensor_tensor_reduce(out=y_nat[:, t, :], in0=x_res[:, t, :], in1=x_res[:, t, :],
                                                             scale=1.0, scalar=0.0, op0=ALU.mult, op1=ALU.add,
                                                             accum_out=stat[:, 0, t:t + 1]))
                        lane.settle()
                        lane.do(dve.tensor_scalar(ss, ss, 1.0 / D, EPS, ALU.mult, ALU.add), s_ms)
                        dve.wait_ge(s_sq, 1)
                        lane.do(dve.reciprocal(rs, ss))
                        lane.settle()
                        for t in range(TILES):
                            lane.do(dve.tensor_scalar(y_nat[:, t, :], x_res[:, t, :], stat[:, 1, t:t + 1], None, ALU.mult), s_xn)
                        for k in range(KD):
                            dve.wait_ge(s_tr, k + 1)
                            lane.do(dve.tensor_scalar(h_t[:, k, NS:T], pair(k % 4)[:, NS:T], mod_l[:, 8 * sc + k, 1:2],
                                                      mod_l[:, 8 * sh + k, 1:2], ALU.mult, ALU.add), s_hc)

                    @block.scalar
                    def _(act):
                        act.wait_ge(s_ms, 1)
                        act.activation(ss, ss, ACT.Sqrt).then_inc(s_sq, 1)
                        for k in range(KD):
                            act.wait_ge(s_tr, k + 1)
                            act.activation(h_t[:, k, 0:NS], pair(k % 4)[:, 0:NS], ACT.Identity,
                                           bias=mod_l[:, 8 * sh + k, 0:1], scale=mod_l[:, 8 * sc + k, 0:1]).then_inc(s_ht, 1)
                        for t in range(TILES if natural else 0):
                            act.wait_ge(s_back, t + 1)
                            act.activation(y_nat[:, t, :], pair(t % 4), ACT.Copy).then_inc(s_nat, 1)

                    @block.tensor
                    def _(pe):
                        for k in range(KD):
                            if k == 0:
                                pe.wait_ge(s_xn, TILES)
                            if k >= 4:
                                pe.wait_ge(s_ht, k - 3)
                                pe.wait_ge(s_hc, k - 3)
                            for t in range(TILES):
                                last = pe.transpose(pair(k % 4)[:, t * P:(t + 1) * P], y_nat[:, t, k * P:(k + 1) * P], ident[:, :])
                            last.then_inc(s_tr, 1)
                        for t in range(TILES if natural else 0):
                            if t == 0:
                                pe.wait_ge(s_ht, KD)
                                pe.wait_ge(s_hc, KD)
                            if t >= 4:
                                pe.wait_ge(s_nat, t - 3)
                            for k in range(KD):
                                last = pe.transpose(pair(t % 4)[:, k * P:(k + 1) * P], h_t[:, k, t * P:(t + 1) * P], ident[:, :])
                            last.then_inc(s_back, 1)

            norm_block("norm1", 0, 1, False)

            own = sem("proj_vector_steps")
            s_gmm = sem("gate_products")
            s_ones = sem("v_ones_made")
            s_qk = sem("qk_products")
            s_conv = sem("qk_convolved")
            s_convfree = sem("qk_banks_free")
            s_silu = sem("qk_silu")
            s_kn = sem("k_scaled")
            s_uv = sem("uv_products")
            s_uve = sem("uv_evacuated")
            s_neg = sem("gate_minus_abs")
            s_sp = sem("gate_softplus")
            s_aown = sem("proj_scalar_steps")
            s_rowx = sem("gate_rows_ready")
            s_rowe = sem("gate_rows_exponentials")
            s_w0free = sem("uv_weights_used")
            ig_ps, fg_ps = pair(2)[0:ROWS, 0:T], pair(3)[0:ROWS, 0:T]
            with nc.Block() as block:
                @block.sync
                def _(sp):
                    sp.wait_ge(s_w0free, 1)
                    sp.dma_start(w0, win[:, :, 4 * D_G:6 * D_G]).then_inc(s_w[2], 16)

                @block.tensor
                def _(pe):
                    for g in range(2):
                        for a, b in ((0, NS), (NS, T)):
                            for k in range(KD):
                                last = pe.matmul(pair(2 + g)[0:ROWS, a:b], wgate[:, k, g, :], h_t[:, k, a:b],
                                                 start=(k == 0), stop=(k == KD - 1))
                        last.then_inc(s_gmm, 1)
                    pe.wait_ge(s_w[1], 16)
                    for j in range(KD):
                        if j >= 2:
                            pe.wait_ge(s_convfree, j - 1)
                        for a, b in ((0, NS), (NS, T)):
                            for k in range(KD):
                                last = pe.matmul(pair(j % 2)[:, a:b], w1[:, k, j * P:(j + 1) * P], h_t[:, k, a:b],
                                                 start=(k == 0), stop=(k == KD - 1))
                        last.then_inc(s_qk, 1)
                    n = 0
                    for phase in range(2):
                        pe.wait_ge(s_w[0] if phase == 0 else s_w[2], 16)
                        for half in range(2):
                            for t in range(TILES):
                                if n < 4:
                                    pe.wait_ge(s_neg, 1)
                                else:
                                    pe.wait_ge(s_uve, n - 3)
                                for k in range(KD):
                                    last = pe.matmul(ps[:, 4 + n % 4, :], h_t[:, k, t * P:(t + 1) * P],
                                                     w0[:, k, half * D_G:(half + 1) * D_G],
                                                     start=(k == 0), stop=(k == KD - 1))
                                last.then_inc(s_uv, 1)
                                n += 1
                        if phase == 0:
                            pe.wait_ge(s_uv, n)
                            pe.sem_inc(s_w0free, 1)

                @block.scalar
                def _(act):
                    act.wait_ge(s_neg, 1)
                    act.activation(g_wp, g_wp, ACT.Exp).then_inc(s_aown, 1)
                    act.wait_ge(s_aown, 1)
                    act.activation(g_wp, g_wp, ACT.Ln, bias=1.0).then_inc(s_sp, 1)
                    for j in range(KD):
                        act.wait_ge(s_conv, j + 1)
                        act.activation(qk_t[:, j, :], qk_t[:, j, :], ACT.Silu).then_inc(s_silu, 1)
                    n = 0
                    for phase in range(2):
                        for half in range(2):
                            for t in range(TILES):
                                act.wait_ge(s_uv, n + 1)
                                src = ps[:, 4 + n % 4, :]
                                if phase == 0 and half == 0:
                                    act.activation(y_nat[:, t, 0:D_G], src, ACT.Copy).then_inc(s_uve, 1)
                                elif phase == 0:
                                    act.activation(vs[:, t, :], src, ACT.Copy).then_inc(s_uve, 1)
                                elif half == 0:
                                    act.activation(v_a[:, t, :, 0:DH], src.rearrange("p (h d) -> p h d", d=DH),
                                                   ACT.Copy).then_inc(s_uve, 1)
                                else:
                                    act.activation(y_nat[:, t, D_G:D], src, ACT.Sigmoid).then_inc(s_uve, 1)
                                n += 1
                    act.wait_ge(s_rowx, 1)
                    act.activation(g_wp, g_wp, ACT.Exp, scale=-1.0).then_inc(s_rowe, 1)
                    act.activation(g_em, g_em, ACT.Exp, scale=-1.0).then_inc(s_rowe, 1)
                    act.activation(g_we, g_we, ACT.Exp).then_inc(s_rowe, 1)
                    act.activation(small[:, 2, :], small[:, 2, :], ACT.Exp).then_inc(s_rowe, 1)

                @block.gpsimd
                def _(pool):
                    pool.memset(v_a[:, :, :, DH:VA], 1.0).then_inc(s_ones, 1)
                    for j in range(HEADS, KD):
                        pool.wait_ge(s_silu, j + 1)
                        pool.tensor_scalar(qk_t[:, j, :], qk_t[:, j, :], float(DH) ** -0.5, None, ALU.mult).then_inc(s_kn, 1)

                @block.vector
                def _(dve):
                    lane = Lane(dve, own)
                    dve.wait_ge(s_gmm, 2)
                    lane.do(dve.tensor_scalar(g_a, ig_ps, bgate[:, 0:1], None, ALU.add))
                    lane.do(dve.tensor_scalar(g_lf, fg_ps, bgate[:, 1:2], None, ALU.add))
                    lane.settle()
                    lane.do(dve.tensor_scalar(g_nm, g_lf, -1.0, None, ALU.mult))
                    lane.settle()
                    lane.do(dve.tensor_tensor(g_wp, g_lf, g_nm, ALU.min), s_neg)
                    lane.settle()
                    for j in range(KD):
                        src, dst = pair(j % 2), qk_t[:, j, :]
                        dve.wait_ge(s_qk, j + 1)
                        lane.do(dve.tensor_scalar(dst, src[:, 0:T], convw[:, j, 4:5], None, ALU.mult))
                        g_src = src[:, 0:NS].rearrange("p (r c) -> p r c", c=GRID_W)
                        g_dst = dst[:, 0:NS].rearrange("p (r c) -> p r c", c=GRID_W)
                        rr = NS // GRID_W
                        for tap in range(9):
                            di, dj = tap // 3 - 1, tap % 3 - 1
                            if tap == 4:
                                continue
                            r0, r1 = max(0, -di), rr - max(0, di)
                            c0, c1 = max(0, -dj), GRID_W - max(0, dj)
                            lane.settle()
                            out = g_dst[:, r0:r1, c0:c1]
                            if di == 0:
                                o2 = dst[:, NS + c0:T - max(0, dj)]
                                lane.do(dve.scalar_tensor_tensor(out=o2, in0=src[:, NS + c0 + dj:T - max(0, dj) + dj],
                                                                 scalar=convw[:, j, tap:tap + 1], in1=o2,
                                                                 op0=ALU.mult, op1=ALU.add))
                            lane.do(dve.scalar_tensor_tensor(out=out, in0=g_src[:, r0 + di:r1 + di, c0 + dj:c1 + dj],
                                                             scalar=convw[:, j, tap:tap + 1], in1=out,
                                                             op0=ALU.mult, op1=ALU.add))
                        lane.settle()
                        dve.engine_nop().then_inc(s_convfree, 1)
                        dve.engine_nop().then_inc(s_conv, 1)
                    dve.wait_ge(s_sp, 1)
                    lane.do(dve.scalar_tensor_tensor(out=g_lf, in0=g_lf, scalar=0.0, in1=g_wp, op0=ALU.min, op1=ALU.subtract))
                    lane.settle()

                    def span(row, c, back, dir_):
                        lo, hi = 32 * dir_, 32 * dir_ + HEADS
                        if not back:
                            return row[lo:hi, c * P:(c + 1) * P]
                        first, last = (c + 1) * P - 1, c * P - 1
                        return row[lo:hi, first:(last if last >= 0 else None):-1]

                    lane.do(dve.memset(g_b, 0.0))
                    lane.do(dve.memset(g_m, 0.0))
                    lane.do(dve.memset(small[:, :, :], 0.0))
                    lane.settle()
                    for c in range(TILES):
                        for d in range(2):
                            lane.do(dve.tensor_tensor_scan(span(g_b, c, d == 1, d), ones_row[32 * d:32 * d + HEADS, :],
                                                           span(g_lf, c, d == 1, d), 0.0, ALU.mult, ALU.add))
                    lane.settle()
                    lane.do(dve.tensor_tensor(g_a, g_a, g_b, ALU.subtract))
                    lane.do(dve.tensor_copy(small[0:HEADS, 0, 0:1], m0[0:HEADS, :]))
                    lane.do(dve.tensor_copy(small[32:32 + HEADS, 0, SAMPLE_TILES - 1:SAMPLE_TILES], m0[32:32 + HEADS, :]))
                    lane.settle()
                    for i in range(TILES):
                        for d in range(2):
                            c = i if d == 0 or i == CTX else SAMPLE_TILES - 1 - i
                            lo, hi = 32 * d, 32 * d + HEADS
                            sa = span(g_a, c, d == 1, d)
                            lane.do(dve.tensor_tensor_scan(span(g_m, c, d == 1, d), sa, sa, small[lo:hi, 0, c:c + 1],
                                                           ALU.max, ALU.max))
                        lane.settle()
                        for d in range(2):
                            c = i if d == 0 or i == CTX else SAMPLE_TILES - 1 - i
                            lo, hi = 32 * d, 32 * d + HEADS
                            end = c * P + (P - 1 if d == 0 else 0)
                            lane.do(dve.tensor_copy(small[lo:hi, 1, c:c + 1], g_m[lo:hi, end:end + 1]))
                            nxt = m_out[lo:hi, :] if i == CTX else None
                            if i < SAMPLE_TILES - 1:
                                cc = i + 1 if d == 0 else SAMPLE_TILES - 2 - i
                                nxt = small[lo:hi, 0, cc:cc + 1]
                            if nxt is not None:
                                lane.do(dve.tensor_tensor(nxt, g_b[lo:hi, end:end + 1], g_m[lo:hi, end:end + 1], ALU.add))
                        lane.settle()
                    by_c = lambda row: row.rearrange("p (c t) -> p c t", t=P)
                    spread = lambda q: small[:, q, :].unsqueeze(2).broadcast_to([ROWS, TILES, P])
                    lane.do(dve.tensor_scalar(g_nm, g_m, -1.0, None, ALU.mult))
                    lane.do(dve.tensor_tensor(by_c(g_wp), by_c(g_m), spread(0), ALU.subtract))
                    lane.do(dve.tensor_tensor(g_em, g_b, g_m, ALU.add))
                    lane.do(dve.tensor_tensor(by_c(g_we), by_c(g_a), spread(1), ALU.subtract))
                    lane.do(dve.tensor_tensor(small[:, 2, :], small[:, 0, :], small[:, 1, :], ALU.subtract))
                    lane.settle()
                    dve.engine_nop().then_inc(s_rowx, 1)

            own2 = sem("gmlp_vector_steps")
            s_v2 = sem("gmlp_mean_squares")
            s_r2 = sem("gmlp_roots")
            s_vh = sem("gmlp_normalised")
            s_mix = sem("gmlp_products")
            s_ya = sem("gmlp_done")
            s_ct = sem("gate_columns_transposed")
            s_kt = sem("k_transposed")
            s_ke = sem("k_natural")
            s_colr = sem("gate_columns_read")
            s_scr = sem("gmlp_squares")
            ms2, rs2 = stat[:, 2, 0:20], stat[:, 3, 0:20]
            with nc.Block() as block:
                @block.vector
                def _(dve):
                    lane = Lane(dve, own2)
                    v20 = vs.rearrange("p t (h d) -> p (t h) d", d=DH)
                    k20 = k_n.rearrange("p t (h d) -> p (t h) d", d=DH)
                    lane.do(dve.tensor_tensor(k20, v20, v20, ALU.mult))
                    lane.settle()
                    lane.do(dve.tensor_reduce(ms2, k20, AX.X, ALU.add))
                    lane.settle()
                    lane.do(dve.tensor_scalar(ms2, ms2, 1.0 / DH, EPS, ALU.mult, ALU.add), s_v2)
                    dve.wait_ge(s_ct, 1)
                    c20 = cols.rearrange("p q c r -> p (q c) r")
                    t20 = ps[:, 4:7, :].rearrange("p a b -> p (a b)")[:, 0:20 * ROWS].rearrange("p (n r) -> p n r", r=ROWS)
                    lane.do(dve.tensor_copy(c20[:, :, 0:HEADS], t20[:, :, 0:HEADS]))
                    lane.do(dve.tensor_copy(c20[:, :, HEADS:R], t20[:, :, 32:32 + HEADS]))
                    lane.do(dve.tensor_copy(decb.rearrange("p r c -> p (r c)"), ps[:, 7, 0:R * TILES]))
                    dve.wait_ge(s_r2, 1)
                    lane.do(dve.reciprocal(rs2, ms2))
                    lane.settle()
                    lane.do(dve.tensor_tensor(v20, v20, rs2.unsqueeze(2).broadcast_to([P, 20, DH]), ALU.mult), s_vh)
                    for h in range(HEADS):
                        dve.wait_ge(s_mix, h + 1)
                        for a, b in ((0, SAMPLE_TILES), (SAMPLE_TILES, TILES)):
                            yv = y_nat[:, a:b, h * DH:(h + 1) * DH]
                            lane.do(dve.scalar_tensor_tensor(
                                out=yv, in0=pair(h % 2)[:, a * P:b * P].rearrange("p (t d) -> p t d", d=DH),
                                scalar=bst[:, h:h + 1], in1=yv, op0=ALU.add, op1=ALU.mult), s_ya)

                @block.scalar
                def _(act):
                    act.wait_ge(s_v2, 1)
                    act.activation(ms2, ms2, ACT.Sqrt).then_inc(s_r2, 1)
                    for c in range(TILES):
                        act.wait_ge(s_kt, c + 1)
                        act.activation(k_n[:, c, :], ps[:, c % 4 if c < 4 else 0, :], ACT.Copy).then_inc(s_ke, 1)

                @block.tensor
                def _(pe):
                    for q, row in enumerate((g_a, g_wp, g_em, g_we)):
                        for c in range(TILES):
                            n = (q * TILES + c) * ROWS
                            pe.transpose(ps[:, 4 + n // 512, n % 512:n % 512 + ROWS], row[:, c * P:(c + 1) * P],
                                         ident[0:ROWS, 0:ROWS])
                    for r in range(R):
                        row = 32 * (r // HEADS) + r % HEADS
                        last = pe.matmul(ps[:, 7, r * TILES:(r + 1) * TILES],
                                         ident[0:ROWS, row:row + 1].broadcast_to([ROWS, P]), small[:, 2, :],
                                         start=True, stop=True)
                    last.then_inc(s_ct, 1)
                    pe.wait_ge(s_v2, 1)
                    for c in range(TILES):
                        if c == 4:
                            pe.wait_ge(s_ke, 1)
                        for h in range(HEADS):
                            last = pe.transpose(ps[:, c % 4, h * DH:(h + 1) * DH], qk_t[:, HEADS + h, c * P:(c + 1) * P], ident[:, :])
                        last.then_inc(s_kt, 1)
                    pe.wait_ge(s_vh, 1)
                    pe.wait_ge(s_ke, TILES)
                    for h in range(HEADS):
                        if h >= 2:
                            pe.wait_ge(s_ya, 2 * (h - 1))
                        for a, b in ((0, SAMPLE_TILES), (SAMPLE_TILES, TILES)):
                            last = pe.matmul(pair(h % 2)[:, a * P:b * P], wst[:, h, :],
                                             vs[:, a:b, h * DH:(h + 1) * DH], start=True, stop=True)
                        last.then_inc(s_mix, 1)

            own3 = sem("intra_vector_steps")
            s_sc = sem("scores")
            s_nm = sem("minus_m_spread")
            s_e1 = sem("exponents")
            s_e2 = sem("exponents_capped")
            s_e3 = sem("exponentials")
            s_p = sem("intra_weights")
            s_cl = sem("states_loaded")
            with nc.Block() as block:
                @block.sync
                def _(sp):
                    sp.dma_start(cn[:, :, 0:DH], of("state_C", "a r d e -> d (a r) e")).then_inc(s_cl, 16)
                    sp.dma_start(n_io[:, :], of("state_n", "a d r -> d (a r)")).then_inc(s_cl, 16)
                    sp.wait_ge(s_cl, 32)

                @block.tensor
                def _(pe):
                    for h in range(HEADS):
                        if h:
                            pe.wait_ge(s_p, 2 * h)
                        for c in range(TILES):
                            last = pe.matmul(pair(0)[:, c * P:(c + 1) * P], qk_t[:, HEADS + h, c * P:(c + 1) * P],
                                             qk_t[:, h, c * P:(c + 1) * P], start=True, stop=True)
                        last.then_inc(s_sc, 1)
                        for d in range(2):
                            row = 32 * d + h
                            for a, b in ((0, NS), (NS, T)):
                                last = pe.matmul(pair(1 + d)[:, a:b], ident[0:ROWS, row:row + 1].broadcast_to([ROWS, P]),
                                                 g_nm[:, a:b], start=True, stop=True)
                            last.then_inc(s_nm, 1)

                @block.vector
                def _(dve):
                    n = 0
                    for h in range(HEADS):
                        for d in range(2):
                            r = d * HEADS + h
                            dve.wait_ge(s_nm, n + d + 1)
                            dve.tensor_tensor(p_w[:, r, :].rearrange("p (c t) -> p c t", t=P),
                                              pair(1 + d)[:, 0:T].rearrange("p (c t) -> p c t", t=P),
                                              cols[:, 0, :, r:r + 1].broadcast_to([P, TILES, P]), ALU.add).then_inc(s_e1, 1)
                        dve.wait_ge(s_sc, h + 1)
                        for d in range(2):
                            r = d * HEADS + h
                            dve.wait_ge(s_e3, n + d + 1)
                            dve.tensor_tensor(p_w[:, r, :], pair(0)[:, 0:T], p_w[:, r, :], ALU.mult).then_inc(s_p, 1)
                        n += 2

                @block.gpsimd
                def _(pool):
                    for n in range(R):
                        h, d = n // 2, n % 2
                        pool.wait_ge(s_e1, n + 1)
                        v = p_w[:, d * HEADS + h, :].rearrange("p (c t) -> p c t", t=P)
                        pool.tensor_tensor(v, v, cap[:, d:d + 1, :].broadcast_to([P, TILES, P]), ALU.add).then_inc(s_e2, 1)

                @block.scalar
                def _(act):
                    for n in range(R):
                        h, d = n // 2, n % 2
                        act.wait_ge(s_e2, n + 1)
                        v = p_w[:, d * HEADS + h, :]
                        act.activation(v, v, ACT.Exp).then_inc(s_e3, 1)

            own4 = sem("chain_vector_steps")
            s_kw = sem("k_weighted")
            s_mm = sem("chain_products")
            s_hn = sem("chain_outputs_read")
            s_cn = sem("chain_state")
            s_n0 = sem("normaliser_placed")
            s_nf = sem("normaliser_taken")
            s_st = sem("states_stored")
            steps = []
            for i in range(TILES):
                for d in range(2):
                    steps.append((d, i if d == 0 or i == CTX else SAMPLE_TILES - 1 - i))
            heads_of = lambda b: ps[:, b:b + 2, 0:2 * VA].rearrange("p a (h e) -> p a h e", e=VA)
            four = lambda ap: ap.rearrange("p (a h) e -> p a h e", a=2)
            with nc.Block() as block:
                @block.gpsimd
                def _(pool):
                    for n, (d, c) in enumerate(steps):
                        if n >= 2:
                            pool.wait_ge(s_mm, n - 1)
                        pool.tensor_tensor(kw[:, n % 2, :].rearrange("p (h e) -> p h e", e=DH),
                                           k_n[:, c, :].rearrange("p (h e) -> p h e", e=DH),
                                           cols[:, 3, c, d * HEADS:(d + 1) * HEADS].unsqueeze(2).broadcast_to([P, HEADS, DH]),
                                           ALU.mult).then_inc(s_kw, 1)

                @block.tensor
                def _(pe):
                    for n, (d, c) in enumerate(steps):
                        pe.wait_ge(s_kw, n + 1)
                        if n == 0:
                            pe.wait_ge(s_n0, 1)
                        if n >= 1:
                            pe.wait_ge(s_cn, n)
                        for h in range(HEADS):
                            r = d * HEADS + h
                            b, e = h // 2, (h % 2) * VA
                            if c != CTX:
                                pe.matmul(ps[:, b, e:e + VA], qk_t[:, h, c * P:(c + 1) * P], cn[:, r, :], start=True, stop=True)
                            pe.matmul(ps[:, 2 + b, e:e + VA], p_w[:, r, c * P:(c + 1) * P], v_a[:, c, h, :], start=True, stop=True)
                            last = pe.matmul(ps[:, 4 + b, e:e + VA], kw[:, n % 2, h * DH:(h + 1) * DH], v_a[:, c, h, :],
                                             start=True, stop=True)
                        last.then_inc(s_mm, 1)

                @block.vector
                def _(dve):
                    lane = Lane(dve, own4)
                    lane.do(dve.memset(hm[:, :, :], 0.0))
                    lane.do(dve.tensor_copy(cn[:, :, DH], n_io[:, :]), s_n0)
                    hn4 = four(hn)
                    for n, (d, c) in enumerate(steps):
                        rr = slice(d * HEADS, (d + 1) * HEADS)
                        dve.wait_ge(s_mm, n + 1)
                        lane.settle()
                        if c != CTX:
                            wp = cols[:, 1, c, rr].unsqueeze(2).broadcast_to([P, HEADS, VA])
                            lane.do(dve.tensor_tensor(hn4, heads_of(0), four(wp), ALU.mult))
                            dec = decb[:, rr, c:c + 1].broadcast_to([P, HEADS, VA])
                            lane.do(dve.tensor_tensor(cn[:, rr, :], cn[:, rr, :], dec, ALU.mult))
                            lane.settle()
                            lane.do(dve.tensor_tensor(hn4, hn4, heads_of(2), ALU.add))
                            lane.do(dve.tensor_tensor(four(cn[:, rr, :]), four(cn[:, rr, :]), heads_of(4), ALU.add), s_cn)
                        else:
                            lane.do(dve.tensor_copy(hn4, heads_of(2)))
                            lane.do(dve.tensor_copy(four(cn[:, rr, :]), heads_of(4)), s_cn)
                        lane.settle()
                        dd = hn[:, :, DH:VA].rearrange("p h o -> p (h o)")
                        lane.do(dve.tensor_scalar(den[:, 0, :], dd, -1.0, None, ALU.mult))
                        lane.settle()
                        lane.do(dve.tensor_tensor(den[:, 0, :], den[:, 0, :], dd, ALU.max))
                        lane.settle()
                        lane.do(dve.tensor_tensor(den[:, 0, :], den[:, 0, :], cols[:, 2, c, rr], ALU.max))
                        lane.settle()
                        lane.do(dve.reciprocal(den[:, 1, :], den[:, 0, :]))
                        lane.settle()
                        lane.do(dve.tensor_tensor(hn[:, :, 0:DH], hn[:, :, 0:DH],
                                                  den[:, 1, :].unsqueeze(2).broadcast_to([P, HEADS, DH]), ALU.mult))
                        lane.settle()
                        hmc = hm[:, c, :].rearrange("p (h e) -> p h e", e=DH)
                        lane.do(dve.tensor_tensor(hmc, hmc, hn[:, :, 0:DH], ALU.add))
                    lane.do(dve.tensor_copy(n_io[:, :], cn[:, :, DH]), s_nf)
                    lane.settle()

                @block.sync
                def _(sp):
                    sp.wait_ge(s_cn, len(steps))
                    for r in range(R):
                        sp.dma_start(io["new_C"][L].rearrange("a r d e -> (a r) d e")[r], cn[:, r, 0:DH]).then_inc(s_st, 16)
                    sp.dma_start(io["new_m"][L].rearrange("a r o -> (a r) o"), m_out[:, :]).then_inc(s_st, 16)
                    sp.wait_ge(s_nf, 1)
                    sp.dma_start(io["new_n"][L].rearrange("a d r -> (a d) r"), n_io[:, :]).then_inc(s_st, 16)
                    sp.wait_ge(s_st, 16 * (R + 2))

            own5 = sem("out_vector_steps")
            s_m5 = sem("head_mean_squares")
            s_r5 = sem("head_roots")
            s_yb = sem("mixed_ready")
            s_tr5 = sem("mixed_transposed")
            s_te5 = sem("mixed_t_ready")
            s_gb = sem("gate1_spread")
            s_gbe = sem("gate1_ready")
            s_o5 = sem("out_products")
            s_x5 = sem("residual_added")
            s_t5 = sem("out_banks_read")
            tmp5 = carve(big, 21504, 2, 512)

            def spread_gate(pe, m, done):
                for cnd in range(2):
                    for k in range(KD):
                        last = pe.matmul(ps[:, 4 + 2 * cnd + k // 4, (k % 4) * P:(k % 4 + 1) * P],
                                         mod_l[:, 8 * m + k, cnd:cnd + 1].broadcast_to([P, P]), ident[:, :], start=True, stop=True)
                last.then_inc(done, 1)

            with nc.Block() as block:
                @block.sync
                def _(sp):
                    sp.dma_start(w0, io["w_out"][L].rearrange("a (k p) n -> p (a k) n", p=P)).then_inc(s_w[3], 16)
                    sp.dma_start(w1, io["peer_wq"][L].rearrange("a (k p) n -> p (a k) n", p=P)[:, :, D:2 * D]).then_inc(s_w[5], 16)

                @block.vector
                def _(dve):
                    lane = Lane(dve, own5)
                    h20 = hm.rearrange("p t (h d) -> p (t h) d", d=DH)
                    j20 = k_n.rearrange("p t (h d) -> p (t h) d", d=DH)
                    lane.do(dve.tensor_tensor(j20, h20, h20, ALU.mult))
                    lane.settle()
                    lane.do(dve.tensor_reduce(ms2, j20, AX.X, ALU.add))
                    lane.settle()
                    lane.do(dve.tensor_scalar(ms2, ms2, 1.0 / DH, EPS, ALU.mult, ALU.add), s_m5)
                    for t in range(TILES):
                        lane.do(dve.tensor_tensor(y_nat[:, t, D_G:D], y_nat[:, t, D_G:D], normw[:, :], ALU.mult))
                    dve.wait_ge(s_r5, 1)
                    lane.do(dve.reciprocal(rs2, ms2))
                    lane.settle()
                    lane.do(dve.tensor_tensor(h20, h20, rs2.unsqueeze(2).broadcast_to([P, 20, DH]), ALU.mult))
                    lane.settle()
                    lane.do(dve.tensor_tensor(y_nat[:, :, D_G:D], y_nat[:, :, D_G:D], hm[:, :, :], ALU.mult), s_yb)
                    n = 0
                    dve.wait_ge(s_gbe, 1)
                    for t in range(TILES):
                        for half in range(2):
                            dve.wait_ge(s_o5, n + 1)
                            cnd = 1 if t == CTX else 0
                            sl = slice(half * 512, (half + 1) * 512)
                            if n >= 2:
                                lane.settle()
                            lane.do(dve.tensor_tensor(tmp5[:, n % 2, :], ps[:, n % 4, :], gate_b[:, cnd, sl], ALU.mult), s_t5)
                            lane.settle()
                            lane.do(dve.tensor_tensor(x_res[:, t, sl], x_res[:, t, sl], tmp5[:, n % 2, :], ALU.add))
                            n += 1

                @block.scalar
                def _(act):
                    act.wait_ge(s_m5, 1)
                    act.activation(ms2, ms2, ACT.Sqrt).then_inc(s_r5, 1)
                    act.wait_ge(s_gb, 1)
                    act.activation(gate_b.rearrange("p a b -> p (a b)"), ps[:, 4:8, :].rearrange("p a b -> p (a b)"), ACT.Copy).then_inc(s_gbe, 1)
                    for k in range(KD):
                        act.wait_ge(s_tr5, k + 1)
                        act.activation(h_t[:, k, :], pair(k % 4)[:, 0:T], ACT.Copy).then_inc(s_te5, 1)

                @block.tensor
                def _(pe):
                    pe.wait_ge(s_m5, 1)
                    spread_gate(pe, 2, s_gb)
                    pe.wait_ge(s_yb, 1)
                    for k in range(KD):
                        if k == 2:
                            pe.wait_ge(s_gbe, 1)
                        if k >= 4:
                            pe.wait_ge(s_te5, k - 3)
                        for t in range(TILES):
                            last = pe.transpose(pair(k % 4)[:, t * P:(t + 1) * P], y_nat[:, t, k * P:(k + 1) * P], ident[:, :])
                        last.then_inc(s_tr5, 1)
                    pe.wait_ge(s_te5, KD)
                    pe.wait_ge(s_w[3], 16)
                    n = 0
                    for t in range(TILES):
                        for half in range(2):
                            if n >= 4:
                                pe.wait_ge(s_t5, n - 3)
                            for k in range(KD):
                                last = pe.matmul(ps[:, n % 4, :], h_t[:, k, t * P:(t + 1) * P],
                                                 w0[:, k, half * 512:(half + 1) * 512], start=(k == 0), stop=(k == KD - 1))
                            last.then_inc(s_o5, 1)
                            n += 1

            s_key = sem("keys_loaded")
            with nc.Block() as block:
                @block.sync
                def _(sp):
                    sp.dma_start(w0, io["peer_wq"][L].rearrange("a (k p) n -> p (a k) n", p=P)[:, :, 0:D]).then_inc(s_w[4], 16)
                    sp.dma_start(keys_t, of("keys_t", "a p g k -> p (a g) k")).then_inc(s_key, 16)

            norm_block("norm2", 3, 4, True)

            own6 = sem("topk_vector_steps")
            s_q = sem("queries")
            s_qe = sem("queries_copied")
            s_s = sem("key_scores")
            s_top = sem("keys_chosen")
            with nc.Block() as block:
                @block.tensor
                def _(pe):
                    for g in range(2 * PH + 1):
                        if g < 2 * PH:
                            w = wq[g // PH]
                            if g % PH == 0:
                                pe.wait_ge(s_w[4 + g // PH], 16)
                            if g >= 2:
                                pe.wait_ge(s_qe, g - 1)
                            for a, b in ((0, NS), (NS, T)):
                                for k in range(KD):
                                    last = pe.matmul(pair(g % 2)[:, a:b], w[:, k, (g % PH) * P:(g % PH + 1) * P], h_t[:, k, a:b],
                                                     start=(k == 0), stop=(k == KD - 1))
                            last.then_inc(s_q, 1)
                        if g >= 1:
                            f = g - 1
                            if f == 0:
                                pe.wait_ge(s_key, 16)
                            pe.wait_ge(s_qe, f + 1)
                            if f >= 2:
                                pe.wait_ge(s_top, f - 1)
                            for t in range(TILES):
                                last = pe.matmul(pair(2 + f % 2)[:, t * P:(t + 1) * P], q_ts[:, f % 2, t * P:(t + 1) * P],
                                                 keys_t[:, f, :], start=True, stop=True)
                            last.then_inc(s_s, 1)

                @block.scalar
                def _(act):
                    for g in range(2 * PH):
                        act.wait_ge(s_q, g + 1)
                        if g >= 2:
                            act.wait_ge(s_s, g - 1)
                        act.activation(q_ts[:, g % 2, :], pair(g % 2)[:, 0:T], ACT.Copy).then_inc(s_qe, 1)

                @block.vector
                def _(dve):
                    lane = Lane(dve, own6)
                    for g in range(2 * PH):
                        dve.wait_ge(s_s, g + 1)
                        src = [pair(2 + g % 2)[:, t * P:(t + 1) * P] for t in range(TILES)]
                        cut = [sc2[:, g % 2, t * P:(t + 1) * P] for t in range(TILES)]
                        for t in range(TILES):
                            lane.do(dve.max(top_v[:, t, g, 0:8], src[t]))
                        lane.settle()
                        for t in range(TILES):
                            lane.do(dve.match_replace(cut[t], top_v[:, t, g, 0:8], src[t], LOWEST))
                        for t in range(TILES):
                            lane.do(dve.max_index(top_i[:, t, g, 0:8], top_v[:, t, g, 0:8], src[t]))
                        lane.settle()
                        for t in range(TILES):
                            lane.do(dve.max(top_v[:, t, g, 8:16], cut[t]))
                        lane.settle()
                        for t in range(TILES - 1):
                            lane.do(dve.max_index(top_i[:, t, g, 8:16], top_v[:, t, g, 8:16], cut[t]))
                        lane.do(dve.max_index(top_i[:, CTX, g, 8:16], top_v[:, CTX, g, 8:16], cut[CTX]), s_top)

            own7 = sem("pair_vector_steps")
            s_b7 = sem("pair_best")
            s_e7 = sem("pair_exponentials")
            with nc.Fori(0, TILES) as t:
                Tt = bass.ds(t, 1)
                with nc.Block() as block:
                    @block.vector
                    def _(dve):
                        lane = Lane(dve, own7)
                        tv = top_v[:, Tt, :, :].rearrange("p a (h x) k -> p (a h) x k", x=2)
                        ti = top_i[:, Tt, :, :].rearrange("p a g k -> p (a g) k")
                        c4 = cand.rearrange("p h (a b) -> p h a b", b=TOPK)
                        lane.do(dve.tensor_copy(top_if, ti))
                        lane.do(dve.tensor_copy(c4, tv[:, :, 0, :].unsqueeze(3).broadcast_to([P, PH, TOPK, TOPK])))
                        lane.settle()
                        lane.do(dve.tensor_tensor(c4, c4, tv[:, :, 1, :].unsqueeze(2).broadcast_to([P, PH, TOPK, TOPK]), ALU.add))
                        lane.settle()
                        for h in range(PH):
                            lane.do(dve.max(best[:, h, 0:8], cand[:, h, :]))
                        lane.settle()
                        for h in range(PH):
                            lane.do(dve.match_replace(cand2[:, h, :], best[:, h, 0:8], cand[:, h, :], LOWEST))
                        for h in range(PH):
                            lane.do(dve.max_index(pos[:, h, 0:8], best[:, h, 0:8], cand[:, h, :]))
                        lane.settle()
                        for h in range(PH):
                            lane.do(dve.max(best[:, h, 8:16], cand2[:, h, :]))
                        lane.settle()
                        for h in range(PH):
                            lane.do(dve.max_index(pos[:, h, 8:16], best[:, h, 8:16], cand2[:, h, :]))
                        lane.settle()
                        g_t = exp_gate[:, Tt, :].rearrange("p a (h k) -> p (a h) k", k=TOPK)
                        lane.do(dve.tensor_tensor(g_t, best, best[:, :, 0:1].broadcast_to([P, PH, TOPK]), ALU.subtract))
                        lane.do(dve.tensor_scalar(pa, pos, 4, None, ALU.logical_shift_right))
                        lane.do(dve.tensor_scalar(pb, pos, 15, None, ALU.bitwise_and))
                        lane.settle()
                        dve.engine_nop().then_inc(s_b7, 1)
                        lane.do(dve.tensor_copy(paf, pa))
                        lane.do(dve.tensor_copy(pbf, pb))
                        lane.settle()
                        it = iota16[:, :].unsqueeze(1).unsqueeze(1).broadcast_to([P, PH, TOPK, TOPK])
                        tif = top_if.rearrange("p (h x) k -> p h x k", x=2)
                        c24 = cand2.rearrange("p h (a b) -> p h a b", b=TOPK)
                        for buf, q in ((c4, paf), (c24, pbf)):
                            lane.do(dve.tensor_tensor(buf, q.unsqueeze(3).broadcast_to([P, PH, TOPK, TOPK]), it, ALU.is_equal))
                        lane.settle()
                        for x, buf in enumerate((c4, c24)):
                            lane.do(dve.tensor_tensor(buf, buf, tif[:, :, x, :].unsqueeze(2).broadcast_to([P, PH, TOPK, TOPK]), ALU.mult))
                        lane.settle()
                        lane.do(dve.tensor_reduce(i1f, c4, AX.X, ALU.add))
                        lane.do(dve.tensor_reduce(i2f, c24, AX.X, ALU.add))
                        lane.settle()
                        lane.do(dve.tensor_copy(exp_i1[:, Tt, :].rearrange("p a (h k) -> p (a h) k", k=TOPK), i1f))
                        lane.do(dve.tensor_copy(exp_i2[:, Tt, :].rearrange("p a (h k) -> p (a h) k", k=TOPK), i2f))
                        lane.do(dve.scalar_tensor_tensor(out=paf, in0=i1f, scalar=float(N_KEYS), in1=i2f, op0=ALU.mult, op1=ALU.add))
                        lane.settle()
                        lane.do(dve.tensor_scalar(exp_idx[:, Tt, :].rearrange("p a (h k) -> p (a h) k", k=TOPK), paf,
                                                  exp_base[:, 0:1], None, ALU.add))
                        dve.wait_ge(s_e7, 1)
                        sm = den.rearrange("p a h -> p (a h)")
                        lane.do(dve.tensor_reduce(sm, g_t, AX.X, ALU.add))
                        lane.settle()
                        lane.do(dve.reciprocal(sm, sm))
                        lane.settle()
                        lane.do(dve.tensor_tensor(g_t, g_t, sm.unsqueeze(2).broadcast_to([P, PH, TOPK]), ALU.mult))
                        lane.settle()

                    @block.scalar
                    def _(act):
                        act.wait_ge(s_b7, 1)
                        act.activation(exp_gate[:, Tt, :], exp_gate[:, Tt, :], ACT.Exp).then_inc(s_e7, 1)

                with nc.Block() as block:
                    @block.gpsimd
                    def _(pool):
                        for s in (own7, s_b7, s_e7):
                            pool.sem_clear(s)

            s_gb2 = sem("gate2_spread")
            s_gbe2 = sem("gate2_ready")
            with nc.Block() as block:
                @block.vector
                def _(dve):
                    dve.tensor_scalar(exp_base[:, :], exp_base[:, :], float(N_EXPERTS), None, ALU.add).then_inc(s_gbe2, 1)
                    dve.wait_ge(s_gb2, 1)
                    dve.tensor_copy(gate_b.rearrange("p a b -> p (a b)"), ps[:, 4:8, :].rearrange("p a b -> p (a b)")).then_inc(s_gbe2, 1)

                @block.tensor
                def _(pe):
                    spread_gate(pe, 5, s_gb2)

            s_io = sem("key_row_made")
            s_f = sem("gates_formed")
            s_ft = sem("choices_transposed")
            s_fe = sem("gates_evacuated")
            s_cc = sem("choices_taken")
            s_oh = sem("one_hots")
            s_gst = sem("gates_stored")
            with nc.Block() as block:
                @block.gpsimd
                def _(pool):
                    pool.iota(iota_k, pattern=[[1, N_KEYS]], base=0, channel_multiplier=0,
                              allow_small_or_imprecise_dtypes=True).then_inc(s_io, 1)

                @block.tensor
                def _(pe):
                    for i in range(DENSE):
                        if i:
                            pe.wait_ge(s_fe, 18 * i)
                        pe.transpose(ps[:, 7, 0:P], exp_i1[:, i, :], ident[:, :]).then_inc(s_f, 1)
                        pe.transpose(ps[:, 7, P:2 * P], exp_i2[:, i, :], ident[:, :]).then_inc(s_f, 1)
                        pe.transpose(ps[:, 7, 2 * P:3 * P], exp_gate[:, i, :], ident[:, :]).then_inc(s_ft, 1)
                        with pe.Fori(0, P // (2 * OCT)) as m:
                            for par in range(2):
                                g = 2 * m + par
                                pe.wait_ge(s_oh, 16 * (16 * i + g + 1))
                                pe.wait_ge(s_fe, 18 * i + g + 1)
                                for tt in range(OCT):
                                    last = pe.matmul(pair(par)[:, tt * P:(tt + 1) * P], hot2[:, par, tt, :], hot1[:, par, tt, :],
                                                     start=True, stop=True)
                                last.then_inc(s_f, 1)

                @block.vector
                def _(dve):
                    dve.wait_ge(s_io, 1)
                    for i in range(DENSE):
                        dve.wait_ge(s_fe, 18 * i + 2)
                        with dve.Fori(0, P // (2 * OCT)) as m:
                            for par in range(2):
                                g = 2 * m + par
                                dve.wait_ge(s_f, 18 * i + g + 1)
                                dve.tensor_copy(choice_c[:, par, :, :], choice_t[:, :, bass.ds(OCT * g, OCT)]).then_inc(s_cc, 1)
                                dve.wait_ge(s_cc, 16 * i + g + 1)
                                for tt in range(OCT):
                                    at = lambda q: choice_c[:, par, q, tt:tt + 1]
                                    dve.tensor_scalar(hot1[:, par, tt, :], iota_k, at(0), at(2), ALU.is_equal, ALU.mult).then_inc(s_oh, 1)
                                    dve.tensor_scalar(hot2[:, par, tt, :], iota_k, at(1), None, ALU.is_equal).then_inc(s_oh, 1)

                @block.scalar
                def _(act):
                    for i in range(DENSE):
                        act.wait_ge(s_ft, i + 1)
                        if i:
                            act.wait_ge(s_oh, 256 * i)
                        act.activation(choice_t[:, 0:2, :], ps[:, 7, 0:2 * P].rearrange("p (a t) -> p a t", t=P), ACT.Copy).then_inc(s_fe, 1)
                        act.activation(choice_t[:, 2, :], ps[:, 7, 2 * P:3 * P], ACT.Copy).then_inc(s_fe, 1)
                        if i:
                            act.wait_ge(s_gst, 16 * i)
                        with act.Fori(0, P // (2 * OCT)) as m:
                            for par in range(2):
                                g = 2 * m + par
                                act.wait_ge(s_f, 18 * i + g + 3)
                                act.activation(gate_s[:, :, bass.ds(OCT * g, OCT)],
                                               pair(par).rearrange("p (t j) -> p j t", j=P), ACT.Copy).then_inc(s_fe, 1)

                @block.sync
                def _(sp):
                    for i in range(DENSE):
                        sp.wait_ge(s_fe, 18 * (i + 1))
                        sp.dma_start(gate_dram[:, :, i * P:(i + 1) * P].rearrange("j p t -> p j t"), gate_s).then_inc(s_gst, 16)
                    sp.wait_ge(s_gst, 16 * DENSE)

            s_us = [sem(f"u_stream_{n}") for n in range(2)]
            s_vs = [sem(f"v_stream_{n}") for n in range(2)]
            s_gs = [sem(f"gate_stream_{n}") for n in range(2)]
            s_a = sem("dense_scores")
            s_ge = sem("dense_gelus")
            s_h = sem("dense_weights")
            s_g2 = sem("dense_products")
            s_dot = sem("dots_done")
            s_act = sem("gathered_gelus")
            s_wa = sem("gathered_weights")
            s_ax = sem("v_rows_added")
            own8 = sem("expert_vector_steps")
            s_fin = sem("dense_finished")
            with nc.Block() as block:
                @block.sync
                def _(sp):
                    def load(j, par):
                        e = bass.ds(l * N_KEYS + j, 1)
                        return (lambda: sp.dma_start(u_s[par], io["peer_ut"][e].rearrange("a p (k e) -> p (a k) e", e=P)).then_inc(s_us[par], 16),
                                lambda: sp.dma_start(g_s[par], gate_dram[bass.ds(j, 1)].rearrange("a p t -> p (a t)")).then_inc(s_gs[par], 16),
                                lambda: sp.dma_start(v_s[par], io["peer_v"].rearrange("(e p) d -> e p d", p=P)[e].rearrange("a p d -> p (a d)")).then_inc(s_vs[par], 16))

                    for par in range(2):
                        for go in load(par, par):
                            go()
                    with sp.Fori(0, N_KEYS // 2 - 1) as m:
                        for par in range(2):
                            u, g, v = load(2 * m + 2 + par, par)
                            sp.wait_ge(s_a, 2 * m + par + 1)
                            u()
                            sp.wait_ge(s_h, 2 * m + par + 3)
                            g()
                            sp.wait_ge(s_g2, 2 * m + par + 3)
                            v()

                @block.tensor
                def _(pe):
                    def scores(par, u_count, free):
                        pe.wait_ge(s_us[par], u_count)
                        pe.wait_ge(s_ge, free)
                        for k in range(KD):
                            last = pe.matmul(ps[:, 6 + par, 0:ND], u_s[par][:, k, :], h_t[:, k, 0:ND], start=(k == 0), stop=(k == KD - 1))
                        last.then_inc(s_a, 1)

                    def products(par, v_count, ready):
                        pe.wait_ge(s_vs[par], v_count)
                        pe.wait_ge(s_h, ready)
                        for n in range(2 * DENSE):
                            last = pe.matmul(ps[:, n, :], h_s[par][:, (n // 2) * P:(n // 2 + 1) * P],
                                             v_s[par][:, (n % 2) * 512:(n % 2 + 1) * 512], start=False, stop=False, skip_group_check=True)
                        last.then_inc(s_g2, 1)

                    pe.wait_ge(s_h, 2)
                    for n in range(2 * DENSE):
                        last = pe.matmul(ps[:, n, :], h_s[1 if n == 2 * DENSE - 1 else 0][:, 0:P],
                                         ident[:, :].unsqueeze(1).broadcast_to([P, 4, P]), start=True, stop=False, skip_group_check=True)
                        if n >= 2 * DENSE - 2:
                            last.then_inc(s_g2, 1)
                    scores(0, 16, 1)
                    with pe.Fori(0, N_KEYS // 2 - 1) as m:
                        scores(1, 16 * (m + 1), 2 * m + 2)
                        products(0, 16 * (m + 1), 2 * m + 3)
                        scores(0, 16 * (m + 2), 2 * m + 3)
                        products(1, 16 * (m + 1), 2 * m + 4)
                    scores(1, 16 * (N_KEYS // 2), N_KEYS)
                    products(0, 16 * (N_KEYS // 2), N_KEYS + 1)
                    products(1, 16 * (N_KEYS // 2), N_KEYS + 2)

                @block.scalar
                def _(act):
                    for n in range(2):
                        act.activation(spare[:, n:n + 1], ident[:, n:n + 1], ACT.Copy).then_inc(s_ge, 1)
                    for i in range(len(GATHERED)):
                        with act.Fori(0, PH) as h:
                            u = h + i * PH
                            for jj in range(STEPS):
                                act.wait_ge(s_a, u * STEPS + jj + 1)
                                act.wait_ge(s_h, u * STEPS + jj + 1)
                                act.activation(gelu_s[jj % 2], ps[:, 6 + jj % 2, 0:ND], ACT.Gelu_apprx_tanh).then_inc(s_ge, 1)
                                if jj == STEPS // 2 - 1:
                                    act.wait_ge(s_dot, (u + 1) * TOPK)
                                    act.activation(act_c, act_c, ACT.Gelu_apprx_tanh).then_inc(s_act, 1)

                @block.vector
                def _(dve):
                    for n in range(2):
                        dve.memset(h_s[n], 0.0).then_inc(s_h, 1)
                    lane = Lane(dve, own8)
                    for i, tile in enumerate(GATHERED):
                        dve.memset(acc, 0.0).then_inc(s_ax, 1)
                        with dve.Fori(0, PH) as h:
                            u = h + i * PH
                            for jj in range(STEPS):
                                j = u * STEPS + jj
                                dve.wait_ge(s_ge, j + 3)
                                dve.wait_ge(s_gs[jj % 2], 16 * (u * (STEPS // 2) + jj // 2 + 1))
                                dve.wait_ge(s_g2, j + 1)
                                dve.tensor_tensor(h_s[jj % 2], gelu_s[jj % 2], g_s[jj % 2], ALU.mult).then_inc(s_h, 1)
                                if jj < STEPS // 2:
                                    for k in range(4 * jj, 4 * jj + 4):
                                        dve.wait_ge(s_gu[k], 16 * (l * 16 + u + 1))
                                        dve.tensor_tensor_reduce(out=u_ring[:, k, :], in0=u_ring[:, k, :], in1=y_nat[:, tile, :],
                                                                 scale=1.0, scalar=0.0, op0=ALU.mult, op1=ALU.add,
                                                                 accum_out=act_c[:, k:k + 1]).then_inc(s_dot, 1)
                                    continue
                                if jj == STEPS // 2:
                                    dve.wait_ge(s_act, u + 1)
                                    dve.wait_ge(s_ax, i + 1 + u * TOPK)
                                    dve.tensor_tensor(wact, act_c, exp_gate[:, tile, bass.ds(h * TOPK, TOPK)], ALU.mult).then_inc(s_wa, 1)
                                    dve.wait_ge(s_wa, u + 1)
                                for k in range(4 * jj - 16, 4 * jj - 12):
                                    v = v_ring[:, k % VSLOTS, :]
                                    dve.wait_ge(s_gv[k % VSLOTS], 16 * (2 * (l * 16 + u) + k // VSLOTS + 1))
                                    dve.wait_ge(s_ax, i + 1 + u * TOPK + k)
                                    dve.scalar_tensor_tensor(out=acc, in0=v, scalar=wact[:, k:k + 1], in1=acc,
                                                             op0=ALU.mult, op1=ALU.add).then_inc(s_ax, 1)
                        dve.wait_ge(s_ax, (i + 1) * (1 + PH * TOPK))
                        lane.do(dve.tensor_tensor(acc, acc, gate_b[:, 1 if tile == CTX else 0, :], ALU.mult))
                        lane.settle()
                        lane.do(dve.tensor_tensor(x_res[:, tile, :], x_res[:, tile, :], acc, ALU.add))
                        lane.settle()
                    dve.wait_ge(s_g2, N_KEYS + 2)
                    for t in range(DENSE):
                        lane.do(dve.tensor_tensor(acc, pair(t), gate_b[:, 0, :], ALU.mult))
                        lane.settle()
                        lane.do(dve.tensor_tensor(x_res[:, t, :], x_res[:, t, :], acc, ALU.add))
                        lane.settle()

                @block.gpsimd
                def _(pool):
                    def u_row(i, h, k):
                        u = i * PH + h
                        if u >= 1:
                            pool.wait_ge(s_dot, (u - 1) * TOPK + k + 1)
                        pool.indirect_dma_start(
                            out=u_ring[:, k, :], out_offset=None, in_=io["peer_u"][:, :],
                            in_offset=bass.IndirectOffsetOnAxis(ap=exp_idx[:, GATHERED[i], h * TOPK + k:h * TOPK + k + 1], axis=0),
                        ).then_inc(s_gu[k], 16)

                    def v_row(i, h, k):
                        n = (i * PH + h) * TOPK + k
                        if n >= VSLOTS:
                            before = n - VSLOTS
                            pool.wait_ge(s_ax, before // (PH * TOPK) + 1 + before + 1)
                        pool.indirect_dma_start(
                            out=v_ring[:, k % VSLOTS, :], out_offset=None, in_=io["peer_v"][:, :],
                            in_offset=bass.IndirectOffsetOnAxis(ap=exp_idx[:, GATHERED[i], h * TOPK + k:h * TOPK + k + 1], axis=0),
                        ).then_inc(s_gv[k % VSLOTS], 16)

                    heads = [(i, h) for i in range(len(GATHERED)) for h in range(PH)]
                    for k in range(TOPK):
                        u_row(0, 0, k)
                    for n, (i, h) in enumerate(heads):
                        for k in range(VSLOTS):
                            v_row(i, h, k)
                        for k in range(TOPK if n + 1 < len(heads) else 0):
                            u_row(*heads[n + 1], k)
                        for k in range(VSLOTS, TOPK):
                            v_row(i, h, k)

            with nc.Block() as block:
                @block.gpsimd
                def _(pool):
                    for s in cleared:
                        pool.sem_clear(s)

        own9 = sem("final_vector_steps")
        s_fw = sem("final_weight_loaded")
        s_m9 = sem("final_mean_squares")
        s_r9 = sem("final_roots")
        s_y9 = sem("final_rows")
        s_out = sem("outputs_stored")
        fw = gates_area[:, 0:D]
        with nc.Block() as block:
            @block.sync
            def _(sp):
                sp.dma_start(fw, io["final_norm_w"].broadcast_to([P, D])).then_inc(s_fw, 16)
                for t in range(TILES):
                    sp.wait_ge(s_y9, t + 1)
                    dst = io["y_prompt"][0] if t == CTX else io["y_sample"][0, t * P:(t + 1) * P, :]
                    sp.dma_start(dst, y_nat[:, t, :]).then_inc(s_out, 16)
                sp.wait_ge(s_out, 16 * TILES)

            @block.scalar
            def _(act):
                act.wait_ge(s_m9, 1)
                act.activation(stat[:, 0, 0:TILES], stat[:, 0, 0:TILES], ACT.Sqrt).then_inc(s_r9, 1)

            @block.vector
            def _(dve):
                lane = Lane(dve, own9)
                ss = stat[:, 0, 0:TILES]
                for t in range(TILES):
                    lane.do(dve.tensor_tensor_reduce(out=y_nat[:, t, :], in0=x_res[:, t, :], in1=x_res[:, t, :],
                                                     scale=1.0, scalar=0.0, op0=ALU.mult, op1=ALU.add,
                                                     accum_out=stat[:, 0, t:t + 1]))
                lane.settle()
                lane.do(dve.tensor_scalar(ss, ss, 1.0 / D, EPS, ALU.mult, ALU.add), s_m9)
                dve.wait_ge(s_r9, 1)
                dve.wait_ge(s_fw, 16)
                lane.do(dve.reciprocal(stat[:, 1, 0:TILES], ss))
                lane.settle()
                for t in range(TILES):
                    lane.do(dve.scalar_tensor_tensor(out=y_nat[:, t, :], in0=x_res[:, t, :], scalar=stat[:, 1, t:t + 1],
                                                     in1=fw, op0=ALU.mult, op1=ALU.mult), s_y9)


def kernel(**inputs):
    import numpy as np
    import concourse.bacc as bacc
    from concourse.bass_utils import run_bass_kernel_spmd

    a = {k: np.ascontiguousarray(v) for k, v in inputs.items()}
    w_g = a["w_in"][:, :, D_IN - 4 * HEADS:].reshape(DEPTH, KD, P, 2, 2, HEADS)
    w_gate = np.zeros((DEPTH, P, KD, 2, ROWS), np.float32)
    b_gate = np.zeros((DEPTH, ROWS, 2), np.float32)
    state_m = np.zeros((DEPTH, ROWS, 1), np.float32)
    for d in range(2):
        rows = slice(32 * d, 32 * d + HEADS)
        w_gate[..., rows] = w_g[:, :, :, d].transpose(0, 2, 1, 3, 4)
        b_gate[:, rows, :] = a["b_gate"].reshape(DEPTH, 2, 2, HEADS)[:, d].transpose(0, 2, 1)
        state_m[:, rows, 0] = a["state_m"][0, :, d]
    cols = lambda v: v.reshape(KD, P).T
    arrays = {
        "x_sample": a["x_sample"], "x_prompt": a["x_prompt"],
        "cond_t": np.stack([cols(a["c"][0]), cols(a["c_ctx"])], axis=2),
        "w_mod": a["w_mod"], "bmod_t": a["b_mod"].reshape(DEPTH, 48, P).transpose(2, 0, 1),
        "w_in": a["w_in"], "w_gate": w_gate, "b_gate": b_gate, "state_m": state_m,
        "conv_w": a["conv_w"].reshape(DEPTH, 9, KD, P).transpose(0, 3, 2, 1),
        "w_st": a["w_s"].transpose(0, 3, 1, 2), "b_st": a["b_s"].transpose(0, 2, 1),
        "mlstm_norm_w": a["mlstm_norm_w"],
        "state_C": a["state_C"].reshape(DEPTH, R, DH, DH),
        "state_n": a["state_n"].reshape(DEPTH, R, DH).transpose(0, 2, 1),
        "w_out": a["w_out"], "peer_wq": a["peer_wq"],
        "keys_t": a["peer_keys"].reshape(DEPTH, 2 * PH, N_KEYS, DH).transpose(0, 3, 1, 2),
        "peer_u": a["peer_u"].reshape(DEPTH * N_EXPERTS, D), "peer_v": a["peer_v"].reshape(DEPTH * N_EXPERTS, D),
        "peer_ut": a["peer_u"].reshape(DEPTH * N_KEYS, N_KEYS, KD, P).transpose(0, 3, 2, 1).reshape(DEPTH * N_KEYS, P, D),
        "final_norm_w": a["final_norm_w"].reshape(1, D),
    }
    arrays = {k: np.ascontiguousarray(v) for k, v in arrays.items()}
    outs = {
        "y_prompt": (1, P, D), "y_sample": (1, NS, D), "new_C": (DEPTH, R, DH, DH),
        "new_n": (DEPTH, DH, R), "new_m": (DEPTH, ROWS, 1),
    }
    nc = bacc.Bacc("TRN2", target_bir_lowering=False, num_devices=1)
    io = {k: nc.dram_tensor(f"in_{k}", v.shape, mybir.dt.from_np(v.dtype), kind="ExternalInput").ap() for k, v in arrays.items()}
    io.update({k: nc.dram_tensor(f"out_{k}", s, F32, kind="ExternalOutput").ap() for k, s in outs.items()})
    build(nc, io)
    r = run_bass_kernel_spmd(nc, [{f"in_{k}": v for k, v in arrays.items()}], core_ids=[0]).results[0]
    return (r["out_y_prompt"], r["out_y_sample"], r["out_new_C"].reshape(1, DEPTH, 2, HEADS, DH, DH),
            r["out_new_n"].transpose(0, 2, 1).reshape(1, DEPTH, 2, HEADS, DH),
            r["out_new_m"].reshape(1, DEPTH, 2, ROWS // 2)[..., 0:HEADS])
```

```python
from contextlib import ExitStack

import concourse.bass as bass
from concourse import mybir

F32 = mybir.dt.float32
U32 = mybir.dt.uint32
ALU = mybir.AluOpType
ACT = mybir.ActivationFunctionType
AX = mybir.AxisListType

P = 128
D = 1024
KD = D // P
SAMPLE_TILES = 4
TILES = SAMPLE_TILES + 1
CTX = TILES - 1
T = TILES * P
NS = SAMPLE_TILES * P
DEPTH = 2
GRID_W = 64
HEADS = 4
DH = 128
R = 2 * HEADS
ROWS = 64
D_G = 512
D_IN = 2 * D_G + 4 * D_G + 4 * HEADS
N_KEYS = 128
N_EXPERTS = N_KEYS * N_KEYS
PH = 8
TOPK = 16
EPS = 1e-6
LOWEST = -3.0e38
DENSE = 3
ND = DENSE * P
GATHERED = (3, 4)
USLOTS, VSLOTS = TOPK, 8
OCT = 8
FIRST_KEYS = 16
POOL_HOT = 3
STEPS = N_KEYS // (len(GATHERED) * PH)
VA = DH + 1


class Lane:

    def __init__(self, eng, own):
        self.eng, self.own, self.sent, self.settled = eng, own, {}, {}

    def do(self, ins, sem=None):
        sem = self.own if sem is None else sem
        ins.then_inc(sem, 1)
        self.sent[sem.name] = (sem, self.sent.get(sem.name, (sem, 0))[1] + 1)
        return ins

    def settle(self):
        for name, (sem, n) in self.sent.items():
            if self.settled.get(name) != n:
                self.eng.wait_ge(sem, n)
                self.settled[name] = n


def build(nc, io):
    ctx = ExitStack()
    cleared = []

    def sb(name, shape, dt=F32):
        return ctx.enter_context(nc.sbuf_tensor(name, shape, dt))

    def sem(name):
        s = ctx.enter_context(nc.semaphore(name))
        cleared.append(s)
        return s

    with ctx:
        x_res = sb("x_res", [P, TILES, D])
        y_nat = sb("y_nat", [P, TILES, D])
        big = sb("big", [P, 32000])
        gates_area = sb("gates_area", [P, 4480])
        kn_area = sb("kn_area", [P, 2560])
        ident = sb("ident", [P, P])
        ones_row = sb("ones_row", [ROWS, P])
        cap = sb("cap", [P, 2, P])
        iota16 = sb("iota16", [P, TOPK])
        cond_t = sb("cond_t", [P, KD, 2])
        mod_t = sb("mod_t", [P, DEPTH, 48, 2])
        bmod_t = sb("bmod_t", [P, DEPTH, 48])
        mod_l = sb("mod_l", [P, 48, 2])
        wgate = sb("wgate", [P, KD, 2, ROWS])
        bgate = sb("bgate", [ROWS, 2])
        convw = sb("convw", [P, KD, 9])
        wst = sb("wst", [P, HEADS, P])
        bst = sb("bst", [P, HEADS])
        normw = sb("normw", [P, D_G])
        m0 = sb("m0", [ROWS, 1])
        stat = sb("stat", [P, 4, 24])
        cols = sb("cols", [P, 4, TILES, R])
        decb = sb("decb", [P, R, TILES])
        small = sb("small", [ROWS, 4, TILES])
        m_out = sb("m_out", [ROWS, 1])
        n_io = sb("n_io", [P, R])
        exp_base = sb("exp_base", [P, 1])
        spare = sb("spare", [P, 2])
        gate_dram = nc.dram_tensor("expert_gates", (N_KEYS, P, ND), F32, kind="Internal").ap()
        den = sb("den", [P, 2, HEADS])
        ps = ctx.enter_context(nc.psum_tensor("ps", [P, 8, 512], F32))

        def carve(area, at, *shape, dt=None):
            n = 1
            for s in shape:
                n *= s
            v = area[:, at:at + n]
            if dt is not None:
                v = v.bitcast(dt)
            if len(shape) == 2:
                return v.rearrange("p (a b) -> p a b", a=shape[0])
            if len(shape) == 3:
                return v.rearrange("p (a b c) -> p a b c", a=shape[0], b=shape[1])
            return v

        mrow = big[0:2, 21504:21504 + 2 * D].rearrange("p (a n) -> p a n", a=2)
        h_t = carve(big, 0, KD, T)
        w0 = carve(big, 5120, KD, D)
        w1 = carve(big, 5120 + 8192, KD, D)
        wq = [w0, w1]
        w_v, w_o = carve(big, 5120, KD, D_G), carve(big, 5120 + KD * D_G, KD, D_G)
        qk_t = carve(big, 21504, KD, T)
        v_a = carve(big, 26624, TILES, HEADS, VA)
        vs = carve(big, 29204, TILES, D_G)
        hm = vs
        p_w = carve(big, 5120 + 8192, R, T)
        kw = carve(big, 5120 + 8192 + R * T, 2, D_G)
        cn = carve(big, 5120, R, VA)
        hn = carve(big, 5120 + R * VA, HEADS, VA)
        k_n = carve(kn_area, 0, TILES, D_G)
        gate_b = carve(kn_area, 0, 2, D)
        keys_t = carve(kn_area, 0, 2 * PH, N_KEYS)

        def rows(i):
            return gates_area[0:ROWS, i * T:(i + 1) * T]

        g_a, g_lf, g_b, g_m, g_wp, g_em, g_nm = [rows(i) for i in range(7)]
        g_we = g_lf
        exp_idx = carve(gates_area, 0, TILES, P, dt=U32)
        exp_gate = carve(gates_area, T, TILES, P)
        exp_i1 = carve(gates_area, 2 * T, TILES, P)
        exp_i2 = carve(gates_area, 3 * T, TILES, P)
        q_ts = carve(big, 21504, 2, T)
        sc2 = carve(big, 21504 + 1280, 2, T)
        top_v = carve(big, 21504 + 2560, TILES, 2 * PH, TOPK)
        top_i = carve(big, 21504 + 3840, TILES, 2 * PH, TOPK, dt=U32)
        cand, cand2, eq1, eq2 = [carve(big, 26624 + n * TILES * 256, TILES, 256) for n in range(4)]
        top_if = carve(gates_area, 4 * T, TILES, 2 * PH, TOPK)
        gate_x = carve(gates_area, 6 * T, TILES, P)
        expf = carve(big, 26624, TILES, P)
        pos, pa, pb = [carve(kn_area, 2048 + 80 * n, TILES, TOPK, dt=U32) for n in range(3)]
        paf, pbf = [carve(kn_area, 2288 + 80 * n, TILES, TOPK) for n in range(2)]
        gate_s = carve(big, 5120, N_KEYS, P)
        hot1 = carve(big, 21504, 2, OCT, P)
        hot2 = carve(big, 21504 + 2 * OCT * P, 2, OCT, P)
        choice_t = carve(big, 25600, 3, P)
        choice_c = carve(big, 25984, 2, 3, OCT)
        iota_k = big[:, 26048:26048 + N_KEYS]
        u_ring = carve(big, 5120, USLOTS, D)
        v_ring = carve(big, 21504, VSLOTS, D)
        acc = big[:, 29696:30720]
        v_s = [big[:, 30720:31744], y_nat[:, 2, :]]
        u_s = [y_nat[:, n, :].rearrange("p (k e) -> p k e", e=P) for n in range(2)]
        g_s = [gates_area[:, 4096:4096 + ND], kn_area[:, 2048:2048 + ND]]
        gelu_s = [gates_area[:, 2560:2560 + ND], gates_area[:, 2944:2944 + ND]]
        h_s = [gates_area[:, 3328:3328 + ND], gates_area[:, 3712:3712 + ND]]
        act_c = kn_area[:, 2432:2432 + TOPK]
        wact = kn_area[:, 2448:2448 + TOPK]

        def pair(q):
            return ps[:, 2 * q:2 * q + 2, :].rearrange("p a b -> p (a b)")

        s_in = sem("inputs_loaded")
        s_const = sem("constants_made")
        s_load = sem("layer_loaded")
        s_cond = sem("condition_activated")
        s_ml = sem("layer_modulation_copied")
        with nc.Block() as block:
            @block.sync
            def _(sp):
                sp.dma_start(x_res[:, 0:SAMPLE_TILES, :], io["x_sample"].rearrange("a (t p) d -> p (a t) d", p=P)).then_inc(s_in, 16)
                sp.dma_start(x_res[:, CTX, :], io["x_prompt"].rearrange("a p d -> (a p) d")).then_inc(s_in, 16)
                sp.dma_start(cond_t[:, :, :], io["cond_t"]).then_inc(s_in, 16)
                sp.dma_start(bmod_t[:, :, :], io["bmod_t"]).then_inc(s_in, 16)
                sp.wait_ge(s_in, 64)

            @block.gpsimd
            def _(pool):
                lane = Lane(pool, s_const)
                lane.do(pool.memset(ident[:, :], 0.0))
                lane.do(pool.memset(cap[:, :, :], 0.0))
                lane.do(pool.memset(ones_row[:, :], 1.0))
                lane.do(pool.memset(exp_base[:, :], 0.0))
                lane.do(pool.memset(m_out[:, :], 0.0))
                lane.do(pool.iota(iota16[:, :], pattern=[[1, TOPK]], base=0, channel_multiplier=0,
                                  allow_small_or_imprecise_dtypes=True))
                lane.settle()
                lane.do(pool.affine_select(out=ident[:, :], in_=ident[:, :], compare_op=ALU.not_equal, fill=1.0,
                                           base=0, pattern=[[-1, P]], channel_multiplier=1))
                lane.do(pool.affine_select(out=cap[:, 0, :], in_=cap[:, 0, :], compare_op=ALU.is_ge, fill=LOWEST,
                                           base=0, pattern=[[1, P]], channel_multiplier=-1))
                lane.do(pool.affine_select(out=cap[:, 1, :], in_=cap[:, 1, :], compare_op=ALU.is_ge, fill=LOWEST,
                                           base=0, pattern=[[-1, P]], channel_multiplier=1))
                lane.settle()

            @block.scalar
            def _(act):
                act.wait_ge(s_in, 64)
                nc.scalar.activation(cond_t[:, :, :], cond_t[:, :, :], ACT.Silu).then_inc(s_cond, 1)

        s_wm = [sem("mod_weights_0"), sem("mod_weights_1")]
        s_wm_used = sem("mod_weights_used")
        s_mod = sem("mod_ready")
        s_mrow = sem("mod_rows")
        s_mcol = sem("mod_columns")
        NB = DEPTH * 6
        wmod = io["w_mod"].rearrange("l (k p) (j n) -> l j p k n", p=P, n=D)
        with nc.Block() as block:
            @block.sync
            def _(sp):
                for j in range(NB):
                    if j >= 2:
                        sp.wait_ge(s_wm_used, j - 1)
                    sp.dma_start(wq[j % 2], wmod[j // 6, j % 6]).then_inc(s_wm[j % 2], 16)

            @block.tensor
            def _(pe):
                for j in range(NB + 1):
                    if j < NB:
                        pe.wait_ge(s_wm[j % 2], 16 * (j // 2 + 1))
                        if j >= 2:
                            pe.wait_ge(s_mrow, j - 1)
                        for half in range(2):
                            for k in range(KD):
                                last = pe.matmul(ps[0:2, 2 * (j % 2) + half, :], cond_t[:, k, :],
                                                 wq[j % 2][:, k, half * 512:(half + 1) * 512], start=(k == 0), stop=(k == KD - 1))
                        last.then_inc(s_wm_used, 1)
                    if j >= 1:
                        i = j - 1
                        pe.wait_ge(s_mrow, i + 1)
                        if i >= 2:
                            pe.wait_ge(s_mod, i - 1)
                        for n in range(8):
                            last = pe.transpose(ps[:, 4 + i % 2, 2 * n:2 * n + 2], mrow[:, i % 2, n * P:(n + 1) * P], ident[0:2, 0:2])
                        last.then_inc(s_mcol, 1)

            @block.scalar
            def _(act):
                for j in range(NB):
                    act.wait_ge(s_wm_used, j + 1)
                    if j >= 2:
                        act.wait_ge(s_mcol, j - 1)
                    act.activation(mrow[:, j % 2, :], ps[0:2, 2 * (j % 2):2 * (j % 2) + 2, :].rearrange("p a b -> p (a b)"),
                                   ACT.Copy).then_inc(s_mrow, 1)

            @block.vector
            def _(dve):
                for j in range(NB):
                    l, m = j // 6, j % 6
                    dve.wait_ge(s_mcol, j + 1)
                    dve.scalar_tensor_tensor(
                        out=mod_t[:, l, 8 * m:8 * m + 8, :],
                        in0=ps[:, 4 + j % 2, 0:16].rearrange("p (a b) -> p a b", b=2),
                        scalar=1.0 if m in (1, 4) else 0.0,
                        in1=bmod_t[:, l, 8 * m:8 * m + 8].unsqueeze(2).broadcast_to([P, 8, 2]),
                        op0=ALU.add, op1=ALU.add).then_inc(s_mod, 1)

        s_gu = [ctx.enter_context(nc.semaphore(f"u_row_{k}")) for k in range(USLOTS)]
        s_gv = [ctx.enter_context(nc.semaphore(f"v_row_{k}")) for k in range(VSLOTS)]

        with nc.Fori(0, DEPTH) as l:
            L = bass.ds(l, 1)

            def of(name, pattern):
                return io[name][L].rearrange(pattern)

            win = io["w_in"][L].rearrange("a (k p) n -> p (a k) n", p=P)
            s_w = [sem(f"w_{n}") for n in ("uv", "qk", "vo", "out", "q0", "q1")]
            with nc.Block() as block:
                @block.sync
                def _(sp):
                    sp.dma_start(wgate[:, :, :, :], of("w_gate", "a p k g r -> p (a k) g r")).then_inc(s_load, 16)
                    sp.dma_start(bgate[:, :], of("b_gate", "a p g -> p (a g)")).then_inc(s_load, 16)
                    sp.dma_start(convw[:, :, :], of("conv_w", "a p k n -> p (a k) n")).then_inc(s_load, 16)
                    sp.dma_start(wst[:, :, :], of("w_st", "a p h t -> p (a h) t")).then_inc(s_load, 16)
                    sp.dma_start(bst[:, :], of("b_st", "a p h -> p (a h)")).then_inc(s_load, 16)
                    sp.dma_start(normw[:, :], of("mlstm_norm_w", "a n -> a n").broadcast_to([P, D_G])).then_inc(s_load, 16)
                    sp.dma_start(m0[:, :], of("state_m", "a p o -> (a p) o")).then_inc(s_load, 16)
                    sp.dma_start(w1, win[:, :, 2 * D_G:4 * D_G]).then_inc(s_w[1], 16)
                    sp.dma_start(w0, win[:, :, 0:2 * D_G]).then_inc(s_w[0], 16)
                    sp.wait_ge(s_load, 7 * 16)

                @block.vector
                def _(dve):
                    dve.tensor_copy(mod_l[:, :, :], mod_t[:, L, :, :].rearrange("p a b c -> p (a b) c")).then_inc(s_ml, 1)

            def norm_block(tag, sh, sc, natural):
                own = sem(f"{tag}_vector_steps")
                s_ms = sem(f"{tag}_mean_squares")
                s_sq = sem(f"{tag}_roots")
                s_xn = sem(f"{tag}_normalised")
                s_tr = sem(f"{tag}_transposed")
                s_ht = sem(f"{tag}_ht_latent")
                s_hc = sem(f"{tag}_ht_context")
                s_back = sem(f"{tag}_back")
                s_nat = sem(f"{tag}_natural")
                ss, rs = stat[:, 0, 0:TILES], stat[:, 1, 0:TILES]
                with nc.Block() as block:
                    @block.vector
                    def _(dve):
                        lane = Lane(dve, own)
                        for t in range(TILES):
                            lane.do(dve.tensor_tensor_reduce(out=y_nat[:, t, :], in0=x_res[:, t, :], in1=x_res[:, t, :],
                                                             scale=1.0, scalar=0.0, op0=ALU.mult, op1=ALU.add,
                                                             accum_out=stat[:, 0, t:t + 1]))
                        lane.settle()
                        lane.do(dve.tensor_scalar(ss, ss, 1.0 / D, EPS, ALU.mult, ALU.add), s_ms)
                        dve.wait_ge(s_sq, 1)
                        lane.do(dve.reciprocal(rs, ss))
                        lane.settle()
                        for t in range(TILES):
                            lane.do(dve.tensor_scalar(y_nat[:, t, :], x_res[:, t, :], stat[:, 1, t:t + 1], None, ALU.mult), s_xn)
                        for k in range(KD):
                            dve.wait_ge(s_tr, k + 1)
                            lane.do(dve.tensor_scalar(h_t[:, k, NS:T], pair(k % 4)[:, NS:T], mod_l[:, 8 * sc + k, 1:2],
                                                      mod_l[:, 8 * sh + k, 1:2], ALU.mult, ALU.add), s_hc)

                    @block.scalar
                    def _(act):
                        act.wait_ge(s_ms, 1)
                        act.activation(ss, ss, ACT.Sqrt).then_inc(s_sq, 1)
                        for k in range(KD):
                            act.wait_ge(s_tr, k + 1)
                            act.activation(h_t[:, k, 0:NS], pair(k % 4)[:, 0:NS], ACT.Identity,
                                           bias=mod_l[:, 8 * sh + k, 0:1], scale=mod_l[:, 8 * sc + k, 0:1]).then_inc(s_ht, 1)
                        for n, t in enumerate(natural):
                            act.wait_ge(s_back, n + 1)
                            act.activation(y_nat[:, t, :], pair(n), ACT.Copy).then_inc(s_nat, 1)

                    @block.tensor
                    def _(pe):
                        for k in range(KD):
                            if k == 0:
                                pe.wait_ge(s_xn, TILES)
                            if k >= 4:
                                pe.wait_ge(s_ht, k - 3)
                                pe.wait_ge(s_hc, k - 3)
                            for t in range(TILES):
                                last = pe.transpose(pair(k % 4)[:, t * P:(t + 1) * P], y_nat[:, t, k * P:(k + 1) * P], ident[:, :])
                            last.then_inc(s_tr, 1)
                        for n, t in enumerate(natural):
                            if n == 0:
                                pe.wait_ge(s_ht, KD)
                                pe.wait_ge(s_hc, KD)
                            for k in range(KD):
                                last = pe.transpose(pair(n)[:, k * P:(k + 1) * P], h_t[:, k, t * P:(t + 1) * P], ident[:, :])
                            last.then_inc(s_back, 1)

            norm_block("norm1", 0, 1, ())

            own = sem("proj_vector_steps")
            s_gmm = sem("gate_products")
            s_ones = sem("v_ones_made")
            s_qk = sem("qk_products")
            s_conv = sem("qk_convolved")
            s_silu = sem("qk_silu")
            s_kn = sem("k_scaled")
            s_uv = sem("uv_products")
            s_uve = sem("uv_evacuated")
            s_neg = sem("gate_minus_abs")
            s_sp = sem("gate_softplus")
            s_aown = sem("proj_scalar_steps")
            s_rowx = sem("gate_rows_ready")
            s_rowe = sem("gate_rows_exponentials")
            s_w0free = sem("uv_weights_used")
            s_wo = sem("w_o")
            ig_ps, fg_ps = pair(2)[0:ROWS, 0:T], pair(3)[0:ROWS, 0:T]
            with nc.Block() as block:
                @block.sync
                def _(sp):
                    sp.wait_ge(s_w0free, 1)
                    sp.dma_start(w_v, win[:, :, 4 * D_G:5 * D_G]).then_inc(s_w[2], 16)
                    sp.dma_start(w_o, win[:, :, 5 * D_G:6 * D_G]).then_inc(s_wo, 16)

                @block.tensor
                def _(pe):
                    for g in range(2):
                        for a, b in ((0, NS), (NS, T)):
                            for k in range(KD):
                                last = pe.matmul(pair(2 + g)[0:ROWS, a:b], wgate[:, k, g, :], h_t[:, k, a:b],
                                                 start=(k == 0), stop=(k == KD - 1))
                        last.then_inc(s_gmm, 1)
                    pe.wait_ge(s_w[1], 16)
                    for j in range(KD):
                        if j >= 2:
                            pe.wait_ge(s_conv, j - 1)
                        for a, b in ((0, NS), (NS, T)):
                            for k in range(KD):
                                last = pe.matmul(pair(j % 2)[:, a:b], w1[:, k, j * P:(j + 1) * P], h_t[:, k, a:b],
                                                 start=(k == 0), stop=(k == KD - 1))
                        last.then_inc(s_qk, 1)
                    n = 0
                    for phase in range(2):
                        pe.wait_ge(s_w[0] if phase == 0 else s_w[2], 16)
                        for half in range(2 - phase):
                            for t in range(TILES):
                                if n < 4:
                                    pe.wait_ge(s_neg, 1)
                                else:
                                    pe.wait_ge(s_uve, n - 3)
                                for k in range(KD):
                                    last = pe.matmul(ps[:, 4 + n % 4, :], h_t[:, k, t * P:(t + 1) * P],
                                                     w_v[:, k, :] if phase else w0[:, k, half * D_G:(half + 1) * D_G],
                                                     start=(k == 0), stop=(k == KD - 1))
                                last.then_inc(s_uv, 1)
                                n += 1
                        if phase == 0:
                            pe.wait_ge(s_uv, n)
                            pe.sem_inc(s_w0free, 1)

                @block.scalar
                def _(act):
                    act.wait_ge(s_neg, 1)
                    act.activation(g_wp, g_wp, ACT.Exp).then_inc(s_aown, 1)
                    act.wait_ge(s_aown, 1)
                    act.activation(g_wp, g_wp, ACT.Ln, bias=1.0).then_inc(s_sp, 1)
                    for j in range(KD):
                        act.wait_ge(s_conv, j + 1)
                        act.activation(qk_t[:, j, :], qk_t[:, j, :], ACT.Silu).then_inc(s_silu, 1)
                    n = 0
                    for phase in range(2):
                        for half in range(2 - phase):
                            for t in range(TILES):
                                act.wait_ge(s_uv, n + 1)
                                src = ps[:, 4 + n % 4, :]
                                if phase == 0 and half == 0:
                                    act.activation(y_nat[:, t, 0:D_G], src, ACT.Copy).then_inc(s_uve, 1)
                                elif phase == 0:
                                    act.activation(vs[:, t, :], src, ACT.Copy).then_inc(s_uve, 1)
                                else:
                                    act.activation(v_a[:, t, :, 0:DH], src.rearrange("p (h d) -> p h d", d=DH),
                                                   ACT.Copy).then_inc(s_uve, 1)
                                n += 1
                    act.wait_ge(s_rowx, 1)
                    act.activation(g_wp, g_wp, ACT.Exp, scale=-1.0).then_inc(s_rowe, 1)
                    act.activation(g_em, g_em, ACT.Exp, scale=-1.0).then_inc(s_rowe, 1)
                    act.activation(g_we, g_we, ACT.Exp).then_inc(s_rowe, 1)
                    act.activation(small[:, 2, :], small[:, 2, :], ACT.Exp).then_inc(s_rowe, 1)

                @block.gpsimd
                def _(pool):
                    pool.memset(v_a[:, :, :, DH:VA], 1.0).then_inc(s_ones, 1)
                    for j in range(HEADS, KD):
                        pool.wait_ge(s_silu, j + 1)
                        pool.tensor_scalar(qk_t[:, j, :], qk_t[:, j, :], float(DH) ** -0.5, None, ALU.mult).then_inc(s_kn, 1)

                @block.vector
                def _(dve):
                    lane = Lane(dve, own)
                    dve.wait_ge(s_gmm, 2)
                    lane.do(dve.tensor_scalar(g_a, ig_ps, bgate[:, 0:1], None, ALU.add))
                    lane.do(dve.tensor_scalar(g_lf, fg_ps, bgate[:, 1:2], None, ALU.add))
                    lane.settle()
                    lane.do(dve.tensor_scalar(g_nm, g_lf, -1.0, None, ALU.mult))
                    lane.settle()
                    lane.do(dve.tensor_tensor(g_wp, g_lf, g_nm, ALU.min), s_neg)
                    lane.settle()
                    for j in range(KD):
                        src, dst = pair(j % 2), qk_t[:, j, :]
                        dve.wait_ge(s_qk, j + 1)
                        lane.do(dve.tensor_scalar(dst, src[:, 0:T], convw[:, j, 4:5], None, ALU.mult))
                        g_src = src[:, 0:NS].rearrange("p (r c) -> p r c", c=GRID_W)
                        g_dst = dst[:, 0:NS].rearrange("p (r c) -> p r c", c=GRID_W)
                        rr = NS // GRID_W
                        for tap in range(9):
                            di, dj = tap // 3 - 1, tap % 3 - 1
                            if tap == 4:
                                continue
                            r0, r1 = max(0, -di), rr - max(0, di)
                            c0, c1 = max(0, -dj), GRID_W - max(0, dj)
                            lane.settle()
                            out = g_dst[:, r0:r1, c0:c1]
                            if di == 0:
                                o2 = dst[:, NS + c0:T - max(0, dj)]
                                lane.do(dve.scalar_tensor_tensor(out=o2, in0=src[:, NS + c0 + dj:T - max(0, dj) + dj],
                                                                 scalar=convw[:, j, tap:tap + 1], in1=o2,
                                                                 op0=ALU.mult, op1=ALU.add))
                            lane.do(dve.scalar_tensor_tensor(out=out, in0=g_src[:, r0 + di:r1 + di, c0 + dj:c1 + dj],
                                                             scalar=convw[:, j, tap:tap + 1], in1=out,
                                                             op0=ALU.mult, op1=ALU.add))
                        lane.settle()
                        dve.engine_nop().then_inc(s_conv, 1)
                    dve.wait_ge(s_sp, 1)
                    lane.do(dve.scalar_tensor_tensor(out=g_lf, in0=g_lf, scalar=0.0, in1=g_wp, op0=ALU.min, op1=ALU.subtract))
                    lane.settle()

                    def span(row, c, back, dir_):
                        lo, hi = 32 * dir_, 32 * dir_ + HEADS
                        if not back:
                            return row[lo:hi, c * P:(c + 1) * P]
                        first, last = (c + 1) * P - 1, c * P - 1
                        return row[lo:hi, first:(last if last >= 0 else None):-1]

                    lane.do(dve.memset(g_b, 0.0))
                    lane.do(dve.memset(g_m, 0.0))
                    lane.do(dve.memset(small[:, :, :], 0.0))
                    lane.settle()
                    for c in range(TILES):
                        for d in range(2):
                            lane.do(dve.tensor_tensor_scan(span(g_b, c, d == 1, d), ones_row[32 * d:32 * d + HEADS, :],
                                                           span(g_lf, c, d == 1, d), 0.0, ALU.mult, ALU.add))
                    lane.settle()
                    lane.do(dve.tensor_tensor(g_a, g_a, g_b, ALU.subtract))
                    lane.do(dve.tensor_copy(small[0:HEADS, 0, 0:1], m0[0:HEADS, :]))
                    lane.do(dve.tensor_copy(small[32:32 + HEADS, 0, SAMPLE_TILES - 1:SAMPLE_TILES], m0[32:32 + HEADS, :]))
                    lane.settle()
                    for i in range(TILES):
                        for d in range(2):
                            c = i if d == 0 or i == CTX else SAMPLE_TILES - 1 - i
                            lo, hi = 32 * d, 32 * d + HEADS
                            sa = span(g_a, c, d == 1, d)
                            lane.do(dve.tensor_tensor_scan(span(g_m, c, d == 1, d), sa, sa, small[lo:hi, 0, c:c + 1],
                                                           ALU.max, ALU.max))
                        lane.settle()
                        for d in range(2):
                            c = i if d == 0 or i == CTX else SAMPLE_TILES - 1 - i
                            lo, hi = 32 * d, 32 * d + HEADS
                            end = c * P + (P - 1 if d == 0 else 0)
                            lane.do(dve.tensor_copy(small[lo:hi, 1, c:c + 1], g_m[lo:hi, end:end + 1]))
                            nxt = m_out[lo:hi, :] if i == CTX else None
                            if i < SAMPLE_TILES - 1:
                                cc = i + 1 if d == 0 else SAMPLE_TILES - 2 - i
                                nxt = small[lo:hi, 0, cc:cc + 1]
                            if nxt is not None:
                                lane.do(dve.tensor_tensor(nxt, g_b[lo:hi, end:end + 1], g_m[lo:hi, end:end + 1], ALU.add))
                        lane.settle()
                    by_c = lambda row: row.rearrange("p (c t) -> p c t", t=P)
                    spread = lambda q: small[:, q, :].unsqueeze(2).broadcast_to([ROWS, TILES, P])
                    lane.do(dve.tensor_scalar(g_nm, g_m, -1.0, None, ALU.mult))
                    lane.do(dve.tensor_tensor(by_c(g_wp), by_c(g_m), spread(0), ALU.subtract))
                    lane.do(dve.tensor_tensor(g_em, g_b, g_m, ALU.add))
                    lane.do(dve.tensor_tensor(by_c(g_we), by_c(g_a), spread(1), ALU.subtract))
                    lane.do(dve.tensor_tensor(small[:, 2, :], small[:, 0, :], small[:, 1, :], ALU.subtract))
                    lane.settle()
                    dve.engine_nop().then_inc(s_rowx, 1)

            own2 = sem("gmlp_vector_steps")
            s_v2 = sem("gmlp_mean_squares")
            s_r2 = sem("gmlp_roots")
            s_vh = sem("gmlp_normalised")
            s_mix = sem("gmlp_products")
            s_ya = sem("gmlp_done")
            s_ct = sem("gate_columns_transposed")
            s_kt = sem("k_transposed")
            s_ke = sem("k_natural")
            ms2, rs2 = stat[:, 2, 0:20], stat[:, 3, 0:20]
            with nc.Block() as block:
                @block.vector
                def _(dve):
                    lane = Lane(dve, own2)
                    v20 = vs.rearrange("p t (h d) -> p (t h) d", d=DH)
                    k20 = k_n.rearrange("p t (h d) -> p (t h) d", d=DH)
                    lane.do(dve.tensor_tensor(k20, v20, v20, ALU.mult))
                    lane.settle()
                    lane.do(dve.tensor_reduce(ms2, k20, AX.X, ALU.add))
                    lane.settle()
                    lane.do(dve.tensor_scalar(ms2, ms2, 1.0 / DH, EPS, ALU.mult, ALU.add), s_v2)
                    dve.wait_ge(s_ct, 1)
                    c20 = cols.rearrange("p q c r -> p (q c) r")
                    t20 = ps[:, 4:7, :].rearrange("p a b -> p (a b)")[:, 0:20 * ROWS].rearrange("p (n r) -> p n r", r=ROWS)
                    lane.do(dve.tensor_copy(c20[:, :, 0:HEADS], t20[:, :, 0:HEADS]))
                    lane.do(dve.tensor_copy(c20[:, :, HEADS:R], t20[:, :, 32:32 + HEADS]))
                    lane.do(dve.tensor_copy(decb.rearrange("p r c -> p (r c)"), ps[:, 7, 0:R * TILES]))
                    dve.wait_ge(s_r2, 1)
                    lane.do(dve.reciprocal(rs2, ms2))
                    lane.settle()
                    lane.do(dve.tensor_tensor(v20, v20, rs2.unsqueeze(2).broadcast_to([P, 20, DH]), ALU.mult), s_vh)
                    for h in range(HEADS):
                        dve.wait_ge(s_mix, h + 1)
                        for a, b in ((0, SAMPLE_TILES), (SAMPLE_TILES, TILES)):
                            yv = y_nat[:, a:b, h * DH:(h + 1) * DH]
                            lane.do(dve.scalar_tensor_tensor(
                                out=yv, in0=pair(h % 2)[:, a * P:b * P].rearrange("p (t d) -> p t d", d=DH),
                                scalar=bst[:, h:h + 1], in1=yv, op0=ALU.add, op1=ALU.mult), s_ya)

                @block.scalar
                def _(act):
                    act.wait_ge(s_v2, 1)
                    act.activation(ms2, ms2, ACT.Sqrt).then_inc(s_r2, 1)
                    for c in range(TILES):
                        act.wait_ge(s_kt, c + 1)
                        act.activation(k_n[:, c, :], ps[:, c % 4 if c < 4 else 0, :], ACT.Copy).then_inc(s_ke, 1)

                @block.tensor
                def _(pe):
                    for q, row in enumerate((g_a, g_wp, g_em, g_we)):
                        for c in range(TILES):
                            n = (q * TILES + c) * ROWS
                            pe.transpose(ps[:, 4 + n // 512, n % 512:n % 512 + ROWS], row[:, c * P:(c + 1) * P],
                                         ident[0:ROWS, 0:ROWS])
                    for r in range(R):
                        row = 32 * (r // HEADS) + r % HEADS
                        last = pe.matmul(ps[:, 7, r * TILES:(r + 1) * TILES],
                                         ident[0:ROWS, row:row + 1].broadcast_to([ROWS, P]), small[:, 2, :],
                                         start=True, stop=True)
                    last.then_inc(s_ct, 1)
                    pe.wait_ge(s_v2, 1)
                    for c in range(TILES):
                        if c == 4:
                            pe.wait_ge(s_ke, 1)
                        for h in range(HEADS):
                            last = pe.transpose(ps[:, c % 4, h * DH:(h + 1) * DH], qk_t[:, HEADS + h, c * P:(c + 1) * P], ident[:, :])
                        last.then_inc(s_kt, 1)
                    pe.wait_ge(s_vh, 1)
                    pe.wait_ge(s_ke, TILES)
                    for h in range(HEADS):
                        if h >= 2:
                            pe.wait_ge(s_ya, 2 * (h - 1))
                        for a, b in ((0, SAMPLE_TILES), (SAMPLE_TILES, TILES)):
                            last = pe.matmul(pair(h % 2)[:, a * P:b * P], wst[:, h, :],
                                             vs[:, a:b, h * DH:(h + 1) * DH], start=True, stop=True)
                        last.then_inc(s_mix, 1)

            s_sc = sem("scores")
            s_nm = sem("minus_m_spread")
            s_e1 = sem("exponents")
            s_e2 = sem("exponents_capped")
            s_e3 = sem("exponentials")
            s_p = sem("intra_weights")
            s_cl = sem("states_loaded")
            with nc.Block() as block:
                @block.sync
                def _(sp):
                    sp.dma_start(cn[:, :, 0:DH], of("state_C", "a r d e -> d (a r) e")).then_inc(s_cl, 16)
                    sp.dma_start(n_io[:, :], of("state_n", "a d r -> d (a r)")).then_inc(s_cl, 16)
                    sp.wait_ge(s_cl, 32)

                @block.tensor
                def _(pe):
                    for h in range(HEADS):
                        if h:
                            pe.wait_ge(s_p, 2 * h)
                        for c in range(TILES):
                            last = pe.matmul(pair(0)[:, c * P:(c + 1) * P], qk_t[:, HEADS + h, c * P:(c + 1) * P],
                                             qk_t[:, h, c * P:(c + 1) * P], start=True, stop=True)
                        last.then_inc(s_sc, 1)
                        for d in range(2):
                            row = 32 * d + h
                            for a, b in ((0, NS), (NS, T)):
                                last = pe.matmul(pair(1 + d)[:, a:b], ident[0:ROWS, row:row + 1].broadcast_to([ROWS, P]),
                                                 g_nm[:, a:b], start=True, stop=True)
                            last.then_inc(s_nm, 1)

                @block.vector
                def _(dve):
                    n = 0
                    for h in range(HEADS):
                        for d in range(2):
                            r = d * HEADS + h
                            dve.wait_ge(s_nm, n + d + 1)
                            dve.tensor_tensor(p_w[:, r, :].rearrange("p (c t) -> p c t", t=P),
                                              pair(1 + d)[:, 0:T].rearrange("p (c t) -> p c t", t=P),
                                              cols[:, 0, :, r:r + 1].broadcast_to([P, TILES, P]), ALU.add).then_inc(s_e1, 1)
                        dve.wait_ge(s_sc, h + 1)
                        for d in range(2):
                            r = d * HEADS + h
                            dve.wait_ge(s_e3, n + d + 1)
                            dve.tensor_tensor(p_w[:, r, :], pair(0)[:, 0:T], p_w[:, r, :], ALU.mult).then_inc(s_p, 1)
                        n += 2

                @block.gpsimd
                def _(pool):
                    for n in range(R):
                        h, d = n // 2, n % 2
                        pool.wait_ge(s_e1, n + 1)
                        v = p_w[:, d * HEADS + h, :].rearrange("p (c t) -> p c t", t=P)
                        pool.tensor_tensor(v, v, cap[:, d:d + 1, :].broadcast_to([P, TILES, P]), ALU.add).then_inc(s_e2, 1)

                @block.scalar
                def _(act):
                    for n in range(R):
                        h, d = n // 2, n % 2
                        act.wait_ge(s_e2, n + 1)
                        v = p_w[:, d * HEADS + h, :]
                        act.activation(v, v, ACT.Exp).then_inc(s_e3, 1)

            own4 = sem("chain_vector_steps")
            s_kw = sem("k_weighted")
            s_mm = sem("chain_products")
            s_cn = sem("chain_state")
            s_n0 = sem("normaliser_placed")
            s_nf = sem("normaliser_taken")
            s_st = sem("states_stored")
            s_og = sem("o_products")
            s_oe = sem("o_gates_ready")
            steps = []
            for i in range(TILES):
                for d in range(2):
                    steps.append((d, i if d == 0 or i == CTX else SAMPLE_TILES - 1 - i))
            heads_of = lambda b: ps[:, b:b + 2, 0:2 * VA].rearrange("p a (h e) -> p a h e", e=VA)
            four = lambda ap: ap.rearrange("p (a h) e -> p a h e", a=2)
            with nc.Block() as block:
                @block.gpsimd
                def _(pool):
                    for n, (d, c) in enumerate(steps):
                        if n >= 2:
                            pool.wait_ge(s_mm, n - 1)
                        pool.tensor_tensor(kw[:, n % 2, :].rearrange("p (h e) -> p h e", e=DH),
                                           k_n[:, c, :].rearrange("p (h e) -> p h e", e=DH),
                                           cols[:, 3, c, d * HEADS:(d + 1) * HEADS].unsqueeze(2).broadcast_to([P, HEADS, DH]),
                                           ALU.mult).then_inc(s_kw, 1)

                @block.tensor
                def _(pe):
                    for n, (d, c) in enumerate(steps):
                        pe.wait_ge(s_kw, n + 1)
                        if n == 0:
                            pe.wait_ge(s_n0, 1)
                        if n >= 1:
                            pe.wait_ge(s_cn, n)
                        for h in range(HEADS):
                            r = d * HEADS + h
                            b, e = h // 2, (h % 2) * VA
                            if c != CTX:
                                pe.matmul(ps[:, b, e:e + VA], qk_t[:, h, c * P:(c + 1) * P], cn[:, r, :], start=True, stop=True)
                            pe.matmul(ps[:, 2 + b, e:e + VA], p_w[:, r, c * P:(c + 1) * P], v_a[:, c, h, :], start=True, stop=True)
                            last = pe.matmul(ps[:, 4 + b, e:e + VA], kw[:, n % 2, h * DH:(h + 1) * DH], v_a[:, c, h, :],
                                             start=True, stop=True)
                        last.then_inc(s_mm, 1)
                        t = n // 2
                        if n == 0:
                            pe.wait_ge(s_wo, 16)
                        if n % 2 == 0 and t >= 2:
                            pe.wait_ge(s_oe, t - 1)
                        for k in range(4 * (n % 2), 4 * (n % 2) + 4):
                            last = pe.matmul(ps[:, 6 + t % 2, :], h_t[:, k, t * P:(t + 1) * P], w_o[:, k, :],
                                             start=(k == 0), stop=(k == KD - 1))
                        if n % 2:
                            last.then_inc(s_og, 1)

                @block.scalar
                def _(act):
                    for t in range(TILES):
                        act.wait_ge(s_og, t + 1)
                        act.activation(y_nat[:, t, D_G:D], ps[:, 6 + t % 2, :], ACT.Sigmoid).then_inc(s_oe, 1)

                @block.vector
                def _(dve):
                    lane = Lane(dve, own4)
                    lane.do(dve.memset(hm[:, :, :], 0.0))
                    lane.do(dve.tensor_copy(cn[:, :, DH], n_io[:, :]), s_n0)
                    hn4 = four(hn)
                    for n, (d, c) in enumerate(steps):
                        rr = slice(d * HEADS, (d + 1) * HEADS)
                        dve.wait_ge(s_mm, n + 1)
                        lane.settle()
                        if c != CTX:
                            wp = cols[:, 1, c, rr].unsqueeze(2).broadcast_to([P, HEADS, VA])
                            lane.do(dve.tensor_tensor(hn4, heads_of(0), four(wp), ALU.mult))
                            dec = decb[:, rr, c:c + 1].broadcast_to([P, HEADS, VA])
                            lane.do(dve.tensor_tensor(cn[:, rr, :], cn[:, rr, :], dec, ALU.mult))
                            lane.settle()
                            lane.do(dve.tensor_tensor(hn4, hn4, heads_of(2), ALU.add))
                            lane.do(dve.tensor_tensor(four(cn[:, rr, :]), four(cn[:, rr, :]), heads_of(4), ALU.add), s_cn)
                        else:
                            lane.do(dve.tensor_copy(hn4, heads_of(2)))
                            lane.do(dve.tensor_copy(four(cn[:, rr, :]), heads_of(4)), s_cn)
                        lane.settle()
                        dd = hn[:, :, DH:VA].rearrange("p h o -> p (h o)")
                        lane.do(dve.tensor_scalar(den[:, 0, :], dd, -1.0, None, ALU.mult))
                        lane.settle()
                        lane.do(dve.tensor_tensor(den[:, 0, :], den[:, 0, :], dd, ALU.max))
                        lane.settle()
                        lane.do(dve.tensor_tensor(den[:, 0, :], den[:, 0, :], cols[:, 2, c, rr], ALU.max))
                        lane.settle()
                        lane.do(dve.reciprocal(den[:, 1, :], den[:, 0, :]))
                        lane.settle()
                        lane.do(dve.tensor_tensor(hn[:, :, 0:DH], hn[:, :, 0:DH],
                                                  den[:, 1, :].unsqueeze(2).broadcast_to([P, HEADS, DH]), ALU.mult))
                        lane.settle()
                        hmc = hm[:, c, :].rearrange("p (h e) -> p h e", e=DH)
                        lane.do(dve.tensor_tensor(hmc, hmc, hn[:, :, 0:DH], ALU.add))
                    lane.do(dve.tensor_copy(n_io[:, :], cn[:, :, DH]), s_nf)
                    lane.settle()

                @block.sync
                def _(sp):
                    sp.wait_ge(s_cn, len(steps))
                    for r in range(R):
                        sp.dma_start(io["new_C"][L].rearrange("a r d e -> (a r) d e")[r], cn[:, r, 0:DH]).then_inc(s_st, 16)
                    sp.dma_start(io["new_m"][L].rearrange("a r o -> (a r) o"), m_out[:, :]).then_inc(s_st, 16)
                    sp.wait_ge(s_nf, 1)
                    sp.dma_start(io["new_n"][L].rearrange("a d r -> (a d) r"), n_io[:, :]).then_inc(s_st, 16)
                    sp.wait_ge(s_st, 16 * (R + 2))

            own5 = sem("out_vector_steps")
            s_m5 = sem("head_mean_squares")
            s_r5 = sem("head_roots")
            s_yb = sem("mixed_ready")
            s_tr5 = sem("mixed_transposed")
            s_te5 = sem("mixed_t_ready")
            s_gb = sem("gate1_spread")
            s_gbe = sem("gate1_ready")
            s_o5 = sem("out_products")
            s_t5 = sem("out_banks_read")
            tmp5 = carve(big, 21504, 2, 512)

            def spread_gate(pe, m, done):
                for cnd in range(2):
                    for k in range(KD):
                        last = pe.matmul(ps[:, 4 + 2 * cnd + k // 4, (k % 4) * P:(k % 4 + 1) * P],
                                         mod_l[:, 8 * m + k, cnd:cnd + 1].broadcast_to([P, P]), ident[:, :], start=True, stop=True)
                last.then_inc(done, 1)

            with nc.Block() as block:
                @block.sync
                def _(sp):
                    sp.dma_start(w0, io["w_out"][L].rearrange("a (k p) n -> p (a k) n", p=P)).then_inc(s_w[3], 16)
                    sp.dma_start(w1, io["peer_wq"][L].rearrange("a (k p) n -> p (a k) n", p=P)[:, :, D:2 * D]).then_inc(s_w[5], 16)

                @block.vector
                def _(dve):
                    lane = Lane(dve, own5)
                    h20 = hm.rearrange("p t (h d) -> p (t h) d", d=DH)
                    j20 = k_n.rearrange("p t (h d) -> p (t h) d", d=DH)
                    lane.do(dve.tensor_tensor(j20, h20, h20, ALU.mult))
                    lane.settle()
                    lane.do(dve.tensor_reduce(ms2, j20, AX.X, ALU.add))
                    lane.settle()
                    lane.do(dve.tensor_scalar(ms2, ms2, 1.0 / DH, EPS, ALU.mult, ALU.add), s_m5)
                    for t in range(TILES):
                        lane.do(dve.tensor_tensor(y_nat[:, t, D_G:D], y_nat[:, t, D_G:D], normw[:, :], ALU.mult))
                    dve.wait_ge(s_r5, 1)
                    lane.do(dve.reciprocal(rs2, ms2))
                    lane.settle()
                    lane.do(dve.tensor_tensor(h20, h20, rs2.unsqueeze(2).broadcast_to([P, 20, DH]), ALU.mult))
                    lane.settle()
                    lane.do(dve.tensor_tensor(y_nat[:, :, D_G:D], y_nat[:, :, D_G:D], hm[:, :, :], ALU.mult), s_yb)
                    n = 0
                    dve.wait_ge(s_gbe, 1)
                    for t in range(TILES):
                        for half in range(2):
                            dve.wait_ge(s_o5, n + 1)
                            cnd = 1 if t == CTX else 0
                            sl = slice(half * 512, (half + 1) * 512)
                            if n >= 2:
                                lane.settle()
                            lane.do(dve.tensor_tensor(tmp5[:, n % 2, :], ps[:, n % 4, :], gate_b[:, cnd, sl], ALU.mult), s_t5)
                            lane.settle()
                            lane.do(dve.tensor_tensor(x_res[:, t, sl], x_res[:, t, sl], tmp5[:, n % 2, :], ALU.add))
                            n += 1

                @block.scalar
                def _(act):
                    act.wait_ge(s_m5, 1)
                    act.activation(ms2, ms2, ACT.Sqrt).then_inc(s_r5, 1)
                    act.wait_ge(s_gb, 1)
                    act.activation(gate_b.rearrange("p a b -> p (a b)"), ps[:, 4:8, :].rearrange("p a b -> p (a b)"), ACT.Copy).then_inc(s_gbe, 1)
                    for k in range(KD):
                        act.wait_ge(s_tr5, k + 1)
                        act.activation(h_t[:, k, :], pair(k % 4)[:, 0:T], ACT.Copy).then_inc(s_te5, 1)

                @block.tensor
                def _(pe):
                    pe.wait_ge(s_m5, 1)
                    spread_gate(pe, 2, s_gb)
                    for k in range(KD):
                        if k == 2:
                            pe.wait_ge(s_gbe, 1)
                        if k == D_G // P:
                            pe.wait_ge(s_yb, 1)
                        if k >= 4:
                            pe.wait_ge(s_te5, k - 3)
                        for t in range(TILES):
                            last = pe.transpose(pair(k % 4)[:, t * P:(t + 1) * P], y_nat[:, t, k * P:(k + 1) * P], ident[:, :])
                        last.then_inc(s_tr5, 1)
                    pe.wait_ge(s_te5, KD)
                    pe.wait_ge(s_w[3], 16)
                    n = 0
                    for t in range(TILES):
                        for half in range(2):
                            if n >= 4:
                                pe.wait_ge(s_t5, n - 3)
                            for k in range(KD):
                                last = pe.matmul(ps[:, n % 4, :], h_t[:, k, t * P:(t + 1) * P],
                                                 w0[:, k, half * 512:(half + 1) * 512], start=(k == 0), stop=(k == KD - 1))
                            last.then_inc(s_o5, 1)
                            n += 1

            s_key = sem("keys_loaded")
            with nc.Block() as block:
                @block.sync
                def _(sp):
                    sp.dma_start(w0, io["peer_wq"][L].rearrange("a (k p) n -> p (a k) n", p=P)[:, :, 0:D]).then_inc(s_w[4], 16)
                    sp.dma_start(keys_t, of("keys_t", "a p g k -> p (a g) k")).then_inc(s_key, 16)

            norm_block("norm2", 3, 4, GATHERED)

            own6 = sem("topk_vector_steps")
            s_q = sem("queries")
            s_qe = sem("queries_copied")
            s_s = sem("key_scores")
            s_top = sem("key_scores_read")
            s_eq = sem("ranks_compared")
            s_pm = sem("ranks_times_keys")
            s_tv = sem("best_scores_taken")
            s_cd = sem("pairs_added")
            s_ps = sem("pair_gpsimd_steps")
            s_b7 = sem("pair_scores_shifted")
            s_e7 = sem("pair_exponentials")
            with nc.Block() as block:
                @block.tensor
                def _(pe):
                    for g in range(2 * PH + 1):
                        if g < 2 * PH:
                            w = wq[g // PH]
                            if g % PH == 0:
                                pe.wait_ge(s_w[4 + g // PH], 16)
                            if g >= 2:
                                pe.wait_ge(s_qe, g - 1)
                            for a, b in ((0, NS), (NS, T)):
                                for k in range(KD):
                                    last = pe.matmul(pair(g % 2)[:, a:b], w[:, k, (g % PH) * P:(g % PH + 1) * P], h_t[:, k, a:b],
                                                     start=(k == 0), stop=(k == KD - 1))
                            last.then_inc(s_q, 1)
                        if g >= 1:
                            f = g - 1
                            if f == 0:
                                pe.wait_ge(s_key, 16)
                            pe.wait_ge(s_qe, f + 1)
                            if f >= 2:
                                pe.wait_ge(s_top, f - 1)
                            for t in range(TILES):
                                last = pe.matmul(pair(2 + f % 2)[:, t * P:(t + 1) * P], q_ts[:, f % 2, t * P:(t + 1) * P],
                                                 keys_t[:, f, :], start=True, stop=True)
                            last.then_inc(s_s, 1)

                @block.scalar
                def _(act):
                    for g in range(2 * PH):
                        act.wait_ge(s_q, g + 1)
                        if g >= 2:
                            act.wait_ge(s_s, g - 1)
                        act.activation(q_ts[:, g % 2, :], pair(g % 2)[:, 0:T], ACT.Copy).then_inc(s_qe, 1)
                    act.wait_ge(s_b7, 1)
                    act.activation(exp_gate, gate_x, ACT.Exp).then_inc(s_e7, 1)

                @block.gpsimd
                def _(pool):
                    lane = Lane(pool, s_ps)
                    by_rank = lambda buf: buf.rearrange("p t (a b) -> p t a b", b=TOPK)
                    for h in range(PH + 1):
                        if h < PH:
                            pool.wait_ge(s_tv, h + 1)
                            lane.do(pool.tensor_tensor(by_rank(cand), top_v[:, :, 2 * h, :].unsqueeze(3).broadcast_to([P, TILES, TOPK, TOPK]),
                                                       top_v[:, :, 2 * h + 1, :].unsqueeze(2).broadcast_to([P, TILES, TOPK, TOPK]),
                                                       ALU.add), s_cd)
                        if h:
                            for x, buf in enumerate((eq1, eq2)):
                                pool.wait_ge(s_eq, 2 * (h - 1) + x + 1)
                                v, key = by_rank(buf), top_if[:, :, 2 * (h - 1) + x, :]
                                lane.do(pool.tensor_tensor(v, v, key.unsqueeze(2).broadcast_to([P, TILES, TOPK, TOPK]), ALU.mult))
                                lane.settle()
                                half = TOPK // 2
                                lane.do(pool.tensor_tensor(v[:, :, :, 0:half], v[:, :, :, 0:half], v[:, :, :, half:TOPK], ALU.add), s_pm)

                @block.vector
                def _(dve):
                    lane = Lane(dve, own6)
                    every = range(TILES)

                    def keys(g):
                        dve.wait_ge(s_s, g + 1)
                        src = [pair(2 + g % 2)[:, t * P:(t + 1) * P] for t in every]
                        cut = [sc2[:, g % 2, t * P:(t + 1) * P] for t in every]
                        for t in every:
                            lane.do(dve.max(top_v[:, t, g, 0:8], src[t]))
                        lane.settle()
                        for t in every:
                            lane.do(dve.match_replace(cut[t], top_v[:, t, g, 0:8], src[t], LOWEST))
                        for t in every:
                            lane.do(dve.max_index(top_i[:, t, g, 0:8], top_v[:, t, g, 0:8], src[t]), s_top if t == CTX else None)
                        lane.settle()
                        for t in every:
                            lane.do(dve.max(top_v[:, t, g, 8:16], cut[t]))
                        lane.settle()
                        for t in every:
                            lane.do(dve.max_index(top_i[:, t, g, 8:16], top_v[:, t, g, 8:16], cut[t]),
                                    s_tv if g % 2 and t == CTX else None)

                    def resolve(h):
                        for x, (buf, dst) in enumerate(((eq1, exp_i1), (eq2, exp_i2))):
                            dve.wait_ge(s_pm, 2 * h + x + 1)
                            lane.do(dve.tensor_reduce(dst[:, :, h * TOPK:(h + 1) * TOPK],
                                                      buf.rearrange("p t (a b) -> p t a b", b=TOPK)[:, :, :, 0:TOPK // 2],
                                                      AX.X, ALU.add))

                    def best_pairs(h):
                        hk = h * TOPK
                        lane.settle()
                        lane.do(dve.tensor_copy(top_if[:, :, 2 * h:2 * h + 2, :], top_i[:, :, 2 * h:2 * h + 2, :]))
                        dve.wait_ge(s_cd, h + 1)
                        for t in every:
                            lane.do(dve.max(exp_gate[:, t, hk:hk + 8], cand[:, t, :]))
                        lane.settle()
                        for t in every:
                            lane.do(dve.match_replace(cand2[:, t, :], exp_gate[:, t, hk:hk + 8], cand[:, t, :], LOWEST))
                        for t in every:
                            lane.do(dve.max_index(pos[:, t, 0:8], exp_gate[:, t, hk:hk + 8], cand[:, t, :]))
                        lane.settle()
                        for t in every:
                            lane.do(dve.max(exp_gate[:, t, hk + 8:hk + 16], cand2[:, t, :]))

                    def ranks(h):
                        hk = h * TOPK
                        lane.settle()
                        for t in every:
                            lane.do(dve.max_index(pos[:, t, 8:16], exp_gate[:, t, hk + 8:hk + 16], cand2[:, t, :]))
                        lane.settle()
                        lane.do(dve.tensor_scalar(pa, pos, 4, None, ALU.logical_shift_right))
                        lane.do(dve.tensor_scalar(pb, pos, 15, None, ALU.bitwise_and))
                        lane.settle()
                        lane.do(dve.tensor_copy(paf, pa))
                        lane.do(dve.tensor_copy(pbf, pb))
                        lane.settle()
                        if h:
                            resolve(h - 1)
                            lane.settle()
                        it = iota16[:, :].unsqueeze(1).unsqueeze(1).broadcast_to([P, TILES, TOPK, TOPK])
                        for buf, q in ((eq1, paf), (eq2, pbf)):
                            lane.do(dve.tensor_tensor(buf.rearrange("p t (a b) -> p t a b", b=TOPK),
                                                      q.unsqueeze(3).broadcast_to([P, TILES, TOPK, TOPK]), it, ALU.is_equal), s_eq)

                    for g in range(2 * PH):
                        keys(g)
                        if g >= 2:
                            (ranks if g % 2 else best_pairs)(g // 2 - 1)
                    best_pairs(PH - 1)
                    ranks(PH - 1)
                    lane.settle()
                    by_head = lambda v: v.rearrange("p t (h k) -> p (t h) k", k=TOPK)
                    spread_k = lambda v: v.broadcast_to([P, TILES * PH, TOPK])
                    lane.do(dve.tensor_tensor(by_head(gate_x), by_head(exp_gate), spread_k(by_head(exp_gate)[:, :, 0:1]), ALU.subtract), s_b7)
                    resolve(PH - 1)
                    lane.settle()
                    lane.do(dve.scalar_tensor_tensor(out=expf, in0=exp_i1, scalar=float(N_KEYS), in1=exp_i2, op0=ALU.mult, op1=ALU.add))
                    dve.wait_ge(s_e7, 1)
                    sm = stat.rearrange("p a b -> p (a b)")[:, 0:TILES * PH]
                    lane.do(dve.tensor_reduce(sm, by_head(exp_gate), AX.X, ALU.add))
                    lane.settle()
                    lane.do(dve.tensor_scalar(exp_idx, expf, exp_base[:, 0:1], None, ALU.add))
                    lane.do(dve.reciprocal(sm, sm))
                    lane.settle()
                    lane.do(dve.tensor_tensor(by_head(exp_gate), by_head(exp_gate), spread_k(sm.unsqueeze(2)), ALU.mult))
                    lane.settle()

            s_io = sem("key_row_made")
            s_f = sem("gates_formed")
            s_ft = sem("choices_transposed")
            s_fe = sem("gates_evacuated")
            s_cc = sem("choices_taken")
            s_oh = sem("one_hots")
            s_oh2 = sem("pool_one_hots")
            s_gst = [sem(f"gates_stored_{n}") for n in range(2)]
            s_glast = sem("last_gates_stored")
            s_gb2 = sem("gate2_spread")
            s_gbe2 = sem("gate2_ready")
            s_base = sem("expert_base_moved")
            s_us = [sem(f"u_stream_{n}") for n in range(2)]
            s_vs = [sem(f"v_stream_{n}") for n in range(2)]
            s_gs = [sem(f"gate_stream_{n}") for n in range(2)]

            def stream(sp, j, par):
                e = bass.ds(l * N_KEYS + j, 1)
                return (lambda: sp.dma_start(u_s[par], io["peer_ut"][e].rearrange("a p (k e) -> p (a k) e", e=P)).then_inc(s_us[par], 16),
                        lambda: sp.dma_start(g_s[par], gate_dram[bass.ds(j, 1)].rearrange("a p t -> p (a t)")).then_inc(s_gs[par], 16),
                        lambda: sp.dma_start(v_s[par], io["peer_v"].rearrange("(e p) d -> e p d", p=P)[e].rearrange("a p d -> p (a d)")).then_inc(s_vs[par], 16))

            with nc.Block() as block:
                @block.gpsimd
                def _(pool):
                    pool.iota(iota_k, pattern=[[1, N_KEYS]], base=0, channel_multiplier=0,
                              allow_small_or_imprecise_dtypes=True).then_inc(s_io, 1)
                    pool.wait_ge(s_io, 1)
                    for i in range(DENSE):
                        for g in range(P // OCT):
                            pool.wait_ge(s_f, 18 * i + g + 1)
                            pool.wait_ge(s_cc, 16 * i + g + 1)
                            for tt in range(OCT - POOL_HOT, OCT):
                                at = lambda q: choice_c[:, g % 2, q, tt:tt + 1]
                                pool.tensor_scalar(hot1[:, g % 2, tt, :], iota_k, at(0), at(2), ALU.is_equal, ALU.mult).then_inc(s_oh2, 1)

                @block.tensor
                def _(pe):
                    for i in range(DENSE):
                        if i:
                            pe.wait_ge(s_fe, 18 * i)
                        pe.transpose(ps[:, 7, 0:P], exp_i1[:, i, :], ident[:, :]).then_inc(s_f, 1)
                        pe.transpose(ps[:, 7, P:2 * P], exp_i2[:, i, :], ident[:, :]).then_inc(s_f, 1)
                        pe.transpose(ps[:, 7, 2 * P:3 * P], exp_gate[:, i, :], ident[:, :]).then_inc(s_ft, 1)
                        with pe.Fori(0, P // (2 * OCT)) as m:
                            for par in range(2):
                                g = 2 * m + par
                                pe.wait_ge(s_oh, (OCT - POOL_HOT + 1) * (16 * i + g + 1))
                                pe.wait_ge(s_oh2, POOL_HOT * (16 * i + g + 1))
                                pe.wait_ge(s_fe, 18 * i + g + 1)
                                for tt in range(OCT):
                                    last = pe.matmul(pair(par)[:, tt * P:(tt + 1) * P], hot2[:, par, tt, :], hot1[:, par, tt, :],
                                                     start=True, stop=True)
                                last.then_inc(s_f, 1)
                    spread_gate(pe, 5, s_gb2)

                @block.vector
                def _(dve):
                    dve.tensor_scalar(exp_base[:, :], exp_base[:, :], float(N_EXPERTS), None, ALU.add).then_inc(s_base, 1)
                    dve.wait_ge(s_io, 1)
                    for i in range(DENSE):
                        dve.wait_ge(s_fe, 18 * i + 2)
                        with dve.Fori(0, P // (2 * OCT)) as m:
                            for par in range(2):
                                g = 2 * m + par
                                dve.wait_ge(s_f, 18 * i + g + 1)
                                dve.tensor_copy(choice_c[:, par, :, :], choice_t[:, :, bass.ds(OCT * g, OCT)]).then_inc(s_cc, 1)
                                dve.wait_ge(s_cc, 16 * i + g + 1)
                                dve.tensor_tensor(hot2[:, par, :, :], iota_k.unsqueeze(1).broadcast_to([P, OCT, N_KEYS]),
                                                  choice_c[:, par, 1, :].unsqueeze(2).broadcast_to([P, OCT, N_KEYS]),
                                                  ALU.is_equal).then_inc(s_oh, 1)
                                for tt in range(OCT - POOL_HOT):
                                    at = lambda q: choice_c[:, par, q, tt:tt + 1]
                                    dve.tensor_scalar(hot1[:, par, tt, :], iota_k, at(0), at(2), ALU.is_equal, ALU.mult).then_inc(s_oh, 1)

                @block.scalar
                def _(act):
                    for i in range(DENSE):
                        act.wait_ge(s_ft, i + 1)
                        if i:
                            act.wait_ge(s_cc, 16 * i)
                        act.activation(choice_t[:, 0:2, :], ps[:, 7, 0:2 * P].rearrange("p (a t) -> p a t", t=P), ACT.Copy).then_inc(s_fe, 1)
                        act.activation(choice_t[:, 2, :], ps[:, 7, 2 * P:3 * P], ACT.Copy).then_inc(s_fe, 1)
                        for half in range(2):
                            if i:
                                act.wait_ge(s_gst[half], 16 * i)
                            with act.Fori(4 * half, 4 * half + 4) as m:
                                for par in range(2):
                                    g = 2 * m + par
                                    act.wait_ge(s_f, 18 * i + g + 3)
                                    act.activation(gate_s[:, :, bass.ds(OCT * g, OCT)],
                                                   pair(par).rearrange("p (t j) -> p j t", j=P), ACT.Copy).then_inc(s_fe, 1)
                    act.wait_ge(s_gb2, 1)
                    act.activation(gate_b.rearrange("p a b -> p (a b)"), ps[:, 4:8, :].rearrange("p a b -> p (a b)"), ACT.Copy).then_inc(s_gbe2, 1)

                @block.sync
                def _(sp):
                    ahead = [stream(sp, par, par) for par in range(2)]
                    for u, _, v in ahead:
                        u()
                        v()
                    for i in range(DENSE):
                        for half in range(2):
                            sp.wait_ge(s_fe, 18 * i + 2 + 8 * (half + 1))
                            at = i * P + half * (P // 2)
                            j0 = FIRST_KEYS if (i, half) == (DENSE - 1, 1) else N_KEYS
                            for a, b, done in ((0, j0, s_gst[half]), (j0, N_KEYS, s_glast)):
                                if a < b:
                                    sp.dma_start(gate_dram[a:b, :, at:at + P // 2].rearrange("j p t -> p j t"),
                                                 gate_s[:, a:b, half * (P // 2):(half + 1) * (P // 2)]).then_inc(done, 16)
                    for half in range(2):
                        sp.wait_ge(s_gst[half], 16 * DENSE)
                    for _, g, _ in ahead:
                        g()

            s_a = sem("dense_scores")
            s_ge = sem("dense_gelus")
            s_h = sem("dense_weights")
            s_g2 = sem("dense_products")
            s_dot = sem("dots_done")
            s_act = sem("gathered_gelus")
            s_wa = sem("gathered_weights")
            s_ax = sem("v_rows_added")
            own8 = sem("expert_vector_steps")
            with nc.Block() as block:
                @block.sync
                def _(sp):
                    sp.wait_ge(s_glast, 16)
                    with sp.Fori(0, N_KEYS // 2 - 1) as m:
                        for par in range(2):
                            u, g, v = stream(sp, 2 * m + 2 + par, par)
                            sp.wait_ge(s_a, 2 * m + par + 1)
                            u()
                            sp.wait_ge(s_h, 2 * m + par + 3)
                            g()
                            sp.wait_ge(s_g2, 2 * m + par + 3)
                            v()

                @block.tensor
                def _(pe):
                    def scores(par, u_count, free):
                        pe.wait_ge(s_us[par], u_count)
                        pe.wait_ge(s_ge, free)
                        for k in range(KD):
                            last = pe.matmul(ps[:, 6 + par, 0:ND], u_s[par][:, k, :], h_t[:, k, 0:ND], start=(k == 0), stop=(k == KD - 1))
                        last.then_inc(s_a, 1)

                    def products(par, v_count, ready):
                        pe.wait_ge(s_vs[par], v_count)
                        pe.wait_ge(s_h, ready)
                        for n in range(2 * DENSE):
                            last = pe.matmul(ps[:, n, :], h_s[par][:, (n // 2) * P:(n // 2 + 1) * P],
                                             v_s[par][:, (n % 2) * 512:(n % 2 + 1) * 512], start=False, stop=False, skip_group_check=True)
                        last.then_inc(s_g2, 1)

                    pe.wait_ge(s_h, 2)
                    for n in range(2 * DENSE):
                        last = pe.matmul(ps[:, n, :], h_s[1 if n == 2 * DENSE - 1 else 0][:, 0:P],
                                         ident[:, :].unsqueeze(1).broadcast_to([P, 4, P]), start=True, stop=False, skip_group_check=True)
                        if n >= 2 * DENSE - 2:
                            last.then_inc(s_g2, 1)
                    scores(0, 16, 1)
                    with pe.Fori(0, N_KEYS // 2 - 1) as m:
                        scores(1, 16 * (m + 1), 2 * m + 2)
                        products(0, 16 * (m + 1), 2 * m + 3)
                        scores(0, 16 * (m + 2), 2 * m + 3)
                        products(1, 16 * (m + 1), 2 * m + 4)
                    scores(1, 16 * (N_KEYS // 2), N_KEYS)
                    products(0, 16 * (N_KEYS // 2), N_KEYS + 1)
                    products(1, 16 * (N_KEYS // 2), N_KEYS + 2)

                @block.scalar
                def _(act):
                    for n in range(2):
                        act.activation(spare[:, n:n + 1], ident[:, n:n + 1], ACT.Copy).then_inc(s_ge, 1)
                    for i in range(len(GATHERED)):
                        with act.Fori(0, PH) as h:
                            u = h + i * PH
                            for jj in range(STEPS):
                                act.wait_ge(s_a, u * STEPS + jj + 1)
                                act.wait_ge(s_h, u * STEPS + jj + 1)
                                act.activation(gelu_s[jj % 2], ps[:, 6 + jj % 2, 0:ND], ACT.Gelu_apprx_tanh).then_inc(s_ge, 1)
                                if jj == STEPS // 2 - 1:
                                    act.wait_ge(s_dot, (u + 1) * TOPK)
                                    act.activation(act_c, act_c, ACT.Gelu_apprx_tanh).then_inc(s_act, 1)

                @block.vector
                def _(dve):
                    for n in range(2):
                        dve.memset(h_s[n], 0.0).then_inc(s_h, 1)
                    lane = Lane(dve, own8)
                    for i, tile in enumerate(GATHERED):
                        dve.memset(acc, 0.0).then_inc(s_ax, 1)
                        with dve.Fori(0, PH) as h:
                            u = h + i * PH
                            for jj in range(STEPS):
                                j = u * STEPS + jj
                                dve.wait_ge(s_ge, j + 3)
                                dve.wait_ge(s_gs[jj % 2], 16 * (u * (STEPS // 2) + jj // 2 + 1))
                                dve.wait_ge(s_g2, j + 1)
                                dve.tensor_tensor(h_s[jj % 2], gelu_s[jj % 2], g_s[jj % 2], ALU.mult).then_inc(s_h, 1)
                                if jj < STEPS // 2:
                                    for k in range(4 * jj, 4 * jj + 4):
                                        dve.wait_ge(s_gu[k], 16 * (l * 16 + u + 1))
                                        dve.tensor_tensor_reduce(out=u_ring[:, k, :], in0=u_ring[:, k, :], in1=y_nat[:, tile, :],
                                                                 scale=1.0, scalar=0.0, op0=ALU.mult, op1=ALU.add,
                                                                 accum_out=act_c[:, k:k + 1]).then_inc(s_dot, 1)
                                    continue
                                if jj == STEPS // 2:
                                    dve.wait_ge(s_act, u + 1)
                                    dve.wait_ge(s_ax, i + 1 + u * TOPK)
                                    dve.tensor_tensor(wact, act_c, exp_gate[:, tile, bass.ds(h * TOPK, TOPK)], ALU.mult).then_inc(s_wa, 1)
                                    dve.wait_ge(s_wa, u + 1)
                                for k in range(4 * jj - 16, 4 * jj - 12):
                                    v = v_ring[:, k % VSLOTS, :]
                                    dve.wait_ge(s_gv[k % VSLOTS], 16 * (2 * (l * 16 + u) + k // VSLOTS + 1))
                                    dve.wait_ge(s_ax, i + 1 + u * TOPK + k)
                                    dve.scalar_tensor_tensor(out=acc, in0=v, scalar=wact[:, k:k + 1], in1=acc,
                                                             op0=ALU.mult, op1=ALU.add).then_inc(s_ax, 1)
                        dve.wait_ge(s_ax, (i + 1) * (1 + PH * TOPK))
                        lane.do(dve.tensor_tensor(acc, acc, gate_b[:, 1 if tile == CTX else 0, :], ALU.mult))
                        lane.settle()
                        lane.do(dve.tensor_tensor(x_res[:, tile, :], x_res[:, tile, :], acc, ALU.add))
                        lane.settle()
                    dve.wait_ge(s_g2, N_KEYS + 2)
                    for t in range(DENSE):
                        lane.do(dve.tensor_tensor(acc, pair(t), gate_b[:, 0, :], ALU.mult))
                        lane.settle()
                        lane.do(dve.tensor_tensor(x_res[:, t, :], x_res[:, t, :], acc, ALU.add))
                        lane.settle()

                @block.gpsimd
                def _(pool):
                    def u_row(i, h, k):
                        u = i * PH + h
                        if u >= 1:
                            pool.wait_ge(s_dot, (u - 1) * TOPK + k + 1)
                        pool.indirect_dma_start(
                            out=u_ring[:, k, :], out_offset=None, in_=io["peer_u"][:, :],
                            in_offset=bass.IndirectOffsetOnAxis(ap=exp_idx[:, GATHERED[i], h * TOPK + k:h * TOPK + k + 1], axis=0),
                        ).then_inc(s_gu[k], 16)

                    def v_row(i, h, k):
                        n = (i * PH + h) * TOPK + k
                        if n >= VSLOTS:
                            before = n - VSLOTS
                            pool.wait_ge(s_ax, before // (PH * TOPK) + 1 + before + 1)
                        pool.indirect_dma_start(
                            out=v_ring[:, k % VSLOTS, :], out_offset=None, in_=io["peer_v"][:, :],
                            in_offset=bass.IndirectOffsetOnAxis(ap=exp_idx[:, GATHERED[i], h * TOPK + k:h * TOPK + k + 1], axis=0),
                        ).then_inc(s_gv[k % VSLOTS], 16)

                    heads = [(i, h) for i in range(len(GATHERED)) for h in range(PH)]
                    for k in range(VSLOTS):
                        v_row(0, 0, k)
                    pool.wait_ge(s_glast, 16)
                    for k in range(TOPK):
                        u_row(0, 0, k)
                    for n, (i, h) in enumerate(heads):
                        for k in range(VSLOTS if n else 0):
                            v_row(i, h, k)
                        for k in range(TOPK if n + 1 < len(heads) else 0):
                            u_row(*heads[n + 1], k)
                        for k in range(VSLOTS, TOPK):
                            v_row(i, h, k)

            quarter = [cleared[n::4] for n in range(4)]
            with nc.Block() as block:
                @block.gpsimd
                def _(pool):
                    for s in quarter[0]:
                        pool.sem_clear(s)

                @block.vector
                def _(dve):
                    for s in quarter[1]:
                        dve.sem_clear(s)

                @block.scalar
                def _(act):
                    for s in quarter[2]:
                        act.sem_clear(s)

                @block.sync
                def _(sp):
                    for s in quarter[3]:
                        sp.sem_clear(s)

        own9 = sem("final_vector_steps")
        s_fw = sem("final_weight_loaded")
        s_m9 = sem("final_mean_squares")
        s_r9 = sem("final_roots")
        s_y9 = sem("final_rows")
        s_out = sem("outputs_stored")
        fw = gates_area[:, 0:D]
        with nc.Block() as block:
            @block.sync
            def _(sp):
                sp.dma_start(fw, io["final_norm_w"].broadcast_to([P, D])).then_inc(s_fw, 16)
                for t in range(TILES):
                    sp.wait_ge(s_y9, t + 1)
                    dst = io["y_prompt"][0] if t == CTX else io["y_sample"][0, t * P:(t + 1) * P, :]
                    sp.dma_start(dst, y_nat[:, t, :]).then_inc(s_out, 16)
                sp.wait_ge(s_out, 16 * TILES)

            @block.scalar
            def _(act):
                act.wait_ge(s_m9, 1)
                act.activation(stat[:, 0, 0:TILES], stat[:, 0, 0:TILES], ACT.Sqrt).then_inc(s_r9, 1)

            @block.vector
            def _(dve):
                lane = Lane(dve, own9)
                ss = stat[:, 0, 0:TILES]
                for t in range(TILES):
                    lane.do(dve.tensor_tensor_reduce(out=y_nat[:, t, :], in0=x_res[:, t, :], in1=x_res[:, t, :],
                                                     scale=1.0, scalar=0.0, op0=ALU.mult, op1=ALU.add,
                                                     accum_out=stat[:, 0, t:t + 1]))
                lane.settle()
                lane.do(dve.tensor_scalar(ss, ss, 1.0 / D, EPS, ALU.mult, ALU.add), s_m9)
                dve.wait_ge(s_r9, 1)
                dve.wait_ge(s_fw, 16)
                lane.do(dve.reciprocal(stat[:, 1, 0:TILES], ss))
                lane.settle()
                for t in range(TILES):
                    lane.do(dve.scalar_tensor_tensor(out=y_nat[:, t, :], in0=x_res[:, t, :], scalar=stat[:, 1, t:t + 1],
                                                     in1=fw, op0=ALU.mult, op1=ALU.mult), s_y9)


def kernel(**inputs):
    import numpy as np
    import concourse.bacc as bacc
    from concourse.bass_utils import run_bass_kernel_spmd

    a = {k: np.ascontiguousarray(v) for k, v in inputs.items()}
    w_g = a["w_in"][:, :, D_IN - 4 * HEADS:].reshape(DEPTH, KD, P, 2, 2, HEADS)
    w_gate = np.zeros((DEPTH, P, KD, 2, ROWS), np.float32)
    b_gate = np.zeros((DEPTH, ROWS, 2), np.float32)
    state_m = np.zeros((DEPTH, ROWS, 1), np.float32)
    for d in range(2):
        rows = slice(32 * d, 32 * d + HEADS)
        w_gate[..., rows] = w_g[:, :, :, d].transpose(0, 2, 1, 3, 4)
        b_gate[:, rows, :] = a["b_gate"].reshape(DEPTH, 2, 2, HEADS)[:, d].transpose(0, 2, 1)
        state_m[:, rows, 0] = a["state_m"][0, :, d]
    cols = lambda v: v.reshape(KD, P).T
    arrays = {
        "x_sample": a["x_sample"], "x_prompt": a["x_prompt"],
        "cond_t": np.stack([cols(a["c"][0]), cols(a["c_ctx"])], axis=2),
        "w_mod": a["w_mod"], "bmod_t": a["b_mod"].reshape(DEPTH, 48, P).transpose(2, 0, 1),
        "w_in": a["w_in"], "w_gate": w_gate, "b_gate": b_gate, "state_m": state_m,
        "conv_w": a["conv_w"].reshape(DEPTH, 9, KD, P).transpose(0, 3, 2, 1),
        "w_st": a["w_s"].transpose(0, 3, 1, 2), "b_st": a["b_s"].transpose(0, 2, 1),
        "mlstm_norm_w": a["mlstm_norm_w"],
        "state_C": a["state_C"].reshape(DEPTH, R, DH, DH),
        "state_n": a["state_n"].reshape(DEPTH, R, DH).transpose(0, 2, 1),
        "w_out": a["w_out"], "peer_wq": a["peer_wq"],
        "keys_t": a["peer_keys"].reshape(DEPTH, 2 * PH, N_KEYS, DH).transpose(0, 3, 1, 2),
        "peer_u": a["peer_u"].reshape(DEPTH * N_EXPERTS, D), "peer_v": a["peer_v"].reshape(DEPTH * N_EXPERTS, D),
        "peer_ut": a["peer_u"].reshape(DEPTH * N_KEYS, N_KEYS, KD, P).transpose(0, 3, 2, 1).reshape(DEPTH * N_KEYS, P, D),
        "final_norm_w": a["final_norm_w"].reshape(1, D),
    }
    arrays = {k: np.ascontiguousarray(v) for k, v in arrays.items()}
    outs = {
        "y_prompt": (1, P, D), "y_sample": (1, NS, D), "new_C": (DEPTH, R, DH, DH),
        "new_n": (DEPTH, DH, R), "new_m": (DEPTH, ROWS, 1),
    }
    nc = bacc.Bacc("TRN2", target_bir_lowering=False, num_devices=1)
    io = {k: nc.dram_tensor(f"in_{k}", v.shape, mybir.dt.from_np(v.dtype), kind="ExternalInput").ap() for k, v in arrays.items()}
    io.update({k: nc.dram_tensor(f"out_{k}", s, F32, kind="ExternalOutput").ap() for k, s in outs.items()})
    build(nc, io)
    r = run_bass_kernel_spmd(nc, [{f"in_{k}": v for k, v in arrays.items()}], core_ids=[0]).results[0]
    return (r["out_y_prompt"], r["out_y_sample"], r["out_new_C"].reshape(1, DEPTH, 2, HEADS, DH, DH),
            r["out_new_n"].transpose(0, 2, 1).reshape(1, DEPTH, 2, HEADS, DH),
            r["out_new_m"].reshape(1, DEPTH, 2, ROWS // 2)[..., 0:HEADS])
```
